# Optimizing a Trainium2 kernel written in Bass

```python
import jax, jax.numpy as jnp
from jax import lax
import numpy as np

D_MODEL = 2048
BATCH = 1
SEQ = 512
DEPTH = 1
DEC_BATCH = 8
DEC_SEQ = 8
PAST_LEN = 4096
PAGE_SIZE = 128

N_META = 16
MIX_W = D_MODEL
RET_HEADS = 4
RET_DK = (MIX_W // 2) // RET_HEADS
RET_DV = (MIX_W // 2) // RET_HEADS
RET_CHUNK = 128
RET_THETA = 10000.0
SWA_HD = 64
SWA_HEADS = (MIX_W // 2) // SWA_HD
SWA_KV_HEADS = 2
SWA_GROUP = SWA_HEADS // SWA_KV_HEADS
WINDOW = 128
BUF_LEN = min(WINDOW, PAST_LEN)
ROPE_THETA = 500000.0
ROT_DIM = SWA_HD // 4
FFN_HIDDEN = -(-8 * D_MODEL // (3 * 256)) * 256
ALPHA = (2.0 * DEPTH) ** 0.25
BETA = (8.0 * DEPTH) ** -0.25
LN_EPS = 1e-5
NEG_INF = -1e30

PROJ_SIZES = (RET_HEADS * RET_DK, RET_HEADS * RET_DK, RET_HEADS * RET_DV, RET_HEADS * RET_DV,
              SWA_HEADS * SWA_HD, SWA_KV_HEADS * SWA_HD, SWA_KV_HEADS * SWA_HD)
PROJ_W = sum(PROJ_SIZES)

kernel_name = "hymba_retention_swa_sink_deepnorm_step"

def layer_norm(x, g, b):
    xf = x.astype(jnp.float32)
    mu = xf.mean(-1, keepdims=True)
    var = jnp.square(xf - mu).mean(-1, keepdims=True)
    return ((xf - mu) * lax.rsqrt(var + LN_EPS) * g + b).astype(x.dtype)

def head_group_norm(o):
    mu = o.mean(-1, keepdims=True)
    var = jnp.square(o - mu).mean(-1, keepdims=True)
    return (o - mu) * lax.rsqrt(var + LN_EPS)

def rope(x, pos, inv_freq):
    ang = pos.astype(jnp.float32)[:, None] * inv_freq[None, :]
    cos = jnp.cos(ang)[:, None, :]
    sin = jnp.sin(ang)[:, None, :]
    x1, x2 = jnp.split(x.astype(jnp.float32), 2, axis=-1)
    return jnp.concatenate([x1 * cos - x2 * sin, x2 * cos + x1 * sin], -1).astype(x.dtype)

def mixer_projections(x, pos, w_in):
    B, T, _ = x.shape
    z = jnp.einsum('btd,de->bte', x, w_in)
    split_at = np.cumsum(PROJ_SIZES)[:-1].tolist()
    rq, rk, rv, rg, sq, sk, sv = jnp.split(z, split_at, axis=-1)
    ret_freq = jnp.power(RET_THETA, -jnp.linspace(0.0, 1.0, RET_DK // 2, dtype=jnp.float32))
    rq = rope(rq.reshape(B, T, RET_HEADS, RET_DK), pos, ret_freq)
    rk = rope(rk.reshape(B, T, RET_HEADS, RET_DK), pos, ret_freq) * (RET_DK ** -0.5)
    rv = rv.reshape(B, T, RET_HEADS, RET_DV)
    rg = rg.reshape(B, T, RET_HEADS, RET_DV)
    swa_freq = jnp.power(ROPE_THETA, -jnp.arange(0, ROT_DIM, 2, dtype=jnp.float32) / ROT_DIM)
    sq = sq.reshape(B, T, SWA_HEADS, SWA_HD)
    sk = sk.reshape(B, T, SWA_KV_HEADS, SWA_HD)
    sq = jnp.concatenate([rope(sq[..., :ROT_DIM], pos, swa_freq), sq[..., ROT_DIM:]], -1)
    sk = jnp.concatenate([rope(sk[..., :ROT_DIM], pos, swa_freq), sk[..., ROT_DIM:]], -1)
    sv = sv.reshape(B, T, SWA_KV_HEADS, SWA_HD)
    return rq, rk, rv, rg, sq, sk, sv

def retention_log_gamma():
    return jnp.log(1.0 - jnp.power(2.0, -5.0 - jnp.arange(RET_HEADS, dtype=jnp.float32)))

def retention_chunk(q, k, v, s_prev, log_gamma):
    C = q.shape[1]
    qf, kf, vf = (a.astype(jnp.float32) for a in (q, k, v))
    s_prev = s_prev.astype(jnp.float32)
    idx = jnp.arange(C, dtype=jnp.float32)
    rel = idx[:, None] - idx[None, :]
    decay = jnp.where(rel[None] >= 0,
                      jnp.exp(jnp.maximum(rel, 0.0)[None] * log_gamma[:, None, None]), 0.0)
    scores = jnp.einsum('bihd,bjhd->bhij', qf, kf) * decay[None]
    inner = jnp.einsum('bhij,bjhe->bihe', scores, vf)
    q_decay = jnp.exp((idx + 1.0)[:, None] * log_gamma[None, :])
    cross = jnp.einsum('bihd,bhde->bihe', qf, s_prev) * q_decay[None, :, :, None]
    k_decay = jnp.exp((C - 1.0 - idx)[:, None] * log_gamma[None, :])
    s_new = (jnp.exp(C * log_gamma)[None, :, None, None] * s_prev
             + jnp.einsum('bjhd,bjhe,jh->bhde', kf, vf, k_decay))
    return inner + cross, s_new

def retention_prompt(q, k, v, log_gamma):
    B, L = q.shape[:2]
    s0 = jnp.zeros((B, RET_HEADS, RET_DK, RET_DV), jnp.float32)
    o_meta, s = retention_chunk(q[:, :N_META], k[:, :N_META], v[:, :N_META], s0, log_gamma)
    n_chunks = (L - N_META) // RET_CHUNK

    def to_chunks(a):
        return a[:, N_META:].reshape(B, n_chunks, RET_CHUNK, *a.shape[2:]).swapaxes(0, 1)

    def step(s_c, qkv):
        o_c, s_c = retention_chunk(qkv[0], qkv[1], qkv[2], s_c, log_gamma)
        return s_c, o_c

    s, o = lax.scan(step, s, (to_chunks(q), to_chunks(k), to_chunks(v)))
    o = o.swapaxes(0, 1).reshape(B, L - N_META, RET_HEADS, RET_DV)
    return jnp.concatenate([o_meta, o], axis=1), s

def sink_softmax(logits, mask, sink):
    logits = jnp.where(mask, logits, NEG_INF)
    m = jnp.maximum(logits.max(-1, keepdims=True), sink)
    p = jnp.exp(logits - m)
    return p / (p.sum(-1, keepdims=True) + jnp.exp(sink - m))

def swa_prompt(q, k, v, sinks):
    B, L = q.shape[:2]
    nb = -(-L // WINDOW)
    Lp = nb * WINDOW
    pad_end = Lp - L
    qb = jnp.pad(q, ((0, 0), (0, pad_end), (0, 0), (0, 0))).reshape(
        B, nb, WINDOW, SWA_KV_HEADS, SWA_GROUP, SWA_HD)

    def band(a):
        ap = jnp.pad(a, ((0, 0), (WINDOW, pad_end), (0, 0), (0, 0)))
        prev = ap[:, :Lp].reshape(B, nb, WINDOW, SWA_KV_HEADS, SWA_HD)
        cur = ap[:, WINDOW:].reshape(B, nb, WINDOW, SWA_KV_HEADS, SWA_HD)
        return jnp.concatenate([prev, cur], axis=2)

    kb, vb = band(k), band(v)
    blk = jnp.arange(nb)[:, None] * WINDOW
    qpos = blk + jnp.arange(WINDOW)[None]
    kpos = blk - WINDOW + jnp.arange(2 * WINDOW)[None]
    diff = qpos[:, :, None] - kpos[:, None, :]
    mask = (diff >= 0) & (diff < WINDOW) & (kpos[:, None, :] >= 0)
    logits = jnp.einsum('bnqgrd,bnkgd->bngrqk', qb.astype(jnp.float32),
                        kb.astype(jnp.float32)) * (SWA_HD ** -0.5)
    sink = sinks.astype(jnp.float32).reshape(SWA_KV_HEADS, SWA_GROUP)[None, None, :, :, None, None]
    probs = sink_softmax(logits, mask[None, :, None, None], sink)
    o = jnp.einsum('bngrqk,bnkgd->bnqgrd', probs, vb.astype(jnp.float32))
    return o.reshape(B, Lp, SWA_HEADS * SWA_HD)[:, :L].astype(v.dtype)

def swa_sample(q, k_new, v_new, k_buf, v_buf, sinks):
    B, T = q.shape[:2]
    kk = jnp.concatenate([k_buf.astype(k_new.dtype), k_new], axis=1)
    vv = jnp.concatenate([v_buf.astype(v_new.dtype), v_new], axis=1)
    qpos = BUF_LEN + jnp.arange(T)
    kpos = jnp.arange(BUF_LEN + T)
    diff = qpos[:, None] - kpos[None, :]
    mask = (diff >= 0) & (diff < WINDOW)
    qg = q.reshape(B, T, SWA_KV_HEADS, SWA_GROUP, SWA_HD).astype(jnp.float32)
    logits = jnp.einsum('btgrd,bkgd->bgrtk', qg, kk.astype(jnp.float32)) * (SWA_HD ** -0.5)
    sink = sinks.astype(jnp.float32).reshape(SWA_KV_HEADS, SWA_GROUP)[None, :, :, None, None]
    probs = sink_softmax(logits, mask[None, None, None], sink)
    o = jnp.einsum('bgrtk,bkgd->btgrd', probs, vv.astype(jnp.float32))
    return (o.reshape(B, T, SWA_HEADS * SWA_HD).astype(v_new.dtype),
            kk[:, -BUF_LEN:], vv[:, -BUF_LEN:])

def layer_tail(x, ret_o, ret_gate, swa_o, w_out, ln_mix_g, ln_mix_b,
               w_ffn_gate, w_ffn_up, w_ffn_down, ln_ffn_g, ln_ffn_b):
    B, T, _ = x.shape
    ret_o = head_group_norm(ret_o).astype(x.dtype) * jax.nn.silu(ret_gate)
    mixed = jnp.concatenate([ret_o.reshape(B, T, -1), swa_o.reshape(B, T, -1)], axis=-1)
    h = layer_norm(ALPHA * x + mixed @ w_out, ln_mix_g, ln_mix_b)
    f = (jax.nn.silu(h @ w_ffn_gate) * (h @ w_ffn_up)) @ w_ffn_down
    return layer_norm(ALPHA * h + f, ln_ffn_g, ln_ffn_b)

def setup_inputs(seed: int = 0) -> dict:
    key = jax.random.key(seed)
    ks = jax.random.split(key, 20)
    f32 = jnp.float32
    nrm = lambda k, shape, s: jax.random.normal(k, shape, f32) * s
    return {
        "x_prompt": nrm(ks[0], (BATCH, SEQ, D_MODEL), 1.0),
        "x_sample": nrm(ks[1], (DEC_BATCH, DEC_SEQ, D_MODEL), 1.0),
        "state_ret": nrm(ks[2], (DEPTH, DEC_BATCH, RET_HEADS, RET_DK, RET_DV), 0.5),
        "cache_swa_k": nrm(ks[3], (DEPTH, DEC_BATCH, BUF_LEN, SWA_KV_HEADS, SWA_HD), 1.0),
        "cache_swa_v": nrm(ks[4], (DEPTH, DEC_BATCH, BUF_LEN, SWA_KV_HEADS, SWA_HD), 1.0),
        "meta_tokens": nrm(ks[5], (N_META, D_MODEL), 1.0),
        "ln_emb_g": 1.0 + nrm(ks[6], (D_MODEL,), 0.02),
        "ln_emb_b": nrm(ks[7], (D_MODEL,), 0.02),
        "w_in": nrm(ks[8], (DEPTH, D_MODEL, PROJ_W), D_MODEL ** -0.5),
        "w_out": nrm(ks[9], (DEPTH, MIX_W, D_MODEL), BETA * MIX_W ** -0.5),
        "swa_sinks": nrm(ks[10], (DEPTH, SWA_HEADS), 0.5),
        "ln_mix_g": 1.0 + nrm(ks[11], (DEPTH, D_MODEL), 0.02),
        "ln_mix_b": nrm(ks[12], (DEPTH, D_MODEL), 0.02),
        "w_ffn_gate": nrm(ks[13], (DEPTH, D_MODEL, FFN_HIDDEN), D_MODEL ** -0.5),
        "w_ffn_up": nrm(ks[14], (DEPTH, D_MODEL, FFN_HIDDEN), D_MODEL ** -0.5),
        "w_ffn_down": nrm(ks[15], (DEPTH, FFN_HIDDEN, D_MODEL), BETA * FFN_HIDDEN ** -0.5),
        "ln_ffn_g": 1.0 + nrm(ks[16], (DEPTH, D_MODEL), 0.02),
        "ln_ffn_b": nrm(ks[17], (DEPTH, D_MODEL), 0.02),
    }

def reference(x_prompt, x_sample, state_ret, cache_swa_k, cache_swa_v, meta_tokens,
              ln_emb_g, ln_emb_b, w_in, w_out, swa_sinks, ln_mix_g, ln_mix_b,
              w_ffn_gate, w_ffn_up, w_ffn_down, ln_ffn_g, ln_ffn_b):
    B, S, D = x_prompt.shape
    T = x_sample.shape[1]
    log_gamma = retention_log_gamma()
    meta = jnp.broadcast_to(meta_tokens.astype(x_prompt.dtype)[None], (B, N_META, D))
    h_p = layer_norm(jnp.concatenate([meta, x_prompt], axis=1), ln_emb_g, ln_emb_b)
    h_s = layer_norm(x_sample, ln_emb_g, ln_emb_b)
    pos_p = jnp.arange(N_META + S)
    pos_s = PAST_LEN + jnp.arange(T)
    ret_p, k_p, v_p, ret_s, k_s, v_s = [], [], [], [], [], []
    for l in range(DEPTH):
        rq, rk, rv, rg, sq, sk, sv = mixer_projections(h_p, pos_p, w_in[l])
        ret_o, s_new = retention_prompt(rq, rk, rv, log_gamma)
        swa_o = swa_prompt(sq, sk, sv, swa_sinks[l])
        ret_p.append(s_new.astype(h_p.dtype))
        k_p.append(sk[:, -BUF_LEN:])
        v_p.append(sv[:, -BUF_LEN:])
        h_p = layer_tail(h_p, ret_o, rg, swa_o, w_out[l], ln_mix_g[l], ln_mix_b[l],
                         w_ffn_gate[l], w_ffn_up[l], w_ffn_down[l], ln_ffn_g[l], ln_ffn_b[l])
        rq, rk, rv, rg, sq, sk, sv = mixer_projections(h_s, pos_s, w_in[l])
        ret_o, s_new = retention_chunk(rq, rk, rv, state_ret[l], log_gamma)
        swa_o, kb_new, vb_new = swa_sample(sq, sk, sv, cache_swa_k[l], cache_swa_v[l], swa_sinks[l])
        ret_s.append(s_new.astype(h_s.dtype))
        k_s.append(kb_new)
        v_s.append(vb_new)
        h_s = layer_tail(h_s, ret_o, rg, swa_o, w_out[l], ln_mix_g[l], ln_mix_b[l],
                         w_ffn_gate[l], w_ffn_up[l], w_ffn_down[l], ln_ffn_g[l], ln_ffn_b[l])
    y_prompt = h_p[:, N_META:]
    y_sample = h_s
    return (y_prompt, y_sample, jnp.stack(ret_p), jnp.stack(k_p), jnp.stack(v_p),
            jnp.stack(ret_s), jnp.stack(k_s), jnp.stack(v_s))


_drawn_inputs = setup_inputs


def setup_inputs(seed=0):
    import zlib

    import numpy as np

    out = dict(_drawn_inputs(seed))
    spreads = {}
    factors = {'swa_sinks': 8.0,
     'ln_mix_g': 2.794,
     'ln_mix_b': 2.792,
     'ln_ffn_g': 2.906,
     'ln_ffn_b': 2.826}
    for name, (base, spread) in spreads.items():
        noise = np.random.default_rng([zlib.crc32(name.encode()), seed]).standard_normal(out[name].shape)
        drawn = base * np.exp(spread * noise) if base else spread * noise
        out[name] = __import__('jax').numpy.asarray(drawn.astype(out[name].dtype))
    for name, factor in factors.items():
        out[name] = (out[name] * factor).astype(out[name].dtype)
    return out
```

```python
from contextlib import ExitStack, contextmanager

import numpy as np

import concourse.bass as bass
from concourse import mybir

F32 = mybir.dt.float32
F32R = mybir.dt.float32r
ALU = mybir.AluOpType
ACT = mybir.ActivationFunctionType
AX_X = mybir.AxisListType.X

P = 128
D = 2048
SEQ, N_META = 512, 16
DEC_B, DEC_T = 8, 8
PAST = 4096
HEADS, DK = 4, 256
HD, WINDOW, ROT = 64, 128, 16
FFN = 5632
LN_EPS = 1e-5
ALPHA = 2.0 ** 0.25

TP = N_META + SEQ
TS = DEC_B * DEC_T
T = TP + TS
NT = T // 2
KT = D // P
KP = 4
SLOTS = 4
HT = FFN // P
GROUPS = HT // KP
Q_COL, K_COL, V_COL, G_COL = 0, 1024, 2048, 3072
SQ_COL, SK_COL, SV_COL = 4096, 5120, 5248
RET_BLOCKS = 8
CHUNKS = [(0, N_META)] + [(N_META + 128 * c, 128) for c in range(4)] + [(TP, TS)]
NCH = len(CHUNKS)
SMP = NCH - 1
HC_DS, HC_KD, HC_KD0, HC_EPS, HC_EPSS, HC_G, HC_G0, HC_GS, HC_KB = 128, 192, 193, 194, 195, 196, 197, 198, 199
HC_W = HC_KB + DEC_B

PER_HEAD = 2 + 3 * NCH


def shape_constants():
    f = np.float32
    pos = np.concatenate([np.arange(TP), np.tile(PAST + np.arange(DEC_T), DEC_B)]).astype(f)
    rf = np.power(f(10000.0), -np.linspace(0.0, 1.0, DK // 2, dtype=f)).astype(f)
    ang = (pos[None, :] * rf[:, None]).astype(f).astype(np.float64)
    ret_rot = np.stack([np.cos(ang), np.sin(ang)], 1).astype(f)
    half = ROT // 2
    sf = np.power(f(500000.0), -np.arange(0, ROT, 2, dtype=f) / f(ROT)).astype(f)
    sang = (pos[None, :] * sf[:, None]).astype(f).astype(np.float64)
    swa_rot = np.zeros((P, 2, T), f)
    swa_rot[:, 0] = 1.0
    swap = np.zeros((P, P), f)
    for b in (0, HD):
        for i in range(half):
            swa_rot[b + i, 0] = swa_rot[b + half + i, 0] = np.cos(sang[i])
            swa_rot[b + i, 1] = -np.sin(sang[i])
            swa_rot[b + half + i, 1] = np.sin(sang[i])
            swap[b + half + i, b + i] = swap[b + i, b + half + i] = 1.0
    perm = np.zeros((P, 3, P), f)
    perm[:, 0] = swap
    for kv in range(2):
        for i in range(HD):
            perm[kv * HD + i, 1 + kv, i] = perm[kv * HD + i, 1 + kv, HD + i] = 1.0
    gam = 1.0 - 2.0 ** (-5.0 - np.arange(HEADS, dtype=np.float64))
    hc = np.zeros((HEADS, P, HC_W), np.float64)
    j = np.arange(P)[:, None]
    i = np.arange(P)[None, :]
    t = np.arange(P) % DEC_T
    bb = np.arange(P) // DEC_T
    for h in range(HEADS):
        g = gam[h]
        hc[h, :, 0:128] = (i >= j) * g ** -(j + 1.0) / 16.0
        ok = (bb[:, None] == bb[None, :64]) & (t[None, :64] >= t[:, None]) & (np.arange(P)[:, None] < TS)
        hc[h, :, HC_DS:HC_DS + 64] = ok * (g ** -(t + 1.0))[:, None] / 16.0
        hc[h, :, HC_KD] = g ** (127.0 - np.arange(P)) / 16.0
        hc[h, :N_META, HC_KD0] = g ** (N_META - 1.0 - np.arange(N_META)) / 16.0
        hc[h, :, HC_EPS] = LN_EPS * g ** (-2.0 * (np.arange(P) + 1.0))
        hc[h, :, HC_EPSS] = LN_EPS * g ** (-2.0 * (t + 1.0))
        hc[h, :, HC_G] = g ** 128
        hc[h, :, HC_GS] = g ** DEC_T
        for b in range(DEC_B):
            hc[h, :, HC_KB + b] = (bb == b) * g ** (DEC_T - 1.0 - t) / 16.0
    neg = f(-1e30)
    q = np.arange(P)[:, None]
    kk = np.arange(2 * P)[None, :]
    diff = q + P - kk
    mask_p = np.where((diff >= 0) & (diff < WINDOW), f(0), neg).astype(f)
    tq = (np.arange(P) % DEC_T)[:, None]
    pc = np.arange(P)[None, :]
    mask_c = np.where(tq + P - pc < WINDOW, f(0), neg).astype(f)
    mask_n = np.full((P, DEC_B, TS), neg, f)
    for b in range(DEC_B):
        for u in range(DEC_T):
            mask_n[:, b, b * DEC_T + u] = np.where(tq[:, 0] >= u, f(0), neg)
    return {
        "c_ret_rot": ret_rot, "c_swa_rot": swa_rot, "c_perm": perm, "c_head": hc.astype(f),
        "c_mask_p": mask_p, "c_mask_c": mask_c, "c_mask_n": mask_n, "c_ident": np.eye(P, dtype=f),
    }


class Count:

    def __init__(self, eng, sem):
        self.eng, self.sem, self.base, self.n = eng, sem, 0, 0

    def link(self, ins, met=None):
        self.n += 1
        ins.then_inc(self.sem, 1)
        value = self.base + self.n
        if met is not None:
            value = self.eng.to_reg(value)
            self.eng.wait_ge(met, 1)
        self.eng.wait_ge(self.sem, value)

    @contextmanager
    def loop(self, i, times, per):
        base, n = self.base, self.n
        self.base, self.n = i * per + (base + n), 0
        yield
        assert self.n == per, f"{self.n} links in a loop of {per}"
        self.base, self.n = base, n + times * per


def hymba_step_kernel(nc, I, O):
    with ExitStack() as ctx:
        RB = KT * T * 4
        R0, R1, R2, R3, R4 = (n * RB for n in range(5))
        END = 212800
        base = -(-nc.sbuf_base // 32) * 32
        slab = ctx.enter_context(nc.sbuf_tensor("slab", [P, END // 4], F32))

        def at(name, shape, off, dt=F32):
            return nc.alloc_sbuf_tensor_at(name, shape, dt, offset=base + off)

        class Area:

            def __init__(self, off, end):
                self.off, self.end = off, end

            def __call__(self, name, shape, dt=F32):
                a = at(name, shape, self.off, dt)
                self.off += (4 * int(np.prod(shape[1:])) + 31) // 32 * 32
                assert self.off <= self.end, (name, self.off, self.end)
                return a

        xh, xl = at("xh", [P, KT, T], R0, F32R), at("xl", [P, KT, T], R1, F32R)
        mh, ml = at("mh", [P, KT, T], R2, F32R), at("ml", [P, KT, T], R3, F32R)
        yb = at("yb", [P, KT, T], R1)
        hh, hl = at("hh", [P, KT, T], R2, F32R), at("hl", [P, KT, T], R3, F32R)
        fh, fl = at("fh", [P, 2, KP, T], R0, F32R), at("fl", [P, 2, KP, T], R0 + RB // 2, F32R)
        g_row, b_row = at("g_row", [P, D], R0 + RB // 4), at("b_row", [P, D], R0 + 3 * RB // 4)
        xin = at("xin", [P, NCH, D], R2)
        yo = at("yo", [P, 5, D], R2)

        PIECE = KP * P * 4
        raw = at("raw", [P, SLOTS, KP, P], R4)
        wh = at("wh", [P, SLOTS, KP, P], R4 + SLOTS * PIECE, F32R)
        wl = at("wl", [P, SLOTS, KP, P], R4 + 2 * SLOTS * PIECE, F32R)

        keep = Area(R4 + 3 * SLOTS * PIECE, END)
        ident = keep("ident", [P, P])
        vec = keep("vec", [P, 4, KT])
        small = keep("small", [P, 160])
        R5 = keep.off
        ia = Area(R5, END)
        xf = ia("xf", [P, 2, T])
        vec_rows = ia("vec_rows", [4 * KT, P])
        ra = Area(R5, END)
        ret_rot = ra("ret_rot", [P, 2, T])
        v_raw = ra("v_raw", [P, 2, T])
        kq_raw = ra("kq_raw", [P, 2, T])
        k_rot = ra("k_rot", [P, 2, T])
        q_rot = ra("q_rot", [P, 2, T])
        rope_v = ra("rope_v", [P, 2, T])
        hc = ra("hc", [P, HC_W])
        state = ra("state", [P, 2, DK])
        kb = ra("kb", [P, 2, DK])
        rb = Area(R2 + RB // 2, R3)
        gate = rb("gate", [P, 2, T])
        ret_out = rb("ret_out", [P, 2, T])
        rope_p = rb("rope_p", [P, 2, T])
        kd = rb("kd", [P, 2, DK])
        vt = rb("vt", [P, 2, DK])
        rc = Area(R3 + RB // 2, R4)
        states = rc("states", [P, DEC_B, 2, DK])
        st = rc("st", [P, 2, P])
        yn = rc("yn", [P, DK])
        xs = rc("xs", [P, 2, TS])
        sa = Area(R5, END)
        swa_rot = sa("swa_rot", [P, 2, T])
        perm = sa("perm", [P, 3, P])
        mask_p = sa("mask_p", [P, 2 * P])
        k2 = sa("k2", [P, 2, T])
        v_tok = sa("v_tok", [P, 6, P])
        k_tok = sa("k_tok", [P, 2, P])
        sinks = sa("sinks", [P, 16])
        sink_s = sa("sink_s", [P, 1])
        qs = sa("qs", [P, DEC_B, 8, DEC_T])
        SX = sa.off
        z_raw = sa("z_raw", [P, T])
        z_tmp = sa("z_tmp", [P, T])
        z_rot = sa("z_rot", [P, T])
        sv_raw = at("sv_raw", [P, T], sa.off)
        lg = sa("lg", [P, 2, 2, 2 * P])
        pt = sa("pt", [P, 2, 2, P])
        sp = Area(SX, END)
        mask_c = sp("mask_c", [P, P])
        mask_n = sp("mask_n", [P, DEC_B, TS])
        kc = sp("kc", [P, 2, P])
        kct = sp("kct", [P, 2, P])
        vc = sp("vc", [P, 2, P])
        ls = sp("ls", [P, 2, 3 * HD])
        ptc = sp("ptc", [P, 2, P])
        ptn = sp("ptn", [TS, 2, P])
        os_ = sp("os_", [P, 8, TS])
        osm = sp("osm", [P, 8, TS])
        ta = Area(R5, END)
        ln_t = ta("ln_t", [P, 2, T])
        ones = ta("ones", [P, P])
        acc_s = ta("acc_s", [P, T])
        acc_q = ta("acc_q", [P, T])
        mean = ta("mean", [P, T])
        rstd = ta("rstd", [P, T])
        ostats = ta("ostats", [P, 5, 24])
        sg = ta("sg", [P, T])
        fu = ta("fu", [P, T])

        G = ctx.enter_context(nc.psum_tensor("G", [P, 2, 2, 512], F32))
        A = ctx.enter_context(nc.psum_tensor("A", [P, 4, 512], F32))

        def gt(par):
            return G[:, par, :, 0:NT]

        def halves(ap):
            return ap.rearrange("p (h t) -> p h t", h=2)

        def f32(ap):
            return ap.bitcast(F32)

        def sem(name):
            return ctx.enter_context(nc.semaphore(name))

        ST6, MV, VE, SD, RS = slice(0, 24), slice(24, 26), slice(26, 27), slice(27, 28), slice(28, 29)

        raw_in = [sem(f"raw_in{i}") for i in range(SLOTS)]
        s_hi, s_lo, s_pe = sem("s_hi"), sem("s_lo"), sem("s_pe")
        g_free = [sem(f"g_free{i}") for i in range(2)]
        dve_c, act_c, pool_c = sem("dve_c"), sem("act_c"), sem("pool_c")
        s_const, s_vecT, s_vec = sem("s_const"), sem("s_vecT"), sem("s_vec")
        x_in = [sem(f"x_in{i}") for i in range(NCH)]
        s_ve0, s_sd0, s_xn, s_xtr, s_xf, s_xh, s_xl = (sem(n) for n in ("s_ve0", "s_sd0", "s_xn", "s_xtr", "s_xf", "s_xh", "s_xl"))
        s_rot_in, s_hc, s_st_in, s_st_out = sem("s_rot_in"), sem("s_hc"), sem("s_st_in"), sem("s_st_out")
        s_kq, s_ropev, s_ropep, s_kvT, s_kv, s_sc, s_mask = (sem(n) for n in ("s_kq", "s_ropev", "s_ropep", "s_kvT", "s_kv", "s_sc", "s_mask"))
        s_out, s_ve, s_sd, s_y, s_stp, s_state, s_yT, s_yTe = (sem(n) for n in ("s_out", "s_ve", "s_sd", "s_y", "s_stp", "s_state", "s_yT", "s_yTe"))
        s_xsp, s_xs, s_kb, s_sbp, s_ss, s_gate, s_gated, s_mh, s_ret = (sem(n) for n in ("s_xsp", "s_xs", "s_kb", "s_sbp", "s_ss", "s_gate", "s_gated", "s_mh", "s_ret"))
        s_ps_out = sem("s_ps_out")
        s_swc, s_zr, s_sw, s_rot, s_ev, s_evd = (sem(n) for n in ("s_swc", "s_zr", "s_sw", "s_rot", "s_ev", "s_evd"))
        s_l, s_lgx, s_negm, s_exp, s_pn, s_tr, s_pt, s_pv, s_smh, s_sml, s_qs = (sem(n) for n in ("s_l", "s_lgx", "s_negm", "s_exp", "s_pn", "s_tr", "s_pt", "s_pv", "s_smh", "s_sml", "s_qs"))
        c_k = [sem(f"c_k{i}") for i in range(2)]
        s_cm, s_kT, s_kTe, s_cl, s_clx, s_cneg, s_cexp, s_cpn, s_ctr, s_cpt, s_cpv, s_os, s_osm, s_omh, s_oml = (
            sem(n) for n in ("s_cm", "s_kT", "s_kTe", "s_cl", "s_clx", "s_cneg", "s_cexp", "s_cpn", "s_ctr", "s_cpt", "s_cpv", "s_os", "s_osm", "s_omh", "s_oml"))
        s_kv_out = sem("s_kv_out")
        s_ones, s_yr, s_acc, s_mu, s_mean, s_dif, s_sq, s_accq, s_var, s_vs, s_sdl, s_rstd, s_nrm, s_h32, s_hh, s_hl, s_yba = (
            sem(n) for n in ("s_ones", "s_yr", "s_acc", "s_mu", "s_mean", "s_dif", "s_sq", "s_accq", "s_var", "s_vs", "s_sdl", "s_rstd", "s_nrm", "s_h32", "s_hh", "s_hl", "s_yba"))
        s_sg, s_fu, s_fh, s_fl, s_add, s_otr, s_ote, s_gb, s_vo, s_so, s_no, s_go, s_bo, s_dout = (
            sem(n) for n in ("s_sg", "s_fu", "s_fh", "s_fl", "s_add", "s_otr", "s_ote", "s_gb", "s_vo", "s_so", "s_no", "s_go", "s_bo", "s_dout"))

        B_SWA = RET_BLOCKS * HEADS
        B_OUT = B_SWA + 10
        B_FFN = B_OUT + KT
        GU, DN = 2 * KP, KT // KP
        B_LOOP = B_FFN + GU
        LOOPS = (GROUPS - 1) // 2
        B_LAST = B_LOOP + LOOPS * 2 * (GU + DN)
        U_IN = KT // 2
        U_FFN = U_IN + B_FFN // 2
        U_LOOP = U_FFN + KP
        U_LAST = U_LOOP + LOOPS * 2 * (KP + KT // 2)
        w_in, w_out = I["w_in"][0], I["w_out"][0]
        w_gate, w_up, w_down = I["w_ffn_gate"][0], I["w_ffn_up"][0], I["w_ffn_down"][0]
        TT = [(N_META + 128 * i, 128) for i in range(4)] + [(TP, TS)]

        def ret_cols(h):
            return [V_COL + h * DK, V_COL + 128 + h * DK, K_COL + h * DK, K_COL + 128 + h * DK,
                    Q_COL + h * DK, Q_COL + 128 + h * DK, G_COL + h * DK, G_COL + 128 + h * DK]

        def wait_apart(eng, s, count, met=s_vec, n=1):
            count = eng.to_reg(count)
            eng.wait_ge(met, n)
            eng.wait_ge(s, count)

        block = ctx.enter_context(nc.Block())

        @block.sync
        def _(sp_):
            def pieces(b, src, col):
                for q in range(SLOTS):
                    wait_apart(sp_, s_lo, b * 4 + (q + 1), s_lo, 4)
                    sp_.dma_start(raw[:, q], src[q * 512:(q + 1) * 512, bass.ds(col, P)].rearrange(
                        "(k p) n -> p k n", p=P)).then_inc(raw_in[q], 16)

            def down(b, g, rb):
                for q in range(SLOTS):
                    sp_.wait_ge(s_lo, b * 4 + (q + 1))
                    sp_.dma_start(raw[:, q], w_down[bass.ds(g * 512, 512), bass.ds(rb * 512 + q * P, P)].rearrange(
                        "(k p) n -> p k n", p=P)).then_inc(raw_in[q], 16)

            def gate_up(b0, g):
                with sp_.Fori(0, KP) as m:
                    pieces(m * 2 + b0, w_gate, g * 512 + m * P)
                    pieces(m * 2 + (b0 + 1), w_up, g * 512 + m * P)

            def downs(b0, g):
                with sp_.Fori(0, DN) as rb_:
                    down(rb_ + b0, g, rb_)

            with sp_.Fori(0, HEADS) as h:
                for z, col in enumerate(ret_cols(h)):
                    pieces(h * RET_BLOCKS + z, w_in, col)
            pieces(B_SWA, w_in, SK_COL)
            pieces(B_SWA + 1, w_in, SV_COL)
            with sp_.Fori(0, 8) as j:
                pieces(j + (B_SWA + 2), w_in, j * P + SQ_COL)
            with sp_.Fori(0, KT) as r:
                pieces(r + B_OUT, w_out, r * P)
            gate_up(B_FFN, 0)
            with sp_.Fori(0, LOOPS) as i:
                b0 = i * (2 * (GU + DN)) + B_LOOP
                gate_up(b0, i * 2 + 1)
                downs(b0 + GU, i * 2)
                gate_up(b0 + GU + DN, i * 2 + 2)
                downs(b0 + 2 * GU + DN, i * 2 + 1)
            downs(B_LAST, GROUPS - 1)

        @block.tensor
        def _(pe):
            def piece(b, q, par, use, hi, lo, first=False):
                pe.wait_ge(s_lo, b * 4 + (q + 5))
                if q == 0:
                    pe.wait_ge(g_free[par], use)
                if first:
                    pe.wait_ge(s_xl, 4 * q + 4)
                for k in range(KP):
                    kk = KP * q + k
                    for w, x, one in ((wh, hi, kk == 0), (wh, lo, False), (wl, hi, False)):
                        for n in range(2):
                            mm = pe.matmul(G[:, par, n, 0:NT], w[:, q, k, :], x[:, kk, n * NT:(n + 1) * NT],
                                           start=one, stop=(kk == KT - 1 and w is wl))
                mm.then_inc(s_pe, 1)

            def tile(b, par, use, hi, lo, **kw):
                for q in range(SLOTS):
                    piece(b, q, par, use, hi, lo, **kw)

            def down(b, gs, use):
                for q in range(SLOTS):
                    pe.wait_ge(s_lo, b * 4 + (q + 5))
                    pe.wait_ge(g_free[q % 2], use + q // 2)
                    for k in range(KP):
                        for w, x, one in ((wh, fh, k == 0), (wh, fl, False), (wl, fh, False)):
                            for n in range(2):
                                mm = pe.matmul(G[:, q % 2, n, 0:NT], w[:, q, k, :], x[:, gs, k, n * NT:(n + 1) * NT],
                                               start=one, stop=(k == KP - 1 and w is wl))
                    mm.then_inc(s_pe, 1)

            pe.wait_ge(s_const, 16 * 5)
            pe.transpose(A[:, 0, 0:4 * KT], vec_rows[:, :], ident[0:4 * KT, 0:4 * KT]).then_inc(s_vecT, 1)
            for k in range(KT):
                if k >= 2:
                    pe.wait_ge(g_free[k % 2], k // 2)
                for c, (t0, n) in enumerate(CHUNKS):
                    if k == 0:
                        pe.wait_ge(s_xn, c + 1)
                    half, col = (0, t0) if c < 4 else (1, t0 - 400)
                    tr = pe.transpose(G[:, k % 2, half, col:col + n], xin[0:n, c, k * P:(k + 1) * P], ident[0:n, 0:n])
                tr.then_inc(s_xtr, 1)

            def part_a(h, c):
                t0, n = CHUNKS[c]
                if c == 0:
                    wait_apart(pe, s_ropev, h * 2 + 2)
                    wait_apart(pe, s_ropep, h * 2 + 2)
                else:
                    wait_apart(pe, s_kv, h * NCH + c)
                for i, x in enumerate((k_rot, k_rot, v_raw, v_raw)):
                    tr = pe.transpose(A[0:n, 0, i * P:(i + 1) * P], x[:, i % 2, t0:t0 + n], ident[:, :])
                tr.then_inc(s_kvT, 1)
                if c == 4:
                    wait_apart(pe, s_yTe, h * NCH + 2)
                elif c > 2:
                    wait_apart(pe, s_yTe, h * NCH + (c - 2))
                if 4 < c:
                    wait_apart(pe, s_yTe, h * NCH + 3)
                if c > 0:
                    wait_apart(pe, s_mask, h * NCH + c)
                for k in range(2):
                    mm = pe.matmul(A[0:n, 1, 0:n], k_rot[:, k, t0:t0 + n], q_rot[:, k, t0:t0 + n],
                                   start=(k == 0), stop=(k == 1))
                mm.then_inc(s_sc, 1)

            def part_b(h, c):
                t0, n = CHUNKS[c]
                wait_apart(pe, s_mask, h * NCH + (c + 1))
                wait_apart(pe, s_kv, h * NCH + (c + 1))
                if c > 0:
                    wait_apart(pe, s_y, h * NCH + c)
                    wait_apart(pe, s_state, h * 5 + c)
                    for k in range(2):
                        pe.matmul(A[0:n, 2, 0:DK], q_rot[:, k, t0:t0 + n], state[:, k, :], start=(k == 0), stop=False)
                pe.matmul(A[0:n, 2, 0:DK], st[0:n, c % 2, 0:n], vt[0:n, c % 2, :],
                          start=(c == 0), stop=True).then_inc(s_out, 1)
                for k in range(2):
                    mm = pe.matmul(A[:, 3, k * DK:(k + 1) * DK], kd[0:n, c % 2, k * P:(k + 1) * P], vt[0:n, c % 2, :],
                                   start=True, stop=True)
                mm.then_inc(s_stp, 1)

            def part_c(h, c, bank=1):
                t0, n = CHUNKS[c]
                wait_apart(pe, s_y, h * NCH + (c + 1))
                if bank == 1:
                    wait_apart(pe, s_mask, h * NCH + min(c + 3, NCH))
                if c > 0:
                    wait_apart(pe, s_yTe, h * NCH + c)
                for e in range(2):
                    tr = pe.transpose(A[:, bank, e * P:e * P + n], yn[0:n, e * P:(e + 1) * P], ident[0:n, 0:n])
                tr.then_inc(s_yT, 1)

            def sample_out(h):
                wait_apart(pe, s_mask, h * NCH + NCH)
                wait_apart(pe, s_kv, h * NCH + NCH)
                wait_apart(pe, s_y, h * NCH + SMP)
                wait_apart(pe, s_st_in, h * (16 * DEC_B) + 16 * DEC_B)
                for e in range(2):
                    pe.matmul(A[:, 2, e * TS:(e + 1) * TS], vt[0:TS, SMP % 2, e * P:(e + 1) * P], st[0:TS, SMP % 2, 0:TS],
                              start=(e == 0), stop=False, skip_group_check=True)
                for b in range(DEC_B):
                    for e in range(2):
                        for k in range(2):
                            c0 = e * TS + b * DEC_T
                            mm = pe.matmul(A[:, 2, c0:c0 + DEC_T], states[:, b, k, e * P:(e + 1) * P],
                                           q_rot[:, k, TP + b * DEC_T:TP + (b + 1) * DEC_T],
                                           start=False, stop=(b == DEC_B - 1 and e == 1 and k == 1), skip_group_check=True)
                mm.then_inc(s_xsp, 1)

            def sample_turn(h):
                wait_apart(pe, s_xs, h + 1)
                wait_apart(pe, s_yTe, h * NCH + SMP)
                for e in range(2):
                    tr = pe.transpose(A[0:TS, 1, e * P:(e + 1) * P], xs[:, e, :], ident[:, :])
                tr.then_inc(s_out, 1)

            def sample_state(h, b):
                bank = (3, 0)[b % 2]
                wait_apart(pe, s_kb, h * DEC_B + (b + 1))
                if b >= 2:
                    wait_apart(pe, s_ss, h * DEC_B + (b - 1))
                if b == 0:
                    wait_apart(pe, s_state, h * 5 + 5)
                for k in range(2):
                    mm = pe.matmul(A[:, bank, k * DK:(k + 1) * DK], kb[0:TS, b % 2, k * P:(k + 1) * P], vt[0:TS, SMP % 2, :],
                                   start=True, stop=True)
                mm.then_inc(s_sbp, 1)

            with pe.Fori(0, HEADS) as h:
                for z in range(6):
                    tile(h * RET_BLOCKS + z, z % 2, h * 4 + (U_IN + z // 2), xh, xl, first=(z == 0))
                for t in range(10):
                    if t < 8:
                        z = 6 + t // 4
                        piece(h * RET_BLOCKS + z, t % 4, z % 2, h * 4 + (U_IN + 3), xh, xl)
                    if 2 <= t < 8:
                        part_a(h, t - 2)
                    if 3 <= t < 8:
                        part_b(h, t - 3)
                    if t == 8:
                        sample_out(h)
                    if 4 <= t < 9:
                        part_c(h, t - 4)
                sample_turn(h)
                for b in range(DEC_B):
                    sample_state(h, b)
                part_c(h, SMP, bank=2)

            tile(B_SWA, 0, U_IN + B_SWA // 2, xh, xl)
            tile(B_SWA + 1, 1, U_IN + B_SWA // 2, xh, xl)

            def swap(src, bank):
                for n in range(2):
                    mm = pe.matmul(A[:, bank + n, 0:NT], perm[:, src, :], (z_raw if src == 0 else z_rot)[:, n * NT:(n + 1) * NT],
                                   start=True, stop=True)
                return mm

            pe.wait_ge(s_swc, 16 * 4)
            pe.wait_ge(g_free[0], U_IN + B_SWA // 2 + 1)
            pe.wait_ge(s_ret, HEADS)
            swap(0, 0).then_inc(s_ev, 1)
            piece(B_SWA + 2, 0, 0, U_IN + B_SWA // 2 + 1, xh, xl)
            pe.wait_ge(g_free[1], U_IN + B_SWA // 2 + 1)
            for n in range(6):
                t0, w = (128 * n, min(128, TP - 128 * n)) if n < 5 else (TP, TS)
                tr = pe.transpose(A[0:w, 2 + n // 4, (n % 4) * P:(n % 4 + 1) * P], sv_raw[:, t0:t0 + w], ident[:, :])
            tr.then_inc(s_ev, 1)
            piece(B_SWA + 2, 1, 0, 0, xh, xl)
            pe.wait_ge(s_rot, 1)
            swap(1, 0).then_inc(s_ev, 1)
            pe.wait_ge(s_evd, 1)
            pe.transpose(A[:, 2, 0:P], z_rot[:, TP - P:TP], ident[:, :])
            pe.transpose(A[0:TS, 2, P:2 * P], z_rot[:, TP:T], ident[:, :]).then_inc(s_ev, 1)
            piece(B_SWA + 2, 2, 0, 0, xh, xl)
            pe.wait_ge(s_evd, 2)
            swap(2, 0).then_inc(s_ev, 1)
            piece(B_SWA + 2, 3, 0, 0, xh, xl)

            def logits(j, n):
                kv = j // 4
                t0, w = 128 * n, min(128, TP - 128 * n)
                k0, k1 = max(0, 128 * (n - 1)), min(TP, 128 * (n + 1))
                c0 = 128 if n == 0 else 0
                if j * 5 + n:
                    pe.wait_ge(s_lgx, j * 5 + n)
                for i in range(2):
                    mm = pe.matmul(A[0:w, 2 + i, c0:c0 + k1 - k0],
                                   z_rot[i * HD:(i + 1) * HD, t0:t0 + w], k2[i * HD:(i + 1) * HD, kv, k0:k1],
                                   start=True, stop=True)
                mm.then_inc(s_l, 1)

            def turn_probs(j, n):
                w = min(128, TP - 128 * n)
                pe.wait_ge(s_pn, j * 5 + n + 1)
                if j * 5 + n:
                    pe.wait_ge(s_pt, j * 5 + n)
                for kt in range(1 if n == 0 else 0, 2):
                    kw = 16 if (n == 4 and kt == 1) else 128
                    for i in range(2):
                        c = (kt * 2 + i) * P
                        tr = pe.transpose(A[0:kw, 0, c:c + w], lg[0:w, n % 2, i, kt * P:kt * P + kw], ident[0:w, 0:w])
                tr.then_inc(s_tr, 1)

            def weigh(j, n):
                kv = j // 4
                w = min(128, TP - 128 * n)
                pe.wait_ge(s_pt, j * 5 + n + 1)
                if j * 5 + n:
                    pe.wait_ge(s_sml, j * 5 + n)
                kts = range(1 if n == 0 else 0, 2)
                for i in range(2):
                    for kt in kts:
                        kw = 16 if (n == 4 and kt == 1) else 128
                        mm = pe.matmul(A[i * HD:(i + 1) * HD, 1, 0:w], v_tok[0:kw, n - 1 + kt, kv * HD:(kv + 1) * HD],
                                       pt[0:kw, kt, i, 0:w], start=(kt == kts[0]), stop=(kt == 1))
                mm.then_inc(s_pv, 1)

            for j in range(8):
                def pc(q):
                    if j < 7:
                        piece(B_SWA + 3 + j, q, (j + 1) % 2, U_IN + (B_SWA + 3 + j) // 2, xh, xl)
                pe.wait_ge(g_free[j % 2], U_IN + (B_SWA + 2 + j) // 2 + 1)
                if j:
                    pe.wait_ge(s_pt, j * 5)
                    pe.wait_ge(s_sml, j * 5)
                else:
                    pe.wait_ge(s_evd, 4)
                swap(0, 0).then_inc(s_sw, 1)
                pc(0)
                pe.wait_ge(s_rot, 2 + j)
                logits(j, 0)
                logits(j, 1)
                pc(1)
                turn_probs(j, 0)
                logits(j, 2)
                pc(2)
                weigh(j, 0)
                turn_probs(j, 1)
                logits(j, 3)
                pc(3)
                weigh(j, 1)
                turn_probs(j, 2)
                logits(j, 4)
                weigh(j, 2)
                turn_probs(j, 3)
                weigh(j, 3)
                turn_probs(j, 4)
                weigh(j, 4)

            def cache_logits(b):
                pe.wait_ge(c_k[b % 2], 32 * (b // 2 + 1))
                if b:
                    pe.wait_ge(s_kTe, b)
                else:
                    pe.wait_ge(s_sml, 40)
                pe.transpose(A[:, 0, 0:P], kc[:, b % 2, :], ident[:, :]).then_inc(s_kT, 1)
                pe.wait_ge(s_kTe, b + 1)
                if b == 0:
                    pe.wait_ge(s_qs, 16 * 16)
                else:
                    pe.wait_ge(s_clx, b)
                for kv in range(2):
                    r = slice(kv * HD, (kv + 1) * HD)
                    q_b = qs[r, b, :, :].rearrange("p r t -> p (r t)")
                    pe.matmul(A[r, 1, 0:P], q_b, kct[r, b % 2, :], start=True, stop=True)
                    mm = pe.matmul(A[r, 1, P:P + TS], q_b, k2[r, kv, TP:T], start=True, stop=True)
                mm.then_inc(s_cl, 1)

            def cache_weigh(b):
                pe.wait_ge(s_cpn, b + 1)
                if b:
                    pe.wait_ge(s_cpt, b)
                pe.transpose(A[:, 2, 0:P], ls[:, b % 2, 0:P], ident[:, :])
                pe.transpose(A[0:TS, 2, P:2 * P], ls[:, b % 2, P:P + TS], ident[:, :]).then_inc(s_ctr, 1)
                pe.wait_ge(s_cpt, b + 1)
                for kv in range(2):
                    r = slice(kv * HD, (kv + 1) * HD)
                    o = A[r, 3, b * TS:(b + 1) * TS]
                    pe.matmul(o, vc[:, b % 2, r], ptc[:, b % 2, r], start=(b == 0), stop=False, skip_group_check=True)
                    mm = pe.matmul(o, v_tok[0:TS, 5, r], ptn[:, b % 2, r], start=False, stop=(b == DEC_B - 1),
                                   skip_group_check=True)
                mm.then_inc(s_cpv, 1)

            for b in range(DEC_B + 1):
                if b < DEC_B:
                    cache_logits(b)
                if b:
                    cache_weigh(b - 1)

            pe.wait_ge(s_oml, 1)
            with pe.Fori(0, KT // 2) as i:
                for par in range(2):
                    tile(i * 2 + (B_OUT + par), par, i + (U_IN + B_OUT // 2), mh, ml)

            def column_sums(acc):
                for n in range(2):
                    mm = pe.matmul(A[:, n, 0:NT], ones[:, :], acc[:, n * NT:(n + 1) * NT], start=True, stop=True)
                return mm

            pe.wait_ge(s_ones, 3)
            pe.wait_ge(s_acc, KT + 1)
            column_sums(acc_s).then_inc(s_mu, 1)
            pe.wait_ge(s_accq, KT)
            pe.wait_ge(s_mean, 1)
            column_sums(acc_q).then_inc(s_var, 1)

            def gate_up(b0, u0, first=False):
                def pair(m):
                    tile(m * 2 + b0, 0, m + u0, hh, hl)
                    tile(m * 2 + (b0 + 1), 1, m + u0, hh, hl)
                with pe.Fori(0, KP) as m:
                    pair(m)

            def downs(b0, u0, gs, fl_count):
                wait_apart(pe, s_fl, fl_count)
                with pe.Fori(0, DN) as r:
                    down(r + b0, gs, r * 2 + u0)

            pe.wait_ge(s_hl, KT)
            gate_up(B_FFN, U_FFN)
            with pe.Fori(0, LOOPS) as i:
                b0 = i * (2 * (GU + DN)) + B_LOOP
                u0 = i * (2 * (KP + KT // 2)) + U_LOOP
                gate_up(b0, u0)
                downs(b0 + GU, u0 + KP, 0, i * 8 + 4)
                gate_up(b0 + GU + DN, u0 + KP + 8)
                downs(b0 + 2 * GU + DN, u0 + 2 * KP + 8, 1, i * 8 + 8)
            pe.wait_ge(s_fl, KP * GROUPS)

            def turn_out(rb_):
                for par in range(2):
                    pe.wait_ge(g_free[par], U_LAST + 2 * rb_ + 2)
                for tt, (t0, n) in enumerate(TT):
                    e = rb_ * 5 + tt
                    if e >= 4:
                        pe.wait_ge(s_ote, e - 3)
                    for q in range(4):
                        tr = pe.transpose(A[0:n, e % 4, q * P:(q + 1) * P], yb[:, rb_ * 4 + q, t0:t0 + n], ident[:, :])
                    tr.then_inc(s_otr, 1)

            for rb_ in range(DN):
                down(B_LAST + rb_, 0, U_LAST + 2 * rb_)
                if rb_:
                    turn_out(rb_ - 1)
            turn_out(DN - 1)

        @block.scalar
        def _(act):
            c = Count(act, act_c)

            def hi(b, q, free=True):
                act.wait_ge(raw_in[q], b * 16 + 16)
                if free:
                    act.wait_ge(s_pe, b * 4 + (q - 3))
                act.copy(wh[:, q], raw[:, q]).then_inc(s_hi, 1)

            def his(b, qs_):
                for q in qs_:
                    hi(b, q)

            for i, (t0, n) in enumerate(CHUNKS):
                src = I["meta_tokens"] if i == 0 else (
                    I["x_sample"].rearrange("b t d -> (b t) d") if i == SMP else I["x_prompt"][0, t0 - N_META:t0 - N_META + n, :])
                act.dma_start(xin[0:n, i, :], src).then_inc(x_in[i], 16)
            for i, (t0, n) in enumerate(CHUNKS):
                act.wait_ge(s_ve0, i + 1)
                act.activation(small[0:n, SD], small[0:n, VE], ACT.Sqrt).then_inc(s_sd0, 1)
            for q in range(SLOTS):
                hi(0, q, free=False)
            act.wait_ge(s_vecT, 1)
            act.copy(vec[:, :, :], A[:, 0, 0:4 * KT].rearrange("p (n k) -> p n k", n=4)).then_inc(s_vec, 1)
            for k in range(KT):
                act.wait_ge(g_free[k % 2], k // 2 + 1)
                act.copy(xh[:, k, :], xf[:, k % 2, :]).then_inc(s_xh, 1)

            def copy_tile(b, par, dst):
                act.wait_ge(s_pe, b * 4 + 4)
                return act.copy(halves(dst), gt(par))

            with act.Fori(0, HEADS) as h:
                for z in range(6):
                    b = h * RET_BLOCKS + z
                    his(b + 1, range(3))
                    if z == 4:
                        act.wait_ge(s_ropev, h * 2 + 1)
                        act.wait_ge(s_ropep, h * 2 + 1)
                    dst = (v_raw, kq_raw, kq_raw)[z // 2][:, z % 2, :]
                    copy_tile(b, z % 2, dst).then_inc(g_free[z % 2], 1)
                    hi(b + 1, 3)

                def tokens_first(i):
                    t0, n = CHUNKS[i]
                    act.wait_ge(s_kvT, h * NCH + (i + 1))
                    if i >= 2 and i < SMP:
                        act.wait_ge(s_stp, h * 5 + (i - 1))
                    if i == SMP:
                        act.wait_ge(s_stp, h * 5 + 4)
                        act.copy(kd[0:n, i % 2, :], A[0:n, 0, 0:DK])
                    else:
                        act.mul(kd[0:n, i % 2, :], A[0:n, 0, 0:DK], hc[0:n, (HC_KD0 if i == 0 else HC_KD):][:, 0:1])
                    act.copy(vt[0:n, i % 2, :], A[0:n, 0, DK:2 * DK]).then_inc(s_kv, 1)

                def root(i):
                    n = CHUNKS[i][1]
                    act.wait_ge(s_ve, h * NCH + (i + 1))
                    act.activation(small[0:n, SD], small[0:n, VE], ACT.Sqrt).then_inc(s_sd, 1)

                act.wait_ge(s_hc, h * 16 + 16)
                for t in range(8):
                    b = h * RET_BLOCKS + 6 + t // 4
                    hi(b + 1, t % 4)
                    if t % 4 == 3:
                        act.wait_ge(s_pe, b * 4 + 4)
                        act.activation(halves(gate[:, t // 4, :]), gt(t // 4), ACT.Silu).then_inc(g_free[t // 4], 1)
                    if 2 <= t:
                        tokens_first(t - 2)
                    if 3 <= t:
                        root(t - 3)
                act.wait_ge(s_xsp, h + 1)
                act.copy(xs[:, :, :], A[:, 2, 0:2 * TS].rearrange("p (e t) -> p e t", e=2)).then_inc(s_xs, 1)
                root(SMP)
                act.wait_ge(s_gated, h + 1)
                act.copy(mh[:, bass.ds(h * 2, 2), :], ret_out[:, :, :]).then_inc(s_mh, 1)

            b = B_SWA
            his(b + 1, range(3))
            act.wait_ge(s_ret, HEADS)
            copy_tile(b, 0, z_raw[:, :]).then_inc(g_free[0], 1)
            hi(b + 1, 3)
            b += 1
            his(b + 1, range(3))
            copy_tile(b, 1, sv_raw[:, :]).then_inc(g_free[1], 1)
            hi(b + 1, 3)
            b += 1
            hi(b + 1, 0)
            act.wait_ge(s_ev, 2)
            act.copy(v_tok[:, 0:4, :], A[:, 2, :].rearrange("p (n d) -> p n d", n=4))
            act.copy(v_tok[0:16, 4, :], A[0:16, 3, 0:P])
            act.copy(v_tok[0:TS, 5, :], A[0:TS, 3, P:2 * P]).then_inc(s_evd, 1)
            hi(b + 1, 1)
            act.wait_ge(s_ev, 3)
            act.copy(halves(k2[:, 0, :]), A[:, 0:2, 0:NT]).then_inc(s_evd, 1)
            act.wait_ge(s_ev, 4)
            act.copy(k_tok[:, 0, :], A[:, 2, 0:P])
            act.copy(k_tok[0:TS, 1, :], A[0:TS, 2, P:2 * P]).then_inc(s_evd, 1)
            hi(b + 1, 2)
            act.wait_ge(s_ev, 5)
            act.copy(halves(k2[:, 1, :]), A[:, 0:2, 0:NT]).then_inc(s_evd, 1)
            act.wait_ge(s_rot, 1)
            copy_tile(b, 0, z_raw[:, :]).then_inc(g_free[0], 1)
            hi(b + 1, 3)

            def exps(j, n):
                w = min(128, TP - 128 * n)
                c0, c1 = (128, 256) if n == 0 else (0, 144 if n == 4 else 256)
                s0 = 40 + 8 * (n % 2)
                act.wait_ge(s_negm, j * 5 + n + 1)
                for i in range(2):
                    act.activation(lg[0:w, n % 2, i, c0:c1], lg[0:w, n % 2, i, c0:c1], ACT.Exp,
                                   bias=small[0:w, s0 + i:s0 + i + 1], accum_out=small[0:w, s0 + 4 + i:s0 + 5 + i])
                act.activation(small[0:w, s0 + 6:s0 + 8], small[0:w, s0 + 2:s0 + 4], ACT.Exp).then_inc(s_exp, 1)

            def keep_probs(j, n):
                w = min(128, TP - 128 * n)
                act.wait_ge(s_tr, j * 5 + n + 1)
                if 0 < n < 4:
                    ins = act.copy(pt[:, :, :, :], A[:, 0, :].rearrange("p (k i q) -> p k i q", k=2, i=2))
                elif n == 0:
                    ins = act.copy(pt[:, 1, :, :], A[:, 0, 2 * P:].rearrange("p (i q) -> p i q", i=2))
                else:
                    v = A[:, 0, :].rearrange("p (k i q) -> p k i q", k=2, i=2)
                    act.copy(pt[:, 0, :, 0:w], v[:, 0, :, 0:w])
                    ins = act.copy(pt[0:16, 1, :, 0:w], v[0:16, 1, :, 0:w])
                ins.then_inc(s_pt, 1)

            def mix_hi(j, n):
                w = min(128, TP - 128 * n)
                act.wait_ge(s_pv, j * 5 + n + 1)
                act.copy(mh[:, 8 + j, 128 * n:128 * n + w], A[:, 1, 0:w]).then_inc(s_smh, 1)

            act.wait_ge(s_st_out, 16 * DEC_B * HEADS)
            for j in range(8):
                b = B_SWA + 3 + j

                def h_(q):
                    if j < 7:
                        hi(b + 1, q)
                h_(0)
                exps(j, 0)
                h_(1)
                exps(j, 1)
                keep_probs(j, 0)
                h_(2)
                exps(j, 2)
                mix_hi(j, 0)
                keep_probs(j, 1)
                if j < 7:
                    copy_tile(b, (j + 1) % 2, z_raw[:, :]).then_inc(g_free[(j + 1) % 2], 1)
                h_(3)
                exps(j, 3)
                mix_hi(j, 1)
                keep_probs(j, 2)
                exps(j, 4)
                mix_hi(j, 2)
                keep_probs(j, 3)
                mix_hi(j, 3)
                keep_probs(j, 4)
                mix_hi(j, 4)

            def cache_exp(b):
                s0 = 60 + 8 * (b % 2)
                act.wait_ge(s_cneg, b + 1)
                act.activation(ls[:, b % 2, :], ls[:, b % 2, :], ACT.Exp, bias=small[:, s0:s0 + 1],
                               accum_out=small[:, s0 + 2:s0 + 3])
                act.activation(small[:, s0 + 3:s0 + 4], small[:, s0 + 1:s0 + 2], ACT.Exp).then_inc(s_cexp, 1)

            for b in range(DEC_B + 1):
                if b < DEC_B:
                    act.wait_ge(s_kT, b + 1)
                    if b == 0:
                        act.wait_ge(s_sml, 40)
                    act.copy(kct[:, b % 2, :], A[:, 0, 0:P]).then_inc(s_kTe, 1)
                    cache_exp(b)
                if b:
                    act.wait_ge(s_ctr, b)
                    act.copy(ptc[:, (b - 1) % 2, :], A[:, 2, 0:P])
                    act.copy(ptn[:, (b - 1) % 2, :], A[0:TS, 2, P:2 * P]).then_inc(s_cpt, 1)
            act.wait_ge(s_cpv, DEC_B)
            act.copy(os_[:, :, :].rearrange("p r (b t) -> p b r t", b=DEC_B),
                     A[:, 3, :].rearrange("p (b r t) -> p b r t", b=DEC_B, r=8)).then_inc(s_os, 1)
            act.wait_ge(s_osm, 64)
            act.copy(mh[:, 8:16, TP:T], osm[:, :, :]).then_inc(s_omh, 1)

            with act.Fori(0, KT // 2) as i:
                for par in range(2):
                    his(i * 2 + (B_OUT + par + 1), range(4))

            for r in range(KT):
                act.wait_ge(s_dif, r + 1)
                if r >= 2:
                    act.wait_ge(s_accq, r - 1)
                act.activation(ln_t[:, r % 2, :], yb[:, r, :], ACT.Square).then_inc(s_sq, 1)
            act.wait_ge(s_vs, 1)
            act.activation(rstd[:, :], rstd[:, :], ACT.Sqrt).then_inc(s_sdl, 1)
            for r in range(KT):
                act.wait_ge(s_nrm, r + 1)
                c.link(act.activation(yb[:, r, :], ln_t[:, r % 2, :], ACT.Identity,
                                      bias=vec[:, 3, r:r + 1], scale=vec[:, 2, r:r + 1]))
                act.copy(hh[:, r, :], yb[:, r, :]).then_inc(s_hh, 1)

            def gate_up(b0, gs, u0):
                with act.Fori(0, KP) as m:
                    b = m * 2 + b0
                    his(b + 1, range(3))
                    act.wait_ge(s_pe, b * 4 + 4)
                    act.activation(halves(sg[:, :]), gt(0), ACT.Silu).then_inc(g_free[0], 1)
                    hi(b + 1, 3)
                    his(b + 2, range(3))
                    act.wait_ge(g_free[1], m + (u0 + 1))
                    act.copy(fh[:, gs, bass.ds(m, 1), :], fu[:, :].rearrange("p (o t) -> p o t", o=1)).then_inc(s_fh, 1)
                    hi(b + 2, 3)

            def downs(b0):
                with act.Fori(0, DN) as r:
                    his(r + (b0 + 1), range(4))

            gate_up(B_FFN, 0, U_FFN)
            with act.Fori(0, LOOPS) as i:
                b0 = i * (2 * (GU + DN)) + B_LOOP
                u0 = i * (2 * (KP + KT // 2)) + U_LOOP
                gate_up(b0, 1, u0)
                downs(b0 + GU)
                gate_up(b0 + GU + DN, 0, u0 + KP + 8)
                downs(b0 + 2 * GU + DN)

            def out_copy(rb_):
                for tt, (t0, n) in enumerate(TT):
                    e = rb_ * 5 + tt
                    act.wait_ge(s_otr, e + 1)
                    act.copy(yo[0:n, tt, rb_ * 512:(rb_ + 1) * 512], A[0:n, e % 4, :]).then_inc(s_ote, 1)

            for rb_ in range(DN):
                if rb_ < DN - 1:
                    his(B_LAST + rb_ + 1, range(4))
                if rb_:
                    out_copy(rb_ - 1)
            out_copy(DN - 1)
            for tt, (t0, n) in enumerate(TT):
                act.wait_ge(s_vo, tt + 1)
                act.activation(small[0:n, 80 + tt:81 + tt], small[0:n, 90 + tt:91 + tt], ACT.Sqrt).then_inc(s_so, 1)

        @block.vector
        def _(dve):
            c = Count(dve, dve_c)

            def lo(b, q):
                dve.wait_ge(s_hi, b * 4 + (q + 1))
                dve.tensor_tensor(wl[:, q], raw[:, q], f32(wh[:, q]), ALU.subtract).then_inc(s_lo, 1)

            def los(b, qs_):
                for q in qs_:
                    lo(b, q)

            dve.memset(small[:, 159:160], 0.0).then_inc(s_lo, 4)

            for i, (t0, n) in enumerate(CHUNKS):
                dve.wait_ge(x_in[i], 16)
                for k in range(4):
                    ins = dve.bn_stats(small[0:n, 6 * k:6 * k + 6], xin[0:n, i, 512 * k:512 * (k + 1)])
                c.link(ins)
                c.link(dve.bn_aggr(small[0:n, MV], small[0:n, ST6]))
                dve.tensor_scalar(small[0:n, VE], small[0:n, 25:26], LN_EPS, None, ALU.add).then_inc(s_ve0, 1)
                dve.wait_ge(s_sd0, i + 1)
                c.link(dve.reciprocal(small[0:n, RS], small[0:n, SD]))
                dve.tensor_scalar(xin[0:n, i, :], xin[0:n, i, :], small[0:n, 24:25], small[0:n, RS],
                                  ALU.subtract, ALU.mult).then_inc(s_xn, 1)
            los(0, range(4))
            dve.wait_ge(s_vec, 1)
            for k in range(KT):
                dve.wait_ge(s_xtr, k + 1)
                if k >= 2:
                    dve.wait_ge(s_xl, k - 1)
                dve.tensor_scalar(xf[:, k % 2, 0:400], G[:, k % 2, 0, 0:400], vec[:, 0, k:k + 1], vec[:, 1, k:k + 1],
                                  ALU.mult, ALU.add)
                dve.tensor_scalar(xf[:, k % 2, 400:T], G[:, k % 2, 1, 0:T - 400], vec[:, 0, k:k + 1],
                                  vec[:, 1, k:k + 1], ALU.mult, ALU.add).then_inc(g_free[k % 2], 1)

            def rope(x, out, count):
                for par in range(2):
                    dve.wait_ge(g_free[par], count)
                dve.tensor_tensor(rope_v[:, 0, :], x[:, 0, :], ret_rot[:, 0, :], ALU.mult)
                c.link(dve.tensor_tensor(rope_v[:, 1, :], x[:, 1, :], ret_rot[:, 1, :], ALU.mult))
                dve.tensor_tensor(out[:, 0, :], rope_v[:, 0, :], rope_v[:, 1, :], ALU.subtract).then_inc(s_ropev, 1)

            with dve.Fori(0, HEADS) as h, c.loop(h, HEADS, PER_HEAD):
                dve.wait_ge(s_rot_in, 16)
                for z in range(6):
                    b = h * RET_BLOCKS + z
                    los(b + 1, range(4))
                    if z in (3, 5):
                        rope(kq_raw, k_rot if z == 3 else q_rot, h * 4 + (U_IN + (2 if z == 3 else 3)))

                def masked(i):
                    n = CHUNKS[i][1]
                    dve.wait_ge(s_sc, h * NCH + (i + 1))
                    if i == SMP:
                        m = hc[0:n, HC_DS:HC_DS + n]
                    else:
                        m = hc[0:n, 0:n]
                    if i >= 2:
                        dve.wait_ge(s_out, h * NCH + (i - 1))
                    dve.tensor_tensor(st[0:n, i % 2, 0:n], A[0:n, 1, 0:n], m, ALU.mult).then_inc(s_mask, 1)

                def norm(i):
                    n = CHUNKS[i][1]
                    src = A[0:n, 1 if i == SMP else 2, 0:DK]
                    dve.wait_ge(s_out, h * NCH + (i + 1))
                    c.link(dve.bn_stats(small[0:n, 0:6], src), met=s_vec)
                    c.link(dve.bn_aggr(small[0:n, MV], small[0:n, 0:6]))
                    e = HC_EPSS if i == SMP else HC_EPS
                    dve.tensor_tensor(small[0:n, VE], small[0:n, 25:26], hc[0:n, e:e + 1], ALU.add).then_inc(s_ve, 1)
                    dve.wait_ge(s_sd, h * NCH + (i + 1))
                    c.link(dve.reciprocal(small[0:n, RS], small[0:n, SD]))
                    if i:
                        dve.wait_ge(s_yT, h * NCH + i)
                    dve.tensor_scalar(yn[0:n, :], src, small[0:n, 24:25], small[0:n, RS],
                                      ALU.subtract, ALU.mult).then_inc(s_y, 1)

                def new_state(i):
                    dve.wait_ge(s_stp, h * 5 + (i + 1))
                    sv = A[:, 3, :].rearrange("p (k e) -> p k e", k=2)
                    if i == 0:
                        dve.tensor_copy(state[:, :, :], sv).then_inc(s_state, 1)
                    else:
                        dve.scalar_tensor_tensor(out=state[:, :, :], in0=state[:, :, :], scalar=hc[:, HC_G:HC_G + 1],
                                                 in1=sv, op0=ALU.mult, op1=ALU.add).then_inc(s_state, 1)

                def turned(i, bank=1):
                    t0, n = CHUNKS[i]
                    dve.wait_ge(s_yT, h * NCH + (i + 1))
                    dve.tensor_copy(ret_out[:, :, t0:t0 + n],
                                    A[:, bank, 0:DK].rearrange("p (e t) -> p e t", e=2)[:, :, 0:n]).then_inc(s_yTe, 1)

                def own_keys(b):
                    dve.tensor_scalar(kb[0:TS, b % 2, :], kd[0:TS, SMP % 2, :], hc[0:TS, HC_KB + b:HC_KB + b + 1], None,
                                      ALU.mult).then_inc(s_kb, 1)

                def sample_state(b):
                    bank = (3, 0)[b % 2]
                    dve.wait_ge(s_sbp, h * DEC_B + (b + 1))
                    dve.scalar_tensor_tensor(out=states[:, b], in0=states[:, b], scalar=hc[:, HC_GS:HC_GS + 1],
                                             in1=A[:, bank, :].rearrange("p (k e) -> p k e", k=2),
                                             op0=ALU.mult, op1=ALU.add).then_inc(s_ss, 1)

                dve.wait_ge(s_hc, h * 16 + 16)
                for t in range(8):
                    lo(h * RET_BLOCKS + (7 + t // 4), t % 4)
                    if 2 <= t:
                        masked(t - 2)
                    if 3 <= t:
                        norm(t - 3)
                        new_state(t - 3)
                    if 4 <= t:
                        turned(t - 4)
                turned(4)
                dve.wait_ge(s_kv, h * NCH + NCH)
                own_keys(0)
                own_keys(1)
                norm(SMP)
                for b in range(DEC_B):
                    sample_state(b)
                    if b + 2 < DEC_B:
                        own_keys(b + 2)
                turned(SMP, bank=2)
                for par in range(2):
                    dve.wait_ge(g_free[par], h * 4 + (U_IN + 4))
                dve.wait_ge(s_yTe, h * NCH + NCH)
                dve.tensor_tensor(ret_out[:, :, :], ret_out[:, :, :], gate[:, :, :], ALU.mult).then_inc(s_gated, 1)
                dve.wait_ge(s_mh, h + 1)
                dve.tensor_tensor(ml[:, bass.ds(h * 2, 2), :], ret_out[:, :, :], f32(mh[:, bass.ds(h * 2, 2), :]),
                                  ALU.subtract).then_inc(s_ret, 1)

            def rotate(count, sem_, val):
                dve.wait_ge(sem_, val)
                dve.tensor_tensor(halves(z_tmp[:, :]), A[:, 0:2, 0:NT], halves(swa_rot[:, 1, :]), ALU.mult)
                c.link(dve.tensor_tensor(z_rot[:, :], z_raw[:, :], swa_rot[:, 0, :], ALU.mult))
                dve.tensor_tensor(z_rot[:, :], z_rot[:, :], z_tmp[:, :], ALU.add).then_inc(s_rot, 1)

            los(B_SWA + 1, range(4))
            los(B_SWA + 2, range(4))
            dve.wait_ge(s_swc, 16 * 4)
            rotate(1, s_ev, 1)
            los(B_SWA + 3, range(4))

            def soft_a(j, n):
                w = min(128, TP - 128 * n)
                c0, c1 = (128, 256) if n == 0 else (0, 144 if n == 4 else 256)
                s0 = 40 + 8 * (n % 2)
                l = lg[0:w, n % 2, :, c0:c1]
                dve.wait_ge(s_l, j * 5 + n + 1)
                dve.scalar_tensor_tensor(out=l, in0=A[0:w, 2:4, c0:c1],
                                         scalar=HD ** -0.5, in1=mask_p[0:w, None, c0:c1].to_broadcast([w, 2, c1 - c0]),
                                         op0=ALU.mult, op1=ALU.add).then_inc(s_lgx, 1)
                dve.wait_ge(s_lgx, j * 5 + n + 1)
                c.link(dve.tensor_reduce(small[0:w, s0:s0 + 2], l, AX_X, ALU.max))
                c.link(dve.tensor_tensor(small[0:w, s0:s0 + 2], small[0:w, s0:s0 + 2], sinks[0:w, 2 * j:2 * j + 2], ALU.max))
                c.link(dve.tensor_tensor(small[0:w, s0 + 2:s0 + 4], sinks[0:w, 2 * j:2 * j + 2], small[0:w, s0:s0 + 2],
                                         ALU.subtract))
                dve.tensor_scalar(small[0:w, s0:s0 + 2], small[0:w, s0:s0 + 2], -1.0, None, ALU.mult).then_inc(s_negm, 1)

            def soft_b(j, n):
                w = min(128, TP - 128 * n)
                c0, c1 = (128, 256) if n == 0 else (0, 144 if n == 4 else 256)
                s0 = 40 + 8 * (n % 2)
                dve.wait_ge(s_exp, j * 5 + n + 1)
                c.link(dve.tensor_tensor(small[0:w, s0 + 4:s0 + 6], small[0:w, s0 + 4:s0 + 6], small[0:w, s0 + 6:s0 + 8], ALU.add))
                c.link(dve.reciprocal(small[0:w, s0 + 4:s0 + 6], small[0:w, s0 + 4:s0 + 6]))
                for i in range(2):
                    ins = dve.tensor_scalar(lg[0:w, n % 2, i, c0:c1], lg[0:w, n % 2, i, c0:c1],
                                            small[0:w, s0 + 4 + i:s0 + 5 + i], None, ALU.mult)
                ins.then_inc(s_pn, 1)

            def mix_lo(j, n):
                w = min(128, TP - 128 * n)
                dve.wait_ge(s_smh, j * 5 + n + 1)
                dve.tensor_tensor(ml[:, 8 + j, 128 * n:128 * n + w], A[:, 1, 0:w], f32(mh[:, 8 + j, 128 * n:128 * n + w]),
                                  ALU.subtract).then_inc(s_sml, 1)

            dve.wait_ge(s_st_out, 16 * DEC_B * HEADS)
            for j in range(8):
                b = B_SWA + 4 + j

                def l_(q):
                    if j < 7:
                        lo(b, q)
                if j:
                    dve.wait_ge(s_qs, 32 * j)
                rotate(2 + j, s_sw, 1 + j)
                l_(0)
                soft_a(j, 0)
                soft_a(j, 1)
                soft_b(j, 0)
                l_(1)
                soft_b(j, 1)
                soft_a(j, 2)
                l_(2)
                mix_lo(j, 0)
                soft_b(j, 2)
                soft_a(j, 3)
                l_(3)
                mix_lo(j, 1)
                soft_b(j, 3)
                soft_a(j, 4)
                mix_lo(j, 2)
                soft_b(j, 4)
                mix_lo(j, 3)
                mix_lo(j, 4)

            dve.wait_ge(s_cm, 16 * 3)
            for b in range(DEC_B):
                s0 = 60 + 8 * (b % 2)
                dve.wait_ge(s_cl, b + 1)
                dve.scalar_tensor_tensor(out=ls[:, b % 2, 0:P], in0=A[:, 1, 0:P], scalar=HD ** -0.5, in1=mask_c[:, :],
                                         op0=ALU.mult, op1=ALU.add)
                dve.scalar_tensor_tensor(out=ls[:, b % 2, P:P + TS], in0=A[:, 1, P:P + TS], scalar=HD ** -0.5,
                                         in1=mask_n[:, b, :], op0=ALU.mult, op1=ALU.add).then_inc(s_clx, 1)
                dve.wait_ge(s_clx, b + 1)
                c.link(dve.tensor_reduce(small[:, s0:s0 + 1], ls[:, b % 2, :], AX_X, ALU.max))
                c.link(dve.tensor_tensor(small[:, s0:s0 + 1], small[:, s0:s0 + 1], sink_s[:, :], ALU.max))
                c.link(dve.tensor_tensor(small[:, s0 + 1:s0 + 2], sink_s[:, :], small[:, s0:s0 + 1], ALU.subtract))
                dve.tensor_scalar(small[:, s0:s0 + 1], small[:, s0:s0 + 1], -1.0, None, ALU.mult).then_inc(s_cneg, 1)
                dve.wait_ge(s_cexp, b + 1)
                c.link(dve.tensor_tensor(small[:, s0 + 2:s0 + 3], small[:, s0 + 2:s0 + 3], small[:, s0 + 3:s0 + 4], ALU.add))
                c.link(dve.reciprocal(small[:, s0 + 2:s0 + 3], small[:, s0 + 2:s0 + 3]))
                dve.tensor_scalar(ls[:, b % 2, :], ls[:, b % 2, :], small[:, s0 + 2:s0 + 3], None, ALU.mult).then_inc(s_cpn, 1)
            dve.wait_ge(s_omh, 1)
            dve.tensor_tensor(ml[:, 8:16, TP:T], osm[:, :, :], f32(mh[:, 8:16, TP:T]), ALU.subtract).then_inc(s_oml, 1)

            dve.wait_ge(s_oml, 1)
            dve.memset(ones[:, :], 1.0 / D).then_inc(s_ones, 1)
            dve.memset(acc_s[:, :], 0.0).then_inc(s_ones, 1)
            dve.memset(acc_q[:, :], 0.0).then_inc(s_ones, 1)
            with dve.Fori(0, KT // 2) as i, c.loop(i, KT // 2, 2):
                for par in range(2):
                    b = i * 2 + (B_OUT + par)
                    r = bass.ds(i * 2 + par, 1)
                    los(b + 1, range(3))
                    y = yb[:, r, :].rearrange("p o (h t) -> p (o h) t", h=2)
                    c.link(dve.tensor_tensor(yb[:, r, :], f32(xh[:, r, :]), f32(xl[:, r, :]), ALU.add))
                    dve.wait_ge(s_pe, b * 4 + 4)
                    dve.scalar_tensor_tensor(out=y, in0=y, scalar=ALPHA, in1=gt(par), op0=ALU.mult,
                                             op1=ALU.add).then_inc(g_free[par], 1)
                    lo(b + 1, 3)

            dve.wait_ge(s_mu, 1)
            dve.tensor_copy(halves(mean[:, :]), A[:, 0:2, 0:NT]).then_inc(s_mean, 1)
            dve.wait_ge(s_mean, 1)
            for r in range(KT):
                dve.tensor_tensor(yb[:, r, :], yb[:, r, :], mean[:, :], ALU.subtract).then_inc(s_dif, 1)
            dve.wait_ge(s_var, 1)
            dve.tensor_scalar(halves(rstd[:, :]), A[:, 0:2, 0:NT], LN_EPS, None, ALU.add).then_inc(s_vs, 1)
            dve.wait_ge(s_sdl, 1)
            c.link(dve.reciprocal(rstd[:, :], rstd[:, :]))

            def split_h(r):
                dve.wait_ge(s_hh, r + 1)
                dve.tensor_tensor(hl[:, r, :], yb[:, r, :], f32(hh[:, r, :]), ALU.subtract).then_inc(s_hl, 1)

            for r in range(KT):
                dve.tensor_tensor(ln_t[:, r % 2, :], yb[:, r, :], rstd[:, :], ALU.mult).then_inc(s_nrm, 1)
                if r:
                    split_h(r - 1)
            split_h(KT - 1)

            def gate_up(b0, gs, u0, m0):
                with dve.Fori(0, KP) as m:
                    b = m * 2 + b0
                    los(b + 1, range(4))
                    los(b + 2, range(3))
                    dve.wait_ge(g_free[0], m + (u0 + 1))
                    dve.wait_ge(s_pe, b * 4 + 8)
                    dve.tensor_tensor(halves(fu[:, :]), gt(1), halves(sg[:, :]), ALU.mult).then_inc(g_free[1], 1)
                    lo(b + 2, 3)
                    dve.wait_ge(s_fh, m + m0 + 1)
                    dve.tensor_tensor(fl[:, gs, bass.ds(m, 1), :], fu[:, :].rearrange("p (o t) -> p o t", o=1),
                                      f32(fh[:, gs, bass.ds(m, 1), :]), ALU.subtract).then_inc(s_fl, 1)

            def add(b, q, r):
                dve.wait_ge(s_pe, b * 4 + (q + 1))
                y = yb[:, r, :].rearrange("p o (h t) -> p (o h) t", h=2)
                return dve.tensor_tensor(y, y, gt(q % 2), ALU.add)

            def downs(b0):
                with dve.Fori(0, DN) as rb_:
                    b = rb_ + b0
                    for q in range(SLOTS):
                        add(b, q, bass.ds(rb_ * 4 + q, 1)).then_inc(g_free[q % 2], 1)
                        lo(b + 1, q)

            dve.wait_ge(s_yba, KT)
            gate_up(B_FFN, 0, U_FFN, 0)
            with dve.Fori(0, LOOPS) as i:
                b0 = i * (2 * (GU + DN)) + B_LOOP
                u0 = i * (2 * (KP + KT // 2)) + U_LOOP
                gate_up(b0, 1, u0, i * 8 + 4)
                downs(b0 + GU)
                gate_up(b0 + GU + DN, 0, u0 + KP + 8, i * 8 + 8)
                downs(b0 + 2 * GU + DN)

            def out_stats(rb_):
                for tt, (t0, n) in enumerate(TT):
                    dve.wait_ge(s_ote, rb_ * 5 + tt + 1)
                    ins = dve.bn_stats(ostats[0:n, tt, 6 * rb_:6 * rb_ + 6], yo[0:n, tt, rb_ * 512:(rb_ + 1) * 512])
                return ins

            for rb_ in range(DN):
                for q in range(SLOTS):
                    add(B_LAST + rb_, q, slice(rb_ * 4 + q, rb_ * 4 + q + 1)).then_inc(g_free[q % 2], 1)
                    if rb_ < DN - 1:
                        lo(B_LAST + rb_ + 1, q)
                if rb_:
                    out_stats(rb_ - 1)
            c.link(out_stats(DN - 1))
            for tt, (t0, n) in enumerate(TT):
                c.link(dve.bn_aggr(small[0:n, 100 + 2 * tt:102 + 2 * tt], ostats[0:n, tt, :]))
                dve.tensor_scalar(small[0:n, 90 + tt:91 + tt], small[0:n, 101 + 2 * tt:102 + 2 * tt], LN_EPS, None,
                                  ALU.add).then_inc(s_vo, 1)
            dve.wait_ge(s_gb, 32)
            for tt, (t0, n) in enumerate(TT):
                dve.wait_ge(s_so, tt + 1)
                c.link(dve.reciprocal(small[0:n, 80 + tt:81 + tt], small[0:n, 80 + tt:81 + tt]))
                c.link(dve.scalar_tensor_tensor(out=yo[0:n, tt, :], in0=yo[0:n, tt, :], scalar=small[0:n, 100 + 2 * tt:101 + 2 * tt],
                                                in1=g_row[0:n, :], op0=ALU.subtract, op1=ALU.mult))
                dve.scalar_tensor_tensor(out=yo[0:n, tt, :], in0=yo[0:n, tt, :], scalar=small[0:n, 80 + tt:81 + tt],
                                         in1=b_row[0:n, :], op0=ALU.mult, op1=ALU.add).then_inc(s_no, 1)

        @block.gpsimd
        def _(pool):
            c = Count(pool, pool_c)
            pool.dma_start(ident[:, :], I["c_ident"]).then_inc(s_const, 16)
            for n, name in enumerate(("ln_emb_g", "ln_emb_b", "ln_mix_g", "ln_mix_b")):
                src = I[name] if n < 2 else I[name][0]
                pool.dma_start(vec_rows[n * KT:(n + 1) * KT, :], src.rearrange("(k p) -> k p", p=P)).then_inc(s_const, 16)
            for k in range(KT):
                pool.wait_ge(s_xh, k + 1)
                pool.tensor_tensor(xl[:, k, :], xf[:, k % 2, :], f32(xh[:, k, :]), ALU.subtract).then_inc(s_xl, 1)
            pool.wait_ge(s_xl, KT)
            pool.dma_start(ret_rot[:, :, :], I["c_ret_rot"]).then_inc(s_rot_in, 16)

            def rope(x, out, count):
                for par in range(2):
                    pool.wait_ge(g_free[par], count)
                pool.tensor_tensor(rope_p[:, 0, :], x[:, 1, :], ret_rot[:, 0, :], ALU.mult)
                c.link(pool.tensor_tensor(rope_p[:, 1, :], x[:, 0, :], ret_rot[:, 1, :], ALU.mult))
                pool.tensor_tensor(out[:, 1, :], rope_p[:, 0, :], rope_p[:, 1, :], ALU.add).then_inc(s_ropep, 1)

            pool.wait_ge(s_rot_in, 16)
            pool.wait_ge(s_xtr, KT)
            with pool.Fori(0, HEADS) as h, c.loop(h, HEADS, 2):
                pool.dma_start(hc[:, :], I["c_head"][bass.ds(h, 1), :, :].rearrange("o p n -> p (o n)")).then_inc(s_hc, 16)
                for b in range(DEC_B):
                    pool.dma_start(states[:, b], I["state_ret"][0, b, bass.ds(h, 1), :, :].rearrange(
                        "o (k p) e -> p (o k) e", p=P)).then_inc(s_st_in, 16)
                rope(kq_raw, k_rot, h * 4 + (U_IN + 2))
                rope(kq_raw, q_rot, h * 4 + (U_IN + 3))
                wait_apart(pool, s_state, h * 5 + 5)
                pool.dma_start(O["ret_p"][0, 0, bass.ds(h, 1), :, :].rearrange("o (k p) e -> p (o k) e", p=P),
                               state[:, :, :]).then_inc(s_ps_out, 16)
                for b in range(DEC_B):
                    wait_apart(pool, s_ss, h * DEC_B + (b + 1))
                    pool.dma_start(O["ret_s"][0, b, bass.ds(h, 1), :, :].rearrange("o (k p) e -> p (o k) e", p=P),
                                   states[:, b]).then_inc(s_st_out, 16)
                wait_apart(pool, s_st_out, h * (16 * DEC_B) + 16 * DEC_B)
                wait_apart(pool, s_ps_out, h * 16 + 16)
                wait_apart(pool, s_ret, h + 1)

            pool.wait_ge(s_ps_out, 16 * HEADS)
            pool.dma_start(swa_rot[:, :, :], I["c_swa_rot"]).then_inc(s_swc, 16)
            pool.dma_start(perm[:, :, :], I["c_perm"]).then_inc(s_swc, 16)
            pool.dma_start(mask_p[:, :], I["c_mask_p"]).then_inc(s_swc, 16)
            pool.dma_start(sinks[:, :], I["swa_sinks"].to_broadcast([P, 16])).then_inc(s_swc, 16)
            pool.wait_ge(s_evd, 3)
            kp = O["k_p"][0, 0].rearrange("t k d -> t (k d)")
            vp = O["v_p"][0, 0].rearrange("t k d -> t (k d)")
            pool.dma_start(kp, k_tok[:, 0, :]).then_inc(s_kv_out, 16)
            pool.dma_start(vp[0:112, :], v_tok[16:128, 3, :]).then_inc(s_kv_out, 16)
            pool.dma_start(vp[112:128, :], v_tok[0:16, 4, :]).then_inc(s_kv_out, 16)
            for b in range(DEC_B):
                r = slice(b * DEC_T, (b + 1) * DEC_T)
                for o, new, old in ((O["k_s"], k_tok[r, 1, :], I["cache_swa_k"]), (O["v_s"], v_tok[r, 5, :], I["cache_swa_v"])):
                    pool.dma_start(o[0, b, WINDOW - DEC_T:, :, :].rearrange("t k d -> t (k d)"), new).then_inc(s_kv_out, 16)
            for o, old in ((O["k_s"], I["cache_swa_k"]), (O["v_s"], I["cache_swa_v"])):
                pool.dma_start(o[0, :, 0:WINDOW - DEC_T].rearrange("b t k d -> b (t k d)"),
                               old[0, :, DEC_T:].rearrange("b t k d -> b (t k d)")).then_inc(s_kv_out, 16)
            for j in range(8):
                kv = j // 4
                pool.wait_ge(s_rot, 2 + j)
                for i in range(2):
                    pool.dma_start(qs[kv * HD:(kv + 1) * HD, :, 2 * (j % 4) + i, :],
                                   z_rot[i * HD:(i + 1) * HD, TP:T].rearrange("p (b t) -> p b t", b=DEC_B))\
                        .then_inc(s_qs, 16)
            pool.wait_ge(s_sml, 40)
            pool.wait_ge(s_qs, 16 * 16)
            pool.dma_start(mask_c[:, :], I["c_mask_c"]).then_inc(s_cm, 16)
            pool.dma_start(mask_n[:, :, :], I["c_mask_n"]).then_inc(s_cm, 16)
            pool.dma_start(sink_s[:, :], I["swa_sinks"].rearrange("o (h u) -> (o h) u", u=1)[:, None, :].to_broadcast([16, 8, 1]))\
                .then_inc(s_cm, 16)
            for b in range(DEC_B):
                if b >= 2:
                    pool.wait_ge(s_cpv, b - 1)
                pool.dma_start(kc[:, b % 2, :], I["cache_swa_k"][0, b].rearrange("t k d -> t (k d)")).then_inc(c_k[b % 2], 16)
                pool.dma_start(vc[:, b % 2, :], I["cache_swa_v"][0, b].rearrange("t k d -> t (k d)")).then_inc(c_k[b % 2], 16)
            pool.wait_ge(s_os, 1)
            for kv in range(2):
                for i in range(2):
                    pool.dma_start(osm[i * HD:(i + 1) * HD, kv * 4:kv * 4 + 4, :], os_[kv * HD:(kv + 1) * HD, i:8:2, :])\
                        .then_inc(s_osm, 16)

            pool.wait_ge(s_ones, 3)
            pool.memset(small[:, 158:159], 0.0).then_inc(s_acc, 1)
            acc_o = acc_s[:, :].rearrange("p (o t) -> p o t", o=1)
            with pool.Fori(0, KT // 2) as i:
                for par in range(2):
                    pool.wait_ge(g_free[par], i + (U_IN + B_OUT // 2 + 1))
                    pool.wait_ge(s_acc, i * 2 + (par + 1))
                    pool.tensor_tensor(acc_o, acc_o, yb[:, bass.ds(i * 2 + par, 1), :], ALU.add).then_inc(s_acc, 1)
            for r in range(KT):
                pool.wait_ge(s_sq, r + 1)
                if r:
                    pool.wait_ge(s_accq, r)
                pool.tensor_tensor(acc_q[:, :], acc_q[:, :], ln_t[:, r % 2, :], ALU.add).then_inc(s_accq, 1)
            for r in range(KT):
                pool.wait_ge(s_hl, r + 1)
                pool.tensor_scalar(yb[:, r, :], yb[:, r, :], ALPHA, None, ALU.mult).then_inc(s_yba, 1)

            pool.wait_ge(s_pe, 4 * B_LAST)
            for row, name in ((g_row, "ln_ffn_g"), (b_row, "ln_ffn_b")):
                pool.dma_start(row[:, :], I[name].to_broadcast([P, D])).then_inc(s_gb, 16)
            for tt, (t0, n) in enumerate(TT):
                pool.wait_ge(s_no, tt + 1)
                dst = O["y_s"].rearrange("b t d -> (b t) d") if tt == 4 else O["y_p"][0, t0 - N_META:t0 - N_META + n, :]
                pool.dma_start(dst, yo[0:n, tt, :]).then_inc(s_dout, 16)
            pool.wait_ge(s_dout, 16 * 5)
            pool.wait_ge(s_kv_out, 16 * (3 + 2 * DEC_B + 2))
            pool.wait_ge(s_ps_out, 16 * HEADS)
            pool.wait_ge(s_st_out, 16 * DEC_B * HEADS)


_INS = ["x_prompt", "x_sample", "state_ret", "cache_swa_k", "cache_swa_v", "meta_tokens", "ln_emb_g", "ln_emb_b",
        "w_in", "w_out", "swa_sinks", "ln_mix_g", "ln_mix_b", "w_ffn_gate", "w_ffn_up", "w_ffn_down", "ln_ffn_g", "ln_ffn_b"]
_OUTS = [("y_p", (1, SEQ, D)), ("y_s", (DEC_B, DEC_T, D)), ("ret_p", (1, 1, HEADS, DK, DK)), ("k_p", (1, 1, WINDOW, 2, HD)),
         ("v_p", (1, 1, WINDOW, 2, HD)), ("ret_s", (1, DEC_B, HEADS, DK, DK)), ("k_s", (1, DEC_B, WINDOW, 2, HD)),
         ("v_s", (1, DEC_B, WINDOW, 2, HD))]


def kernel(**inputs):
    import concourse.bacc as bacc
    from concourse.bass_utils import run_bass_kernel_spmd

    nc = bacc.Bacc("TRN2", target_bir_lowering=False, num_devices=1)
    arrays = {n: np.ascontiguousarray(inputs[n]) for n in _INS}
    arrays.update(shape_constants())
    ins = {n: nc.dram_tensor(f"in_{n}", a.shape, F32, kind="ExternalInput").ap() for n, a in arrays.items()}
    outs = {n: nc.dram_tensor(f"out_{n}", s, F32, kind="ExternalOutput").ap() for n, s in _OUTS}
    hymba_step_kernel(nc, ins, outs)
    r = run_bass_kernel_spmd(nc, [{f"in_{n}": a for n, a in arrays.items()}], core_ids=[0])
    return tuple(r.results[0][f"out_{n}"] for n, _ in _OUTS)
```

```python
from contextlib import ExitStack, contextmanager

import numpy as np

import concourse.bass as bass
from concourse import mybir

F32 = mybir.dt.float32
F32R = mybir.dt.float32r
ALU = mybir.AluOpType
ACT = mybir.ActivationFunctionType
AX_X = mybir.AxisListType.X

P = 128
D = 2048
SEQ, N_META = 512, 16
DEC_B, DEC_T = 8, 8
PAST = 4096
HEADS, DK = 4, 256
HD, WINDOW, ROT = 64, 128, 16
FFN = 5632
LN_EPS = 1e-5
ALPHA = 2.0 ** 0.25

TP = N_META + SEQ
TS = DEC_B * DEC_T
T = TP + TS
NT = T // 2
KT = D // P
KP = 4
SLOTS = 4
HT = FFN // P
GROUPS = HT // KP
Q_COL, K_COL, V_COL, G_COL = 0, 1024, 2048, 3072
SQ_COL, SK_COL, SV_COL = 4096, 5120, 5248
RET_BLOCKS = 8
CHUNKS = [(0, N_META)] + [(N_META + 128 * c, 128) for c in range(4)] + [(TP, TS)]
NCH = len(CHUNKS)
IN_TILES = [128, 128, 128, 128, TS + N_META]
XF_SLOTS = 4
SMP = NCH - 1
HC_KD, HC_KD0, HC_EPS, HC_G, HC_W = 128, 129, 130, 131, 132
HS_EPS, HS_G, HS_KB = TS, TS + 1, TS + 2
HS_W = HS_KB + DEC_B

PER_HEAD = 2 + 3 * NCH
SAMPLE_STEPS = 12
LN_PIECES = (5, 7, 9, 11, 13, 15)
CACHE_SLOTS = 3


def shape_constants():
    f = np.float32
    pos = np.concatenate([np.arange(TP), np.tile(PAST + np.arange(DEC_T), DEC_B)]).astype(f)
    rf = np.power(f(10000.0), -np.linspace(0.0, 1.0, DK // 2, dtype=f)).astype(f)
    ang = (pos[None, :] * rf[:, None]).astype(f).astype(np.float64)
    ret_rot = np.stack([np.cos(ang), np.sin(ang)], 1).astype(f)
    half = ROT // 2
    sf = np.power(f(500000.0), -np.arange(0, ROT, 2, dtype=f) / f(ROT)).astype(f)
    sang = (pos[None, :] * sf[:, None]).astype(f).astype(np.float64)
    swa_rot = np.zeros((P, 2, T), f)
    swa_rot[:, 0] = 1.0
    swap = np.zeros((P, P), f)
    for b in (0, HD):
        for i in range(half):
            swa_rot[b + i, 0] = swa_rot[b + half + i, 0] = np.cos(sang[i])
            swa_rot[b + i, 1] = -np.sin(sang[i])
            swa_rot[b + half + i, 1] = np.sin(sang[i])
            swap[b + half + i, b + i] = swap[b + i, b + half + i] = 1.0
    perm = np.zeros((P, 3, P), f)
    perm[:, 0] = swap
    for kv in range(2):
        for i in range(HD):
            perm[kv * HD + i, 1 + kv, i] = perm[kv * HD + i, 1 + kv, HD + i] = 1.0
    gam = 1.0 - 2.0 ** (-5.0 - np.arange(HEADS, dtype=np.float64))
    hc = np.zeros((HEADS, P, HC_W + HS_W), np.float64)
    j = np.arange(P)[:, None]
    i = np.arange(P)[None, :]
    t = np.arange(P) % DEC_T
    bb = np.arange(P) // DEC_T
    for h in range(HEADS):
        g = gam[h]
        hc[h, :, 0:128] = (i >= j) * g ** -(j + 1.0) / 16.0
        ok = (bb[:, None] == bb[None, :64]) & (t[None, :64] >= t[:, None]) & (np.arange(P)[:, None] < TS)
        hc[h, :, HC_W:HC_W + TS] = ok * (g ** -(t + 1.0))[:, None] / 16.0
        hc[h, :, HC_KD] = g ** (127.0 - np.arange(P)) / 16.0
        hc[h, :N_META, HC_KD0] = g ** (N_META - 1.0 - np.arange(N_META)) / 16.0
        hc[h, :, HC_EPS] = LN_EPS * g ** (-2.0 * (np.arange(P) + 1.0))
        hc[h, :, HC_W + HS_EPS] = LN_EPS * g ** (-2.0 * (t + 1.0))
        hc[h, :, HC_G] = g ** 128
        hc[h, :, HC_W + HS_G] = g ** DEC_T
        for b in range(DEC_B):
            hc[h, :, HC_W + HS_KB + b] = (bb == b) * g ** (DEC_T - 1.0 - t) / 16.0
    neg = f(-1e30)
    q = np.arange(P)[:, None]
    kk = np.arange(2 * P)[None, :]
    diff = q + P - kk
    mask_p = np.where((diff >= 0) & (diff < WINDOW), f(0), neg).astype(f)
    tq = (np.arange(P) % DEC_T)[:, None]
    pc = np.arange(P)[None, :]
    mask_c = np.where(tq + P - pc < WINDOW, f(0), neg).astype(f)
    mask_n = np.full((P, DEC_B, TS), neg, f)
    for b in range(DEC_B):
        for u in range(DEC_T):
            mask_n[:, b, b * DEC_T + u] = np.where(tq[:, 0] >= u, f(0), neg)
    return {
        "c_ret_rot": ret_rot, "c_swa_rot": swa_rot, "c_perm": perm, "c_head": hc.astype(f),
        "c_mask_p": mask_p, "c_mask_c": mask_c, "c_mask_n": mask_n, "c_ident": np.eye(P, dtype=f),
    }


class Count:

    def __init__(self, eng, sem):
        self.eng, self.sem, self.base, self.n = eng, sem, 0, 0

    def link(self, ins, met=None):
        self.n += 1
        ins.then_inc(self.sem, 1)
        value = self.base + self.n
        if met is not None and not isinstance(value, int):
            value = self.eng.to_reg(value)
            self.eng.wait_ge(met, 1)
        self.eng.wait_ge(self.sem, value)

    @contextmanager
    def loop(self, i, times, per):
        base, n = self.base, self.n
        self.base, self.n = i * per + (base + n), 0
        yield
        assert self.n == per, f"{self.n} links in a loop of {per}"
        self.base, self.n = base, n + times * per


def hymba_step_kernel(nc, I, O):
    with ExitStack() as ctx:
        RB = KT * T * 4
        R0, R1, R2, R3, R4 = (n * RB for n in range(5))
        END = 212800
        base = -(-nc.sbuf_base // 32) * 32
        slab = ctx.enter_context(nc.sbuf_tensor("slab", [P, END // 4], F32))

        def at(name, shape, off, dt=F32):
            return nc.alloc_sbuf_tensor_at(name, shape, dt, offset=base + off)

        class Area:

            def __init__(self, off, end):
                self.off, self.end = off, end

            def __call__(self, name, shape, dt=F32):
                a = at(name, shape, self.off, dt)
                self.off += (4 * int(np.prod(shape[1:])) + 31) // 32 * 32
                assert self.off <= self.end, (name, self.off, self.end)
                return a

        xh, xl = at("xh", [P, KT, T], R0, F32R), at("xl", [P, KT, T], R1, F32R)
        mh, ml = at("mh", [P, KT, T], R2, F32R), at("ml", [P, KT, T], R3, F32R)
        yb = at("yb", [P, KT, T], R1)
        hh, hl = at("hh", [P, KT, T], R2, F32R), at("hl", [P, KT, T], R3, F32R)
        fh, fl = at("fh", [P, 2, KP, T], R0, F32R), at("fl", [P, 2, KP, T], R0 + RB // 2, F32R)
        g_row, b_row = at("g_row", [P, D], R0 + RB // 4), at("b_row", [P, D], R0 + 3 * RB // 4)
        xin = at("xin", [P, len(IN_TILES), D], R2)
        yo = at("yo", [P, 5, D], R2)

        PIECE = KP * P * 4
        raw = at("raw", [P, SLOTS, KP, P], R4)
        wh = at("wh", [P, SLOTS, KP, P], R4 + SLOTS * PIECE, F32R)
        wl = at("wl", [P, SLOTS, KP, P], R4 + 2 * SLOTS * PIECE, F32R)

        keep = Area(R4 + 3 * SLOTS * PIECE, END)
        ident = keep("ident", [P, P])
        vec = keep("vec", [P, 4, KT])
        small = keep("small", [P, 160])
        R5 = keep.off
        ia = Area(R5, END)
        xf = ia("xf", [P, XF_SLOTS, T])
        vec_rows = ia("vec_rows", [4 * KT, P])
        ra = Area(R5, END)
        ret_rot = ra("ret_rot", [P, 2, T])
        v_raw = ra("v_raw", [P, 2, T])
        kq_raw = ra("kq_raw", [P, 2, T])
        k_rot = ra("k_rot", [P, 2, T])
        q_rot = ra("q_rot", [P, 2, T])
        rope_v = ra("rope_v", [P, 2, T])
        hc = ra("hc", [P, HC_W])
        state = ra("state", [P, 2, DK])
        rb = Area(R2 + RB // 2, R3)
        gate = rb("gate", [P, 2, T])
        ret_out = rb("ret_out", [P, 2, T])
        rope_p = rb("rope_p", [P, 2, T])
        kd = rb("kd", [P, 2, DK])
        vt = rb("vt", [P, 2, DK])
        hcs = rb("hcs", [P, HS_W])
        st_s = rb("st_s", [TS, TS])
        rd = Area(R2 + 6 * T * 4, R2 + RB // 2)
        kb = rd("kb", [P, 2, DK])
        kd_s = rd("kd_s", [P, DK])
        vt_s = rd("vt_s", [P, DK])
        rc = Area(R3 + RB // 2, R4)
        states = rc("states", [P, DEC_B, 2, DK])
        st = rc("st", [P, 2, P])
        yn = rc("yn", [P, DK])
        xs = rc("xs", [P, 2, TS])
        sa = Area(R5, END)
        swa_rot = sa("swa_rot", [P, 2, T])
        perm = sa("perm", [P, 3, P])
        mask_p = sa("mask_p", [P, 2 * P])
        k2 = sa("k2", [P, 2, T])
        v_tok = sa("v_tok", [P, 6, P])
        k_tok = sa("k_tok", [P, 2, P])
        sinks = sa("sinks", [P, 16])
        sink_s = sa("sink_s", [P, 1])
        qs = sa("qs", [P, DEC_B, 8, DEC_T])
        SX = sa.off
        z_raw = sa("z_raw", [P, T])
        z_tmp = sa("z_tmp", [P, T])
        z_rot = sa("z_rot", [P, T])
        sv_raw = at("sv_raw", [P, T], sa.off)
        lg = sa("lg", [P, 2, 2, 2 * P])
        pt = sa("pt", [P, 2, 2, P])
        mask_c = sa("mask_c", [P, P])
        kc = sa("kc", [P, CACHE_SLOTS, P])
        vc = sa("vc", [P, CACHE_SLOTS, P])
        sp = Area(SX, END)
        mask_n = sp("mask_n", [P, DEC_B, TS])
        kct = sp("kct", [P, 2, P])
        ls = sp("ls", [P, 2, 3 * HD])
        ptc = sp("ptc", [P, 2, P])
        ptn = sp("ptn", [TS, 2, P])
        os_ = sp("os_", [P, 8, TS])
        osm = sp("osm", [P, 8, TS])
        ta = Area(R5, END)
        ln_t = ta("ln_t", [P, 2, T])
        ones = ta("ones", [P, P])
        shift = ta("shift", [P, T])
        msq = ta("msq", [P, T])
        acc_s = ta("acc_s", [P, T])
        acc_q = ta("acc_q", [P, T])
        mean = ta("mean", [P, T])
        rstd = ta("rstd", [P, T])
        ostats = ta("ostats", [P, 5, 24])
        sg = ta("sg", [P, T])
        fu = ta("fu", [P, T])

        G = ctx.enter_context(nc.psum_tensor("G", [P, 2, 2, 512], F32))
        A = ctx.enter_context(nc.psum_tensor("A", [P, 4, 512], F32))

        def gt(par):
            return G[:, par, :, 0:NT]

        def halves(ap):
            return ap.rearrange("p (h t) -> p h t", h=2)

        def f32(ap):
            return ap.bitcast(F32)

        def sem(name):
            return ctx.enter_context(nc.semaphore(name))

        def in_col(what, i, n=1):
            return slice(100 + 5 * i + what, 100 + 5 * i + what + n)

        ST6, MV, VE, SD, RS = slice(0, 24), slice(24, 26), slice(26, 27), slice(27, 28), slice(28, 29)

        raw_in = [sem(f"raw_in{i}") for i in range(SLOTS)]
        s_hi, s_lo, s_pe = sem("s_hi"), sem("s_lo"), sem("s_pe")
        g_free = [sem(f"g_free{i}") for i in range(2)]
        dve_c, act_c, pool_c = sem("dve_c"), sem("act_c"), sem("pool_c")
        s_const, s_vecT, s_vec = sem("s_const"), sem("s_vecT"), sem("s_vec")
        x_in = [sem(f"x_in{i}") for i in range(len(IN_TILES))]
        s_ve0, s_sd0, s_xn, s_xtr, s_xf, s_xh, s_xl = (sem(n) for n in ("s_ve0", "s_sd0", "s_xn", "s_xtr", "s_xf", "s_xh", "s_xl"))
        s_rot_in, s_hc, s_st_in, s_st_out = sem("s_rot_in"), sem("s_hc"), sem("s_st_in"), sem("s_st_out")
        s_kq, s_ropev, s_ropep, s_kvT, s_kv, s_sc, s_mask = (sem(n) for n in ("s_kq", "s_ropev", "s_ropep", "s_kvT", "s_kv", "s_sc", "s_mask"))
        s_out, s_ve, s_sd, s_y, s_stp, s_state, s_yT, s_yTe = (sem(n) for n in ("s_out", "s_ve", "s_sd", "s_y", "s_stp", "s_state", "s_yT", "s_yTe"))
        s_xsp, s_xs, s_kb, s_sbp, s_ss, s_gate, s_gated, s_mh, s_ret = (sem(n) for n in ("s_xsp", "s_xs", "s_kb", "s_sbp", "s_ss", "s_gate", "s_gated", "s_mh", "s_ret"))
        s_ps_out, s_hcs = sem("s_ps_out"), sem("s_hcs")
        s_xm, s_zc = sem("s_xm"), sem("s_zc")
        s_shp, s_shift, s_sub, s_cen, s_msq = (sem(n) for n in ("s_shp", "s_shift", "s_sub", "s_cen", "s_msq"))
        s_swc, s_zr, s_sw, s_rot, s_ev, s_evd = (sem(n) for n in ("s_swc", "s_zr", "s_sw", "s_rot", "s_ev", "s_evd"))
        s_l, s_lgx, s_negm, s_exp, s_pn, s_tr, s_pt, s_pv, s_smh, s_sml, s_qs = (sem(n) for n in ("s_l", "s_lgx", "s_negm", "s_exp", "s_pn", "s_tr", "s_pt", "s_pv", "s_smh", "s_sml", "s_qs"))
        c_k = [sem(f"c_k{i}") for i in range(CACHE_SLOTS)]
        s_cm, s_kT, s_kTe, s_cl, s_clx, s_cneg, s_cexp, s_cpn, s_ctr, s_cpt, s_cpv, s_os, s_osm, s_omh, s_oml = (
            sem(n) for n in ("s_cm", "s_kT", "s_kTe", "s_cl", "s_clx", "s_cneg", "s_cexp", "s_cpn", "s_ctr", "s_cpt", "s_cpv", "s_os", "s_osm", "s_omh", "s_oml"))
        s_kv_out = sem("s_kv_out")
        s_ones, s_yr, s_acc, s_mu, s_mean, s_dif, s_sq, s_accq, s_var, s_vs, s_sdl, s_rstd, s_nrm, s_h32, s_hh, s_hl, s_yba = (
            sem(n) for n in ("s_ones", "s_yr", "s_acc", "s_mu", "s_mean", "s_dif", "s_sq", "s_accq", "s_var", "s_vs", "s_sdl", "s_rstd", "s_nrm", "s_h32", "s_hh", "s_hl", "s_yba"))
        s_sg, s_fu, s_fh, s_fl, s_add, s_otr, s_ote, s_gb, s_vo, s_so, s_no, s_go, s_bo, s_dout = (
            sem(n) for n in ("s_sg", "s_fu", "s_fh", "s_fl", "s_add", "s_otr", "s_ote", "s_gb", "s_vo", "s_so", "s_no", "s_go", "s_bo", "s_dout"))

        B_SWA = RET_BLOCKS * HEADS
        B_OUT = B_SWA + 10
        B_FFN = B_OUT + KT
        GU, DN = 2 * KP, KT // KP
        B_LOOP = B_FFN + GU
        LOOPS = (GROUPS - 1) // 2
        B_LAST = B_LOOP + LOOPS * 2 * (GU + DN)
        U_IN = KT // 2
        U_OUT = U_IN + B_OUT // 2
        U_OUT2 = U_OUT + KT // 2
        U_FFN = U_OUT2 + KT // 2
        U_LOOP = U_FFN + KP
        U_LAST = U_LOOP + LOOPS * 2 * (KP + KT // 2)
        w_in, w_out = I["w_in"][0], I["w_out"][0]
        w_gate, w_up, w_down = I["w_ffn_gate"][0], I["w_ffn_up"][0], I["w_ffn_down"][0]
        TT = [(N_META + 128 * i, 128) for i in range(4)] + [(TP, TS)]

        def ret_cols(h):
            return [V_COL + h * DK, V_COL + 128 + h * DK, K_COL + h * DK, K_COL + 128 + h * DK,
                    Q_COL + h * DK, Q_COL + 128 + h * DK, G_COL + h * DK, G_COL + 128 + h * DK]

        def third_piece(b):
            return b % 2 == 0 and b < DEC_B

        def wait_apart(eng, s, count, met=s_vec, n=1):
            if isinstance(count, int):
                eng.wait_ge(s, count)
                return
            count = eng.to_reg(count)
            eng.wait_ge(met, n)
            eng.wait_ge(s, count)

        block = ctx.enter_context(nc.Block())

        @block.sync
        def _(sp_):
            def pieces(b, src, col):
                for q in range(SLOTS):
                    wait_apart(sp_, s_lo, b * 4 + (q + 1), s_lo, 4)
                    sp_.dma_start(raw[:, q], src[q * 512:(q + 1) * 512, bass.ds(col, P)].rearrange(
                        "(k p) n -> p k n", p=P)).then_inc(raw_in[q], 16)

            def down(b, g, rb):
                for q in range(SLOTS):
                    sp_.wait_ge(s_lo, b * 4 + (q + 1))
                    sp_.dma_start(raw[:, q], w_down[bass.ds(g * 512, 512), bass.ds(rb * 512 + q * P, P)].rearrange(
                        "(k p) n -> p k n", p=P)).then_inc(raw_in[q], 16)

            def out_pieces(b, i, half):
                for q in range(SLOTS):
                    wait_apart(sp_, s_lo, b * 4 + (q + 1), s_lo, 4)
                    r0 = half * (D // 2) + q % 2 * 512
                    sp_.dma_start(raw[:, q], w_out[r0:r0 + 512, bass.ds(i * 256 + q // 2 * P, P)].rearrange(
                        "(k p) n -> p k n", p=P)).then_inc(raw_in[q], 16)

            def gate_up(b0, g, m0=0):
                with sp_.Fori(m0, KP) as m:
                    pieces(m * 2 + b0, w_gate, g * 512 + m * P)
                    pieces(m * 2 + (b0 + 1), w_up, g * 512 + m * P)

            def downs(b0, g):
                with sp_.Fori(0, DN) as rb_:
                    down(rb_ + b0, g, rb_)

            with sp_.Fori(0, HEADS) as h:
                for z, col in enumerate(ret_cols(h)):
                    pieces(h * RET_BLOCKS + z, w_in, col)
            pieces(B_SWA, w_in, SK_COL)
            pieces(B_SWA + 1, w_in, SV_COL)
            with sp_.Fori(0, 8) as j:
                pieces(j + (B_SWA + 2), w_in, j * P + SQ_COL)
            for half in range(2):
                with sp_.Fori(0, KT // 2) as i:
                    out_pieces(i + (B_OUT + half * (KT // 2)), i, half)
            for p in range(2 * SLOTS):
                sp_.wait_ge(s_lo, B_FFN * 4 + (p + 1))
                sp_.dma_start(raw[:, p % SLOTS], (w_gate, w_up)[p % 2][p // 2 * 512:(p // 2 + 1) * 512, 0:P].rearrange(
                    "(k p) n -> p k n", p=P)).then_inc(raw_in[p % SLOTS], 16)
            gate_up(B_FFN, 0, 1)
            with sp_.Fori(0, LOOPS) as i:
                b0 = i * (2 * (GU + DN)) + B_LOOP
                gate_up(b0, i * 2 + 1)
                downs(b0 + GU, i * 2)
                gate_up(b0 + GU + DN, i * 2 + 2)
                downs(b0 + 2 * GU + DN, i * 2 + 1)
            downs(B_LAST, GROUPS - 1)

        @block.tensor
        def _(pe):
            def piece(b, q, par, use, hi, lo, first=False, ks=(0, KP)):
                if ks[0] == 0:
                    pe.wait_ge(s_lo, b * 4 + (q + 5))
                    if q == 0:
                        pe.wait_ge(g_free[par], use)
                if first:
                    pe.wait_ge(s_xl, 4 * q + 4)
                for k in range(*ks):
                    kk = KP * q + k
                    for w, x, one in ((wh, hi, kk == 0), (wh, lo, False), (wl, hi, False)):
                        for n in range(2):
                            mm = pe.matmul(G[:, par, n, 0:NT], w[:, q, k, :], x[:, kk, n * NT:(n + 1) * NT],
                                           start=one, stop=(kk == KT - 1 and w is wl))
                if ks[1] == KP:
                    mm.then_inc(s_pe, 1)

            def tile(b, par, use, hi, lo, **kw):
                for q in range(SLOTS):
                    piece(b, q, par, use, hi, lo, **kw)

            def down(b, gs, use, then=None):
                for q in range(SLOTS):
                    pe.wait_ge(s_lo, b * 4 + (q + 5))
                    pe.wait_ge(g_free[q % 2], use + q // 2)
                    for k in range(KP):
                        for w, x, one in ((wh, fh, k == 0), (wh, fl, False), (wl, fh, False)):
                            for n in range(2):
                                mm = pe.matmul(G[:, q % 2, n, 0:NT], w[:, q, k, :], x[:, gs, k, n * NT:(n + 1) * NT],
                                               start=one, stop=(k == KP - 1 and w is wl))
                    mm.then_inc(s_pe, 1)
                    if then:
                        then[q]()

            def out_piece(b, q, use, half, ks=(0, KP)):
                if ks[0] == 0:
                    pe.wait_ge(s_lo, b * 4 + (q + 5))
                    if q % 2 == 0:
                        pe.wait_ge(g_free[q // 2], use)
                for k in range(*ks):
                    kk = half * (KT // 2) + q % 2 * KP + k
                    for w, x, one in ((wh, mh, q % 2 == 0 and k == 0), (wh, ml, False), (wl, mh, False)):
                        for n in range(2):
                            mm = pe.matmul(G[:, q // 2, n, 0:NT], w[:, q, k, :], x[:, kk, n * NT:(n + 1) * NT],
                                           start=one, stop=(q % 2 == 1 and k == KP - 1 and w is wl))
                if ks[1] == KP:
                    mm.then_inc(s_pe, 1)

            pe.wait_ge(s_const, 16 * 5)
            pe.transpose(A[:, 0, 0:4 * KT], vec_rows[:, :], ident[0:4 * KT, 0:4 * KT]).then_inc(s_vecT, 1)
            for k in range(KT):
                if k >= 2:
                    pe.wait_ge(g_free[k % 2], k // 2)
                for c, n in enumerate(IN_TILES):
                    if k == 0:
                        pe.wait_ge(s_xn, c + 1)
                    half, col = (c // 3, c % 3 * 128)
                    tr = pe.transpose(G[:, k % 2, half, col:col + n], xin[0:n, c, k * P:(k + 1) * P], ident[0:n, 0:n])
                tr.then_inc(s_xtr, 1)

            def part_a(h, c):
                t0, n = CHUNKS[c]
                if c == 0:
                    wait_apart(pe, s_ropev, h * 2 + 2)
                    wait_apart(pe, s_ropep, h * 2 + 2)
                else:
                    wait_apart(pe, s_kv, h * NCH + c)
                for i, x in enumerate((k_rot, k_rot, v_raw, v_raw)):
                    tr = pe.transpose(A[0:n, 0, i * P:(i + 1) * P], x[:, i % 2, t0:t0 + n], ident[:, :])
                tr.then_inc(s_kvT, 1)
                if c == 4:
                    wait_apart(pe, s_yTe, h * NCH + 2)
                elif c > 2:
                    wait_apart(pe, s_yTe, h * NCH + (c - 2))
                if 4 < c:
                    wait_apart(pe, s_yTe, h * NCH + 3)
                if c > 0:
                    wait_apart(pe, s_mask, h * NCH + c)
                for k in range(2):
                    mm = pe.matmul(A[0:n, 1, 0:n], k_rot[:, k, t0:t0 + n], q_rot[:, k, t0:t0 + n],
                                   start=(k == 0), stop=(k == 1))
                mm.then_inc(s_sc, 1)

            def part_b(h, c):
                t0, n = CHUNKS[c]
                wait_apart(pe, s_mask, h * NCH + (c + 1))
                wait_apart(pe, s_kv, h * NCH + (c + 1))
                if c > 0:
                    wait_apart(pe, s_y, h * NCH + c)
                    wait_apart(pe, s_state, h * 5 + c)
                    for k in range(2):
                        pe.matmul(A[0:n, 2, 0:DK], q_rot[:, k, t0:t0 + n], state[:, k, :], start=(k == 0), stop=False)
                pe.matmul(A[0:n, 2, 0:DK], st[0:n, c % 2, 0:n], vt[0:n, c % 2, :],
                          start=(c == 0), stop=True).then_inc(s_out, 1)
                for k in range(2):
                    mm = pe.matmul(A[:, 3, k * DK:(k + 1) * DK], kd[0:n, c % 2, k * P:(k + 1) * P], vt[0:n, c % 2, :],
                                   start=True, stop=True)
                mm.then_inc(s_stp, 1)

            def part_c(h, c, bank=1):
                t0, n = CHUNKS[c]
                wait_apart(pe, s_y, h * NCH + (c + 1))
                if bank == 1:
                    wait_apart(pe, s_mask, h * NCH + min(c + 3, NCH))
                if c > 0:
                    wait_apart(pe, s_yTe, h * NCH + c)
                for e in range(2):
                    tr = pe.transpose(A[:, bank, e * P:e * P + n], yn[0:n, e * P:(e + 1) * P], ident[0:n, 0:n])
                tr.then_inc(s_yT, 1)

            def sample_out(h):
                wait_apart(pe, s_mask, h * NCH + NCH)
                wait_apart(pe, s_kv, h * NCH + NCH)
                wait_apart(pe, s_y, h * NCH + SMP)
                wait_apart(pe, s_st_in, h * (16 * DEC_B) + 16 * DEC_B)
                for e in range(2):
                    pe.matmul(A[:, 2, e * TS:(e + 1) * TS], vt_s[0:TS, e * P:(e + 1) * P], st_s[:, :],
                              start=(e == 0), stop=False, skip_group_check=True)
                for b in range(DEC_B):
                    for e in range(2):
                        for k in range(2):
                            c0 = e * TS + b * DEC_T
                            mm = pe.matmul(A[:, 2, c0:c0 + DEC_T], states[:, b, k, e * P:(e + 1) * P],
                                           q_rot[:, k, TP + b * DEC_T:TP + (b + 1) * DEC_T],
                                           start=False, stop=(b == DEC_B - 1 and e == 1 and k == 1), skip_group_check=True)
                mm.then_inc(s_xsp, 1)

            def sample_turn(h):
                wait_apart(pe, s_xs, h + 1)
                wait_apart(pe, s_yTe, h * NCH + SMP)
                for e in range(2):
                    tr = pe.transpose(A[0:TS, 1, e * P:(e + 1) * P], xs[:, e, :], ident[:, :])
                tr.then_inc(s_out, 1)

            def sample_state(h, b):
                bank = (3, 0)[b % 2]
                wait_apart(pe, s_kb, h * DEC_B + (b + 1))
                if b >= 2:
                    wait_apart(pe, s_ss, h * DEC_B + (b - 1))
                if b == 0:
                    wait_apart(pe, s_state, h * 5 + 5)
                for k in range(2):
                    mm = pe.matmul(A[:, bank, k * DK:(k + 1) * DK], kb[0:TS, b % 2, k * P:(k + 1) * P], vt_s[0:TS, :],
                                   start=True, stop=True)
                mm.then_inc(s_sbp, 1)

            def sample_step(h, i):
                if i == 0:
                    part_c(h, 4)
                elif i == 1:
                    sample_out(h)
                elif i == 2:
                    sample_turn(h)
                elif i < 3 + DEC_B:
                    sample_state(h, i - 3)
                elif i == 3 + DEC_B:
                    part_c(h, SMP, bank=2)

            def values_keys_queries(h, last=None):
                for z in range(6):
                    for q in range(SLOTS):
                        piece(h * RET_BLOCKS + z, q, z % 2, h * 4 + (U_IN + z // 2), xh, xl, first=(last is None and z == 0))
                        if last is not None:
                            sample_step(last, 4 * z + q)

            def prompt(h):
                for t in range(8):
                    z = 6 + t // 4
                    piece(h * RET_BLOCKS + z, t % 4, z % 2, h * 4 + (U_IN + 3), xh, xl)
                    if 2 <= t:
                        part_a(h, t - 2)
                    if 3 <= t:
                        part_b(h, t - 3)
                    if 4 <= t:
                        part_c(h, t - 4)

            values_keys_queries(0)
            prompt(0)
            with pe.Fori(0, HEADS - 1) as i:
                values_keys_queries(i + 1, i)
                prompt(i + 1)

            for i in range(SAMPLE_STEPS):
                b = B_SWA + i // 4
                piece(b, i % 4, b % 2, U_IN + b // 2, xh, xl)
                sample_step(HEADS - 1, i)

            def swap(src, bank):
                for n in range(2):
                    mm = pe.matmul(A[:, bank + n, 0:NT], perm[:, src, :], (z_raw if src == 0 else z_rot)[:, n * NT:(n + 1) * NT],
                                   start=True, stop=True)
                return mm

            piece(B_SWA + 3, 0, 1, U_IN + B_SWA // 2 + 1, xh, xl)
            pe.wait_ge(s_swc, 16 * 4)
            pe.wait_ge(g_free[0], U_IN + B_SWA // 2 + 1)
            pe.wait_ge(s_ret, HEADS)
            swap(0, 0).then_inc(s_ev, 1)
            piece(B_SWA + 3, 1, 1, 0, xh, xl)
            pe.wait_ge(g_free[1], U_IN + B_SWA // 2 + 1)
            for n in range(6):
                t0, w = (128 * n, min(128, TP - 128 * n)) if n < 5 else (TP, TS)
                tr = pe.transpose(A[0:w, 2 + n // 4, (n % 4) * P:(n % 4 + 1) * P], sv_raw[:, t0:t0 + w], ident[:, :])
            tr.then_inc(s_ev, 1)
            piece(B_SWA + 3, 2, 1, 0, xh, xl)
            pe.wait_ge(s_rot, 1)
            swap(1, 0).then_inc(s_ev, 1)
            pe.wait_ge(s_evd, 1)
            pe.transpose(A[:, 2, 0:P], z_rot[:, TP - P:TP], ident[:, :])
            pe.transpose(A[0:TS, 2, P:2 * P], z_rot[:, TP:T], ident[:, :]).then_inc(s_ev, 1)
            piece(B_SWA + 3, 3, 1, 0, xh, xl)
            pe.wait_ge(s_evd, 2)
            swap(2, 0).then_inc(s_ev, 1)

            def logits(j, n):
                kv = j // 4
                t0, w = 128 * n, min(128, TP - 128 * n)
                k0, k1 = max(0, 128 * (n - 1)), min(TP, 128 * (n + 1))
                c0 = 128 if n == 0 else 0
                if j * 5 + n:
                    pe.wait_ge(s_lgx, j * 5 + n)
                for i in range(2):
                    mm = pe.matmul(A[0:w, 2 + i, c0:c0 + k1 - k0],
                                   z_rot[i * HD:(i + 1) * HD, t0:t0 + w], k2[i * HD:(i + 1) * HD, kv, k0:k1],
                                   start=True, stop=True)
                mm.then_inc(s_l, 1)

            def turn_probs(j, n):
                w = min(128, TP - 128 * n)
                pe.wait_ge(s_pn, j * 5 + n + 1)
                if j * 5 + n:
                    pe.wait_ge(s_pt, j * 5 + n)
                for kt in range(1 if n == 0 else 0, 2):
                    kw = 16 if (n == 4 and kt == 1) else 128
                    for i in range(2):
                        c = (kt * 2 + i) * P
                        tr = pe.transpose(A[0:kw, 0, c:c + w], lg[0:w, (j + n) % 2, i, kt * P:kt * P + kw], ident[0:w, 0:w])
                tr.then_inc(s_tr, 1)

            def weigh(j, n):
                kv = j // 4
                w = min(128, TP - 128 * n)
                pe.wait_ge(s_pt, j * 5 + n + 1)
                if j * 5 + n:
                    pe.wait_ge(s_sml, j * 5 + n)
                kts = range(1 if n == 0 else 0, 2)
                for i in range(2):
                    for kt in kts:
                        kw = 16 if (n == 4 and kt == 1) else 128
                        mm = pe.matmul(A[i * HD:(i + 1) * HD, 1, 0:w], v_tok[0:kw, n - 1 + kt, kv * HD:(kv + 1) * HD],
                                       pt[0:kw, kt, i, 0:w], start=(kt == kts[0]), stop=(kt == 1))
                mm.then_inc(s_pv, 1)

            def ret_out_piece(p, ks=(0, KP)):
                out_piece(B_OUT + p // 4, p % 4, U_OUT + p // 4, 0, ks)

            for j in range(8):
                def half_piece(i):
                    ks = (0, KP // 2) if i % 2 == 0 else (KP // 2, KP)
                    if j < 6:
                        piece(B_SWA + 4 + j, i // 2, j % 2, U_IN + (B_SWA + 4 + j) // 2, xh, xl, ks=ks)
                    else:
                        ret_out_piece(4 * (j - 6) + i // 2, ks)

                half_piece(0)
                if j:
                    weigh(j - 1, 3)
                half_piece(1)
                pe.wait_ge(g_free[j % 2], U_IN + (B_SWA + 2 + j) // 2 + 1)
                if j:
                    pe.wait_ge(s_pt, j * 5 - 1)
                    pe.wait_ge(s_sml, j * 5 - 1)
                else:
                    pe.wait_ge(s_evd, 4)
                swap(0, 0).then_inc(s_sw, 1)
                half_piece(2)
                pe.wait_ge(s_rot, 2 + j)
                if j:
                    turn_probs(j - 1, 4)
                logits(j, 0)
                if j:
                    weigh(j - 1, 4)
                half_piece(3)
                logits(j, 1)
                half_piece(4)
                turn_probs(j, 0)
                logits(j, 2)
                weigh(j, 0)
                half_piece(5)
                turn_probs(j, 1)
                logits(j, 3)
                half_piece(6)
                weigh(j, 1)
                turn_probs(j, 2)
                logits(j, 4)
                half_piece(7)
                weigh(j, 2)
                turn_probs(j, 3)
            ret_pieces = iter(range(8, 4 * (KT // 2)))
            ret_out_piece(next(ret_pieces))
            weigh(7, 3)
            turn_probs(7, 4)
            ret_out_piece(next(ret_pieces))
            weigh(7, 4)

            def cache_turn(b):
                pe.wait_ge(c_k[b % CACHE_SLOTS], 32 * (b // CACHE_SLOTS + 1))
                if b:
                    pe.wait_ge(s_kTe, b)
                else:
                    pe.wait_ge(s_sml, 40)
                pe.transpose(A[:, 0, 0:P], kc[:, b % CACHE_SLOTS, :], ident[:, :]).then_inc(s_kT, 1)

            def cache_logits(b):
                pe.wait_ge(s_kTe, b + 1)
                if b == 0:
                    pe.wait_ge(s_qs, 16 * 16)
                else:
                    pe.wait_ge(s_clx, b)
                for kv in range(2):
                    r = slice(kv * HD, (kv + 1) * HD)
                    q_b = qs[r, b, :, :].rearrange("p r t -> p (r t)")
                    pe.matmul(A[r, 1, 0:P], q_b, kct[r, b % 2, :], start=True, stop=True)
                    mm = pe.matmul(A[r, 1, P:P + TS], q_b, k2[r, kv, TP:T], start=True, stop=True)
                mm.then_inc(s_cl, 1)

            def cache_probs(b):
                pe.wait_ge(s_cpn, b + 1)
                if b:
                    pe.wait_ge(s_cpt, b)
                pe.transpose(A[:, 2, 0:P], ls[:, b % 2, 0:P], ident[:, :])
                pe.transpose(A[0:TS, 2, P:2 * P], ls[:, b % 2, P:P + TS], ident[:, :]).then_inc(s_ctr, 1)

            def cache_weigh(b):
                pe.wait_ge(s_cpt, b + 1)
                for kv in range(2):
                    r = slice(kv * HD, (kv + 1) * HD)
                    o = A[r, 3, b * TS:(b + 1) * TS]
                    pe.matmul(o, vc[:, b % CACHE_SLOTS, r], ptc[:, b % 2, r], start=(b == 0), stop=False,
                              skip_group_check=True)
                    mm = pe.matmul(o, v_tok[0:TS, 5, r], ptn[:, b % 2, r], start=False, stop=(b == DEC_B - 1),
                                   skip_group_check=True)
                mm.then_inc(s_cpv, 1)

            for b in range(DEC_B + 1):
                if b:
                    ret_out_piece(next(ret_pieces))
                if b < DEC_B:
                    cache_turn(b)
                    ret_out_piece(next(ret_pieces))
                    cache_logits(b)
                if b:
                    cache_probs(b - 1)
                if third_piece(b):
                    ret_out_piece(next(ret_pieces))
                if b:
                    cache_weigh(b - 1)
            for p in ret_pieces:
                ret_out_piece(p)

            def column_sums(x, bank=0):
                for n in range(2):
                    mm = pe.matmul(A[:, bank + n, 0:NT], ones[:, :], x[:, n * NT:(n + 1) * NT], start=True, stop=True)
                return mm

            pe.wait_ge(s_oml, 1)
            for q in range(SLOTS):
                out_piece(B_OUT + KT // 2, q, U_OUT2, 1)
                if q == 0:
                    pe.wait_ge(s_ones, 3)
                    column_sums(yb[:, 0, :]).then_inc(s_shp, 1)
            with pe.Fori(1, KT // 2) as i:
                for q in range(SLOTS):
                    out_piece(i + (B_OUT + KT // 2), q, i + U_OUT2, 1)

            pe.wait_ge(s_shift, 1)
            pe.wait_ge(s_acc, KT + 1)
            column_sums(acc_s).then_inc(s_mu, 1)
            pe.wait_ge(s_accq, KT)
            column_sums(acc_q, 2).then_inc(s_var, 1)

            def gate_up(b0, u0, m0=0):
                with pe.Fori(m0, KP) as m:
                    tile(m * 2 + b0, 0, m + u0, hh, hl)
                    tile(m * 2 + (b0 + 1), 1, m + u0, hh, hl)

            def downs(b0, u0, gs, fl_count):
                wait_apart(pe, s_fl, fl_count)
                with pe.Fori(0, DN) as r:
                    down(r + b0, gs, r * 2 + u0)

            for p in range(2 * SLOTS):
                pe.wait_ge(s_lo, B_FFN * 4 + (p + 5))
                if p < 2:
                    pe.wait_ge(g_free[p], U_FFN)
                pe.wait_ge(s_hl, KP * (p // 2) + KP)
                for k in range(KP):
                    kk = KP * (p // 2) + k
                    for w, x, one in ((wh, hh, kk == 0), (wh, hl, False), (wl, hh, False)):
                        for n in range(2):
                            mm = pe.matmul(G[:, p % 2, n, 0:NT], w[:, p % SLOTS, k, :], x[:, kk, n * NT:(n + 1) * NT],
                                           start=one, stop=(kk == KT - 1 and w is wl))
                mm.then_inc(s_pe, 1)
            gate_up(B_FFN, U_FFN, 1)
            with pe.Fori(0, LOOPS) as i:
                b0 = i * (2 * (GU + DN)) + B_LOOP
                u0 = i * (2 * (KP + KT // 2)) + U_LOOP
                gate_up(b0, u0)
                downs(b0 + GU, u0 + KP, 0, i * 8 + 4)
                gate_up(b0 + GU + DN, u0 + KP + 8)
                downs(b0 + 2 * GU + DN, u0 + 2 * KP + 8, 1, i * 8 + 8)
            pe.wait_ge(s_fl, KP * GROUPS)

            def turn_out(rb_, tts=range(len(TT))):
                for par in range(2):
                    pe.wait_ge(g_free[par], U_LAST + 2 * rb_ + 2)
                for tt in tts:
                    t0, n = TT[tt]
                    e = rb_ * 5 + tt
                    if e >= 4:
                        pe.wait_ge(s_ote, e - 3)
                    for q in range(4):
                        tr = pe.transpose(A[0:n, e % 4, q * P:(q + 1) * P], yb[:, rb_ * 4 + q, t0:t0 + n], ident[:, :])
                    tr.then_inc(s_otr, 1)

            for rb_ in range(DN):
                down(B_LAST + rb_, 0, U_LAST + 2 * rb_, 
                     then=[lambda tts=tts: turn_out(rb_ - 1, tts) for tts in ((), (0, 1), (2, 3), (4,))] if rb_ else None)
            turn_out(DN - 1)

        @block.scalar
        def _(act):
            c = Count(act, act_c)

            def hi(b, q, free=True):
                act.wait_ge(raw_in[q], b * 16 + 16)
                if free:
                    act.wait_ge(s_pe, b * 4 + (q - 3))
                act.copy(wh[:, q], raw[:, q]).then_inc(s_hi, 1)

            def his(b, qs_):
                for q in qs_:
                    hi(b, q)

            for i in range(4):
                act.dma_start(xin[:, i, :], I["x_prompt"][0, i * P:(i + 1) * P, :]).then_inc(x_in[i], 16)
            act.dma_start(xin[0:TS, 4, :], I["x_sample"].rearrange("b t d -> (b t) d")).then_inc(x_in[4], 16)
            act.dma_start(xin[TS:TS + N_META, 4, :], I["meta_tokens"]).then_inc(x_in[4], 16)
            for i, n in enumerate(IN_TILES):
                act.wait_ge(s_ve0, i + 1)
                act.activation(small[0:n, in_col(3, i)], small[0:n, in_col(2, i)], ACT.Sqrt).then_inc(s_sd0, 1)
                act.wait_ge(s_xm, i + 1)
                act.activation(xin[0:n, i, :], xin[0:n, i, :], ACT.Identity, bias=small[0:n, in_col(4, i)],
                               scale=small[0:n, in_col(3, i)]).then_inc(s_xn, 1)
            for q in range(SLOTS):
                hi(0, q, free=False)
            act.wait_ge(s_vecT, 1)
            act.copy(vec[:, :, :], A[:, 0, 0:4 * KT].rearrange("p (n k) -> p n k", n=4)).then_inc(s_vec, 1)
            for k in range(KT):
                act.wait_ge(g_free[k % 2], k // 2 + 1)
                act.copy(xh[:, k, :], xf[:, k % XF_SLOTS, :]).then_inc(s_xh, 1)

            def copy_tile(b, par, dst):
                act.wait_ge(s_pe, b * 4 + 4)
                return act.copy(halves(dst), gt(par))

            def tokens_first(h, i):
                t0, n = CHUNKS[i]
                act.wait_ge(s_kvT, h * NCH + (i + 1))
                if i == SMP:
                    act.wait_ge(s_ss, h * DEC_B)
                    act.copy(kd_s[0:n, :], A[0:n, 0, 0:DK])
                    act.copy(vt_s[0:n, :], A[0:n, 0, DK:2 * DK]).then_inc(s_kv, 1)
                    return
                if i >= 2:
                    act.wait_ge(s_stp, h * 5 + (i - 1))
                act.mul(kd[0:n, i % 2, :], A[0:n, 0, 0:DK], hc[0:n, (HC_KD0 if i == 0 else HC_KD):][:, 0:1])
                act.copy(vt[0:n, i % 2, :], A[0:n, 0, DK:2 * DK]).then_inc(s_kv, 1)

            def root(h, i):
                n = CHUNKS[i][1]
                act.wait_ge(s_ve, h * NCH + (i + 1))
                act.activation(small[0:n, SD], small[0:n, VE], ACT.Sqrt).then_inc(s_sd, 1)

            def sample_step(h, i):
                if i == 1:
                    act.wait_ge(s_xsp, h + 1)
                    act.copy(xs[:, :, :], A[:, 2, 0:2 * TS].rearrange("p (e t) -> p e t", e=2)).then_inc(s_xs, 1)
                elif i == 2:
                    root(h, SMP)
                elif i == SAMPLE_STEPS:
                    act.wait_ge(s_gated, h + 1)
                    act.copy(mh[:, bass.ds(h * 2, 2), :], ret_out[:, :, :]).then_inc(s_mh, 1)

            def values_keys_queries(h, last=None):
                for z in range(6):
                    b = h * RET_BLOCKS + z
                    for q in range(SLOTS):
                        if q == 3:
                            if z == 4:
                                act.wait_ge(s_ropev, h * 2 + 1)
                                act.wait_ge(s_ropep, h * 2 + 1)
                            dst = (v_raw, kq_raw, kq_raw)[z // 2][:, z % 2, :]
                            copy_tile(b, z % 2, dst).then_inc(g_free[z % 2], 1)
                        hi(b + 1, q)
                        if last is not None:
                            sample_step(last, 4 * z + q)

            def prompt(h):
                act.wait_ge(s_hc, h * 16 + 16)
                for t in range(8):
                    b = h * RET_BLOCKS + 6 + t // 4
                    hi(b + 1, t % 4)
                    if t % 4 == 3:
                        act.wait_ge(s_pe, b * 4 + 4)
                        act.activation(halves(gate[:, t // 4, :]), gt(t // 4), ACT.Silu).then_inc(g_free[t // 4], 1)
                    if 2 <= t:
                        tokens_first(h, t - 2)
                    if 3 <= t:
                        root(h, t - 3)

            values_keys_queries(0)
            prompt(0)
            with act.Fori(0, HEADS - 1) as i:
                values_keys_queries(i + 1, i)
                prompt(i + 1)

            for i in range(SAMPLE_STEPS):
                b = B_SWA + i // 4
                if i in (3, 7):
                    copy_tile(b, b % 2, (z_raw if i == 3 else sv_raw)[:, :]).then_inc(g_free[b % 2], 1)
                hi(b + 1, i % 4)
                sample_step(HEADS - 1, i)
            sample_step(HEADS - 1, SAMPLE_STEPS)
            b = B_SWA + 3
            hi(b + 1, 0)
            hi(b + 1, 1)
            act.wait_ge(s_ev, 2)
            act.copy(v_tok[:, 0:4, :], A[:, 2, :].rearrange("p (n d) -> p n d", n=4))
            act.copy(v_tok[0:16, 4, :], A[0:16, 3, 0:P])
            act.copy(v_tok[0:TS, 5, :], A[0:TS, 3, P:2 * P]).then_inc(s_evd, 1)
            act.wait_ge(s_rot, 1)
            copy_tile(b - 1, 0, z_raw[:, :]).then_inc(g_free[0], 1)
            hi(b + 1, 2)
            act.wait_ge(s_ev, 3)
            act.copy(halves(k2[:, 0, :]), A[:, 0:2, 0:NT]).then_inc(s_evd, 1)
            act.wait_ge(s_ev, 4)
            act.copy(k_tok[:, 0, :], A[:, 2, 0:P])
            act.copy(k_tok[0:TS, 1, :], A[0:TS, 2, P:2 * P]).then_inc(s_evd, 1)
            hi(b + 1, 3)
            act.wait_ge(s_ev, 5)
            act.copy(halves(k2[:, 1, :]), A[:, 0:2, 0:NT]).then_inc(s_evd, 1)

            def exps(j, n):
                w = min(128, TP - 128 * n)
                c0, c1 = (128, 256) if n == 0 else (0, 144 if n == 4 else 256)
                s0 = 40 + 8 * ((j + n) % 2)
                act.wait_ge(s_negm, j * 5 + n + 1)
                for i in range(2):
                    act.activation(lg[0:w, (j + n) % 2, i, c0:c1], lg[0:w, (j + n) % 2, i, c0:c1], ACT.Exp,
                                   bias=small[0:w, s0 + i:s0 + i + 1], accum_out=small[0:w, s0 + 4 + i:s0 + 5 + i])
                act.activation(small[0:w, s0 + 6:s0 + 8], small[0:w, s0 + 2:s0 + 4], ACT.Exp).then_inc(s_exp, 1)

            def keep_probs(j, n):
                w = min(128, TP - 128 * n)
                act.wait_ge(s_tr, j * 5 + n + 1)
                if 0 < n < 4:
                    ins = act.copy(pt[:, :, :, :], A[:, 0, :].rearrange("p (k i q) -> p k i q", k=2, i=2))
                elif n == 0:
                    ins = act.copy(pt[:, 1, :, :], A[:, 0, 2 * P:].rearrange("p (i q) -> p i q", i=2))
                else:
                    v = A[:, 0, :].rearrange("p (k i q) -> p k i q", k=2, i=2)
                    act.copy(pt[:, 0, :, 0:w], v[:, 0, :, 0:w])
                    ins = act.copy(pt[0:16, 1, :, 0:w], v[0:16, 1, :, 0:w])
                ins.then_inc(s_pt, 1)

            def mix_hi(j, n):
                w = min(128, TP - 128 * n)
                act.wait_ge(s_pv, j * 5 + n + 1)
                act.copy(mh[:, 8 + j, 128 * n:128 * n + w], A[:, 1, 0:w]).then_inc(s_smh, 1)

            act.wait_ge(s_st_out, 16 * DEC_B * HEADS)
            for j in range(8):
                b = B_SWA + 3 + j

                def h_(q):
                    hi(b + 2, q)
                if j:
                    mix_hi(j - 1, 3)
                h_(0)
                if j:
                    keep_probs(j - 1, 4)
                    mix_hi(j - 1, 4)
                exps(j, 0)
                if j < 7:
                    copy_tile(b, (j + 1) % 2, z_raw[:, :]).then_inc(g_free[(j + 1) % 2], 1)
                h_(1)
                keep_probs(j, 0)
                exps(j, 1)
                mix_hi(j, 0)
                h_(2)
                exps(j, 2)
                keep_probs(j, 1)
                mix_hi(j, 1)
                exps(j, 3)
                keep_probs(j, 2)
                h_(3)
                mix_hi(j, 2)
                keep_probs(j, 3)
                exps(j, 4)

            def cache_exp(b):
                s0 = 60 + 8 * (b % 2)
                act.wait_ge(s_cneg, b + 1)
                act.activation(ls[:, b % 2, :], ls[:, b % 2, :], ACT.Exp, bias=small[:, s0:s0 + 1],
                               accum_out=small[:, s0 + 2:s0 + 3])
                act.activation(small[:, s0 + 3:s0 + 4], small[:, s0 + 1:s0 + 2], ACT.Exp).then_inc(s_cexp, 1)

            ret_pieces = iter(range(8, 4 * (KT // 2)))

            def ret_hi(p):
                hi(B_OUT + 1 + p // 4, p % 4)

            ret_hi(next(ret_pieces))
            mix_hi(7, 3)
            keep_probs(7, 4)
            ret_hi(next(ret_pieces))
            mix_hi(7, 4)
            for b in range(DEC_B + 1):
                if b:
                    ret_hi(next(ret_pieces))
                if b < DEC_B:
                    act.wait_ge(s_kT, b + 1)
                    if b == 0:
                        act.wait_ge(s_sml, 40)
                    act.copy(kct[:, b % 2, :], A[:, 0, 0:P]).then_inc(s_kTe, 1)
                    ret_hi(next(ret_pieces))
                if b:
                    act.wait_ge(s_ctr, b)
                    act.copy(ptc[:, (b - 1) % 2, :], A[:, 2, 0:P])
                    act.copy(ptn[:, (b - 1) % 2, :], A[0:TS, 2, P:2 * P]).then_inc(s_cpt, 1)
                if b < DEC_B:
                    cache_exp(b)
                if third_piece(b):
                    ret_hi(next(ret_pieces))
            act.wait_ge(s_cpv, DEC_B)
            act.copy(os_[:, :, :].rearrange("p r (b t) -> p b r t", b=DEC_B),
                     A[:, 3, :].rearrange("p (b r t) -> p b r t", b=DEC_B, r=8)).then_inc(s_os, 1)
            for p in ret_pieces:
                ret_hi(p)
            act.wait_ge(s_osm, 64)
            act.copy(mh[:, 8:16, TP:T], osm[:, :, :]).then_inc(s_omh, 1)

            def square(r, par, done):
                act.wait_ge(g_free[par], done)
                if not isinstance(r, int) or r >= 2:
                    act.wait_ge(s_accq, r - 1)
                act.activation(ln_t[:, par, :], yb[:, r, :] if isinstance(r, int) else
                               yb[:, bass.ds(r, 1), :].rearrange("p o t -> p (o t)"), ACT.Square).then_inc(s_sq, 1)

            b = B_OUT + KT // 2
            his(b + 1, range(3))
            square(0, 0, U_OUT2 + 1)
            hi(b + 1, 3)
            with act.Fori(1, KT // 2) as i:
                hi(i + (b + 1), 0)
                square(i * 2 - 1, 1, i + U_OUT2)
                hi(i + (b + 1), 1)
                hi(i + (b + 1), 2)
                square(i * 2, 0, i + (U_OUT2 + 1))
                hi(i + (b + 1), 3)
            square(KT - 1, 1, U_FFN)

            def first_hi(p):
                hi(B_FFN + 1 + p // 4, p % 4)

            act.wait_ge(s_mean, 1)
            act.activation(msq[:, :], mean[:, :], ACT.Square).then_inc(s_msq, 1)
            act.wait_ge(s_vs, 1)
            act.activation(rstd[:, :], rstd[:, :], ACT.Sqrt).then_inc(s_sdl, 1)
            for r in range(KT):
                act.wait_ge(s_nrm, r + 1)
                c.link(act.activation(yb[:, r, :], ln_t[:, r % 2, :], ACT.Identity,
                                      bias=vec[:, 3, r:r + 1], scale=vec[:, 2, r:r + 1]))
                act.copy(hh[:, r, :], yb[:, r, :]).then_inc(s_hh, 1)
                if r in LN_PIECES:
                    first_hi(LN_PIECES.index(r))
            for p in range(len(LN_PIECES), 7):
                first_hi(p)

            def gate_up(b0, gs, u0, m0=0):
                with act.Fori(m0, KP) as m:
                    b = m * 2 + b0
                    his(b + 1, range(3))
                    act.wait_ge(s_pe, b * 4 + 4)
                    act.activation(halves(sg[:, :]), gt(0), ACT.Silu).then_inc(g_free[0], 1)
                    hi(b + 1, 3)
                    his(b + 2, range(3))
                    act.wait_ge(g_free[1], m + (u0 + 1))
                    act.copy(fh[:, gs, bass.ds(m, 1), :], fu[:, :].rearrange("p (o t) -> p o t", o=1)).then_inc(s_fh, 1)
                    hi(b + 2, 3)

            def downs(b0):
                with act.Fori(0, DN) as r:
                    his(r + (b0 + 1), range(4))

            act.wait_ge(s_pe, B_FFN * 4 + 7)
            act.activation(halves(sg[:, :]), gt(0), ACT.Silu).then_inc(g_free[0], 1)
            act.wait_ge(g_free[1], U_FFN + 1)
            act.copy(fh[:, 0, 0, :], fu[:, :]).then_inc(s_fh, 1)
            hi(B_FFN + 2, 3)
            gate_up(B_FFN, 0, U_FFN, 1)
            with act.Fori(0, LOOPS) as i:
                b0 = i * (2 * (GU + DN)) + B_LOOP
                u0 = i * (2 * (KP + KT // 2)) + U_LOOP
                gate_up(b0, 1, u0)
                downs(b0 + GU)
                gate_up(b0 + GU + DN, 0, u0 + KP + 8)
                downs(b0 + 2 * GU + DN)

            def out_copy(rb_, tts=range(len(TT))):
                for tt in tts:
                    n = TT[tt][1]
                    e = rb_ * 5 + tt
                    act.wait_ge(s_otr, e + 1)
                    act.copy(yo[0:n, tt, rb_ * 512:(rb_ + 1) * 512], A[0:n, e % 4, :]).then_inc(s_ote, 1)

            for rb_ in range(DN):
                for q, tts in enumerate(((), (0, 1), (2, 3), (4,))):
                    if rb_ < DN - 1:
                        hi(B_LAST + rb_ + 1, q)
                    if rb_:
                        out_copy(rb_ - 1, tts)
            out_copy(DN - 1)
            for tt, (t0, n) in enumerate(TT):
                act.wait_ge(s_vo, tt + 1)
                act.activation(small[0:n, 80 + tt:81 + tt], small[0:n, 90 + tt:91 + tt], ACT.Sqrt).then_inc(s_so, 1)

        @block.vector
        def _(dve):
            c = Count(dve, dve_c)

            def lo(b, q):
                dve.wait_ge(s_hi, b * 4 + (q + 1))
                dve.tensor_tensor(wl[:, q], raw[:, q], f32(wh[:, q]), ALU.subtract).then_inc(s_lo, 1)

            def los(b, qs_):
                for q in qs_:
                    lo(b, q)

            dve.memset(small[:, 159:160], 0.0).then_inc(s_lo, 4)

            def in_scale(i):
                n = IN_TILES[i]
                dve.wait_ge(s_sd0, i + 1)
                c.link(dve.reciprocal(small[0:n, in_col(3, i)], small[0:n, in_col(3, i)]))
                dve.scalar_tensor_tensor(out=small[0:n, in_col(4, i)], in0=small[0:n, in_col(0, i)], scalar=-1.0,
                                         in1=small[0:n, in_col(3, i)], op0=ALU.mult, op1=ALU.mult).then_inc(s_xm, 1)

            for i, n in enumerate(IN_TILES):
                dve.wait_ge(x_in[i], 32 if i == 4 else 16)
                for k in range(4):
                    ins = dve.bn_stats(small[0:n, 6 * k:6 * k + 6], xin[0:n, i, 512 * k:512 * (k + 1)])
                    if k == 0 and i:
                        in_scale(i - 1)
                c.link(ins)
                c.link(dve.bn_aggr(small[0:n, in_col(0, i, 2)], small[0:n, ST6]))
                dve.tensor_scalar(small[0:n, in_col(2, i)], small[0:n, in_col(1, i)], LN_EPS, None, ALU.add).then_inc(s_ve0, 1)
            in_scale(4)
            los(0, range(4))
            dve.wait_ge(s_vec, 1)
            for k in range(KT):
                dve.wait_ge(s_xtr, k + 1)
                if k >= XF_SLOTS:
                    dve.wait_ge(s_xl, k - XF_SLOTS + 1)
                x = xf[:, k % XF_SLOTS, :]
                for dst, src in ((x[:, 16:400], G[:, k % 2, 0, 0:384]), (x[:, 400:T], G[:, k % 2, 1, 0:192]),
                                 (x[:, 0:16], G[:, k % 2, 1, 192:208])):
                    ins = dve.tensor_scalar(dst, src, vec[:, 0, k:k + 1], vec[:, 1, k:k + 1], ALU.mult, ALU.add)
                ins.then_inc(g_free[k % 2], 1)

            def rope(x, out, count):
                for par in range(2):
                    dve.wait_ge(g_free[par], count)
                dve.tensor_tensor(rope_v[:, 0, :], x[:, 0, :], ret_rot[:, 0, :], ALU.mult)
                c.link(dve.tensor_tensor(rope_v[:, 1, :], x[:, 1, :], ret_rot[:, 1, :], ALU.mult))
                dve.tensor_tensor(out[:, 0, :], rope_v[:, 0, :], rope_v[:, 1, :], ALU.subtract).then_inc(s_ropev, 1)

            def masked(h, i):
                n = CHUNKS[i][1]
                dve.wait_ge(s_sc, h * NCH + (i + 1))
                if i == SMP:
                    dve.wait_ge(s_hcs, h * 16 + 16)
                    dve.tensor_tensor(st_s[:, :], A[0:n, 1, 0:n], hcs[0:n, 0:n], ALU.mult).then_inc(s_mask, 1)
                    return
                if i >= 2:
                    dve.wait_ge(s_out, h * NCH + (i - 1))
                dve.tensor_tensor(st[0:n, i % 2, 0:n], A[0:n, 1, 0:n], hc[0:n, 0:n], ALU.mult).then_inc(s_mask, 1)

            def norm(h, i):
                n = CHUNKS[i][1]
                src = A[0:n, 1 if i == SMP else 2, 0:DK]
                dve.wait_ge(s_out, h * NCH + (i + 1))
                c.link(dve.bn_stats(small[0:n, 0:6], src), met=s_vec)
                c.link(dve.bn_aggr(small[0:n, MV], small[0:n, 0:6]))
                eps = hcs[0:n, HS_EPS:HS_EPS + 1] if i == SMP else hc[0:n, HC_EPS:HC_EPS + 1]
                dve.tensor_tensor(small[0:n, VE], small[0:n, 25:26], eps, ALU.add).then_inc(s_ve, 1)
                dve.wait_ge(s_sd, h * NCH + (i + 1))
                c.link(dve.reciprocal(small[0:n, RS], small[0:n, SD]))
                if i:
                    dve.wait_ge(s_yT, h * NCH + i)
                dve.tensor_scalar(yn[0:n, :], src, small[0:n, 24:25], small[0:n, RS],
                                  ALU.subtract, ALU.mult).then_inc(s_y, 1)

            def new_state(h, i):
                dve.wait_ge(s_stp, h * 5 + (i + 1))
                sv = A[:, 3, :].rearrange("p (k e) -> p k e", k=2)
                if i == 0:
                    dve.tensor_copy(state[:, :, :], sv).then_inc(s_state, 1)
                else:
                    dve.scalar_tensor_tensor(out=state[:, :, :], in0=state[:, :, :], scalar=hc[:, HC_G:HC_G + 1],
                                             in1=sv, op0=ALU.mult, op1=ALU.add).then_inc(s_state, 1)

            def turned(h, i, bank=1):
                t0, n = CHUNKS[i]
                dve.wait_ge(s_yT, h * NCH + (i + 1))
                dve.tensor_copy(ret_out[:, :, t0:t0 + n],
                                A[:, bank, 0:DK].rearrange("p (e t) -> p e t", e=2)[:, :, 0:n]).then_inc(s_yTe, 1)

            def own_keys(h, b):
                if b == 0:
                    dve.wait_ge(s_kv, h * NCH + NCH)
                dve.tensor_scalar(kb[0:TS, b % 2, :], kd_s[0:TS, :], hcs[0:TS, HS_KB + b:HS_KB + b + 1], None,
                                  ALU.mult).then_inc(s_kb, 1)

            def sample_state(h, b):
                bank = (3, 0)[b % 2]
                dve.wait_ge(s_sbp, h * DEC_B + (b + 1))
                dve.scalar_tensor_tensor(out=states[:, b], in0=states[:, b], scalar=hcs[:, HS_G:HS_G + 1],
                                         in1=A[:, bank, :].rearrange("p (k e) -> p k e", k=2),
                                         op0=ALU.mult, op1=ALU.add).then_inc(s_ss, 1)

            def sample_step(h, i):
                if i == 0:
                    turned(h, 4)
                    own_keys(h, 0)
                    own_keys(h, 1)
                elif i == 2:
                    norm(h, SMP)
                elif 3 <= i < 3 + DEC_B:
                    sample_state(h, i - 3)
                    if i - 1 < DEC_B:
                        own_keys(h, i - 1)
                elif i == 3 + DEC_B:
                    turned(h, SMP, bank=2)
                    dve.wait_ge(s_yTe, h * NCH + NCH)
                    for par in range(2):
                        dve.wait_ge(g_free[par], h * 4 + (U_IN + 4))
                    dve.tensor_tensor(ret_out[:, :, :], ret_out[:, :, :], gate[:, :, :], ALU.mult).then_inc(s_gated, 1)
                elif i == SAMPLE_STEPS:
                    dve.wait_ge(s_mh, h + 1)
                    dve.tensor_tensor(ml[:, bass.ds(h * 2, 2), :], ret_out[:, :, :], f32(mh[:, bass.ds(h * 2, 2), :]),
                                      ALU.subtract).then_inc(s_ret, 1)

            def values_keys_queries(h, last=None):
                for z in range(6):
                    b = h * RET_BLOCKS + z
                    for q in range(SLOTS):
                        lo(b + 1, q)
                        if last is not None:
                            sample_step(last, 4 * z + q)
                    if z in (3, 5):
                        rope(kq_raw, k_rot if z == 3 else q_rot, h * 4 + (U_IN + (2 if z == 3 else 3)))

            def prompt(h):
                dve.wait_ge(s_hc, h * 16 + 16)
                for t in range(8):
                    lo(h * RET_BLOCKS + (7 + t // 4), t % 4)
                    if 2 <= t:
                        masked(h, t - 2)
                    if 3 <= t:
                        norm(h, t - 3)
                        new_state(h, t - 3)
                    if 4 <= t:
                        turned(h, t - 4)

            dve.wait_ge(s_rot_in, 16)
            values_keys_queries(0)
            prompt(0)
            with dve.Fori(0, HEADS - 1) as i, c.loop(i, HEADS - 1, PER_HEAD):
                values_keys_queries(i + 1, i)
                prompt(i + 1)
            for i in range(SAMPLE_STEPS):
                lo(B_SWA + i // 4 + 1, i % 4)
                sample_step(HEADS - 1, i)
            sample_step(HEADS - 1, SAMPLE_STEPS)

            def rotate(count, sem_, val):
                dve.wait_ge(sem_, val)
                c.link(dve.tensor_tensor(halves(z_tmp[:, :]), A[:, 0:2, 0:NT], halves(swa_rot[:, 1, :]), ALU.mult))
                dve.wait_ge(s_zc, count)
                dve.tensor_tensor(z_rot[:, :], z_rot[:, :], z_tmp[:, :], ALU.add).then_inc(s_rot, 1)

            dve.wait_ge(s_swc, 16 * 4)
            lo(B_SWA + 4, 0)
            rotate(1, s_ev, 1)
            los(B_SWA + 4, range(1, 4))

            def soft_a(j, n):
                w = min(128, TP - 128 * n)
                c0, c1 = (128, 256) if n == 0 else (0, 144 if n == 4 else 256)
                s0 = 40 + 8 * ((j + n) % 2)
                l = lg[0:w, (j + n) % 2, :, c0:c1]
                dve.wait_ge(s_l, j * 5 + n + 1)
                dve.scalar_tensor_tensor(out=l, in0=A[0:w, 2:4, c0:c1],
                                         scalar=HD ** -0.5, in1=mask_p[0:w, None, c0:c1].to_broadcast([w, 2, c1 - c0]),
                                         op0=ALU.mult, op1=ALU.add).then_inc(s_lgx, 1)
                dve.wait_ge(s_lgx, j * 5 + n + 1)
                c.link(dve.tensor_reduce(small[0:w, s0:s0 + 2], l, AX_X, ALU.max))
                c.link(dve.tensor_tensor(small[0:w, s0:s0 + 2], small[0:w, s0:s0 + 2], sinks[0:w, 2 * j:2 * j + 2], ALU.max))
                c.link(dve.tensor_tensor(small[0:w, s0 + 2:s0 + 4], sinks[0:w, 2 * j:2 * j + 2], small[0:w, s0:s0 + 2],
                                         ALU.subtract))
                dve.tensor_scalar(small[0:w, s0:s0 + 2], small[0:w, s0:s0 + 2], -1.0, None, ALU.mult).then_inc(s_negm, 1)

            def soft_b(j, n):
                w = min(128, TP - 128 * n)
                c0, c1 = (128, 256) if n == 0 else (0, 144 if n == 4 else 256)
                s0 = 40 + 8 * ((j + n) % 2)
                dve.wait_ge(s_exp, j * 5 + n + 1)
                c.link(dve.tensor_tensor(small[0:w, s0 + 4:s0 + 6], small[0:w, s0 + 4:s0 + 6], small[0:w, s0 + 6:s0 + 8], ALU.add))
                c.link(dve.reciprocal(small[0:w, s0 + 4:s0 + 6], small[0:w, s0 + 4:s0 + 6]))
                for i in range(2):
                    ins = dve.tensor_scalar(lg[0:w, (j + n) % 2, i, c0:c1], lg[0:w, (j + n) % 2, i, c0:c1],
                                            small[0:w, s0 + 4 + i:s0 + 5 + i], None, ALU.mult)
                ins.then_inc(s_pn, 1)

            def mix_lo(j, n):
                w = min(128, TP - 128 * n)
                dve.wait_ge(s_smh, j * 5 + n + 1)
                dve.tensor_tensor(ml[:, 8 + j, 128 * n:128 * n + w], A[:, 1, 0:w], f32(mh[:, 8 + j, 128 * n:128 * n + w]),
                                  ALU.subtract).then_inc(s_sml, 1)

            def residual(p):
                if p % 2:
                    r = p // 2
                    dve.wait_ge(s_pe, B_OUT * 4 + (p + 1))
                    c.link(dve.tensor_tensor(yb[:, r, :], f32(xh[:, r, :]), f32(xl[:, r, :]), ALU.add))
                    dve.scalar_tensor_tensor(out=halves(yb[:, r, :]), in0=halves(yb[:, r, :]), scalar=ALPHA, in1=gt(r % 2),
                                             op0=ALU.mult, op1=ALU.add).then_inc(g_free[r % 2], 1)

            def ret_lo(p):
                lo(B_OUT + 1 + p // 4, p % 4)
                residual(p)

            dve.wait_ge(s_st_out, 16 * DEC_B * HEADS)
            for j in range(8):
                def l_(q):
                    if j >= 6:
                        residual(4 * (j - 6) + q)
                if j:
                    dve.wait_ge(s_qs, 32 * j)
                if j:
                    mix_lo(j - 1, 3)
                l_(0)
                rotate(2 + j, s_sw, 1 + j)
                soft_a(j, 0)
                if j:
                    mix_lo(j - 1, 4)
                soft_b(j, 0)
                l_(1)
                soft_a(j, 1)
                soft_b(j, 1)
                mix_lo(j, 0)
                soft_a(j, 2)
                l_(2)
                soft_b(j, 2)
                soft_a(j, 3)
                mix_lo(j, 1)
                soft_b(j, 3)
                soft_a(j, 4)
                l_(3)
                mix_lo(j, 2)
                soft_b(j, 4)

            def cache_soft_a(b):
                s0 = 60 + 8 * (b % 2)
                dve.wait_ge(s_cl, b + 1)
                dve.scalar_tensor_tensor(out=ls[:, b % 2, 0:P], in0=A[:, 1, 0:P], scalar=HD ** -0.5, in1=mask_c[:, :],
                                         op0=ALU.mult, op1=ALU.add)
                dve.scalar_tensor_tensor(out=ls[:, b % 2, P:P + TS], in0=A[:, 1, P:P + TS], scalar=HD ** -0.5,
                                         in1=mask_n[:, b, :], op0=ALU.mult, op1=ALU.add).then_inc(s_clx, 1)
                dve.wait_ge(s_clx, b + 1)
                c.link(dve.tensor_reduce(small[:, s0:s0 + 1], ls[:, b % 2, :], AX_X, ALU.max))
                c.link(dve.tensor_tensor(small[:, s0:s0 + 1], small[:, s0:s0 + 1], sink_s[:, :], ALU.max))
                c.link(dve.tensor_tensor(small[:, s0 + 1:s0 + 2], sink_s[:, :], small[:, s0:s0 + 1], ALU.subtract))
                dve.tensor_scalar(small[:, s0:s0 + 1], small[:, s0:s0 + 1], -1.0, None, ALU.mult).then_inc(s_cneg, 1)

            def cache_soft_b(b):
                s0 = 60 + 8 * (b % 2)
                dve.wait_ge(s_cexp, b + 1)
                c.link(dve.tensor_tensor(small[:, s0 + 2:s0 + 3], small[:, s0 + 2:s0 + 3], small[:, s0 + 3:s0 + 4], ALU.add))
                c.link(dve.reciprocal(small[:, s0 + 2:s0 + 3], small[:, s0 + 2:s0 + 3]))
                dve.tensor_scalar(ls[:, b % 2, :], ls[:, b % 2, :], small[:, s0 + 2:s0 + 3], None, ALU.mult).then_inc(s_cpn, 1)

            ret_pieces = iter(range(8, 4 * (KT // 2)))
            dve.wait_ge(s_lo, (B_OUT + 3) * 4 + 4)
            ret_lo(next(ret_pieces))
            mix_lo(7, 3)
            ret_lo(next(ret_pieces))
            mix_lo(7, 4)
            dve.wait_ge(s_cm, 16 * 3)
            for b in range(DEC_B + 1):
                if b:
                    ret_lo(next(ret_pieces))
                if b < DEC_B:
                    ret_lo(next(ret_pieces))
                    cache_soft_a(b)
                    cache_soft_b(b)
                if third_piece(b):
                    ret_lo(next(ret_pieces))
            for p in ret_pieces:
                ret_lo(p)
            dve.wait_ge(s_omh, 1)
            dve.tensor_tensor(ml[:, 8:16, TP:T], osm[:, :, :], f32(mh[:, 8:16, TP:T]), ALU.subtract).then_inc(s_oml, 1)

            dve.wait_ge(s_oml, 1)
            dve.memset(ones[:, :], 1.0 / D).then_inc(s_ones, 1)
            dve.memset(acc_s[:, :], 0.0).then_inc(s_ones, 1)
            dve.memset(acc_q[:, :], 0.0).then_inc(s_ones, 1)

            def complete(b, q, r):
                dve.wait_ge(s_sub, r + 1)
                dve.wait_ge(s_pe, b * 4 + (q + 1))
                y = yb[:, bass.ds(r, 1), :].rearrange("p o (h t) -> p (o h) t", h=2)
                dve.tensor_tensor(y, y, gt(q // 2), ALU.add).then_inc(g_free[q // 2], 1)

            b = B_OUT + KT // 2
            lo(b + 1, 0)
            dve.wait_ge(s_shp, 1)
            dve.tensor_scalar(halves(shift[:, :]), A[:, 0:2, 0:NT], float(KT), None, ALU.mult).then_inc(s_shift, 1)
            lo(b + 1, 1)
            complete(b, 1, 0)
            lo(b + 1, 2)
            lo(b + 1, 3)
            complete(b, 3, 1)
            with dve.Fori(1, KT // 2) as i:
                for q in range(SLOTS):
                    lo(i + (b + 1), q)
                    if q % 2:
                        complete(i + b, q, i * 2 + q // 2)

            dve.wait_ge(s_mu, 1)
            dve.tensor_copy(halves(mean[:, :]), A[:, 0:2, 0:NT]).then_inc(s_mean, 1)
            dve.wait_ge(s_msq, 1)
            dve.wait_ge(s_var, 1)
            dve.scalar_tensor_tensor(out=halves(rstd[:, :]), in0=A[:, 2:4, 0:NT], scalar=LN_EPS, in1=halves(msq[:, :]),
                                     op0=ALU.add, op1=ALU.subtract).then_inc(s_vs, 1)
            dve.wait_ge(s_sdl, 1)
            c.link(dve.reciprocal(rstd[:, :], rstd[:, :]))

            def first_lo(p):
                lo(B_FFN + 1 + p // 4, p % 4)

            def split_h(r):
                dve.wait_ge(s_hh, r + 1)
                dve.tensor_tensor(hl[:, r, :], yb[:, r, :], f32(hh[:, r, :]), ALU.subtract).then_inc(s_hl, 1)

            for r in range(KT):
                dve.wait_ge(s_cen, r + 1)
                dve.tensor_tensor(ln_t[:, r % 2, :], yb[:, r, :], rstd[:, :], ALU.mult).then_inc(s_nrm, 1)
                if r:
                    split_h(r - 1)
                    if r - 1 in LN_PIECES:
                        first_lo(LN_PIECES.index(r - 1))
            split_h(KT - 1)
            if KT - 1 in LN_PIECES:
                first_lo(LN_PIECES.index(KT - 1))
            for p in range(len(LN_PIECES), 7):
                first_lo(p)

            def gate_up(b0, gs, u0, m0, first=0):
                with dve.Fori(first, KP) as m:
                    b = m * 2 + b0
                    los(b + 1, range(4))
                    los(b + 2, range(3))
                    dve.wait_ge(g_free[0], m + (u0 + 1))
                    dve.wait_ge(s_pe, b * 4 + 8)
                    dve.tensor_tensor(halves(fu[:, :]), gt(1), halves(sg[:, :]), ALU.mult).then_inc(g_free[1], 1)
                    lo(b + 2, 3)
                    dve.wait_ge(s_fh, m + m0 + 1)
                    dve.tensor_tensor(fl[:, gs, bass.ds(m, 1), :], fu[:, :].rearrange("p (o t) -> p o t", o=1),
                                      f32(fh[:, gs, bass.ds(m, 1), :]), ALU.subtract).then_inc(s_fl, 1)

            def add(b, q, r):
                dve.wait_ge(s_pe, b * 4 + (q + 1))
                y = yb[:, r, :].rearrange("p o (h t) -> p (o h) t", h=2)
                return dve.tensor_tensor(y, y, gt(q % 2), ALU.add)

            def downs(b0):
                with dve.Fori(0, DN) as rb_:
                    b = rb_ + b0
                    for q in range(SLOTS):
                        add(b, q, bass.ds(rb_ * 4 + q, 1)).then_inc(g_free[q % 2], 1)
                        lo(b + 1, q)

            dve.wait_ge(s_yba, KT)
            dve.wait_ge(g_free[0], U_FFN + 1)
            dve.wait_ge(s_pe, B_FFN * 4 + 8)
            dve.tensor_tensor(halves(fu[:, :]), gt(1), halves(sg[:, :]), ALU.mult).then_inc(g_free[1], 1)
            lo(B_FFN + 2, 3)
            dve.wait_ge(s_fh, 1)
            dve.tensor_tensor(fl[:, 0, 0, :], fu[:, :], f32(fh[:, 0, 0, :]), ALU.subtract).then_inc(s_fl, 1)
            gate_up(B_FFN, 0, U_FFN, 0, 1)
            with dve.Fori(0, LOOPS) as i:
                b0 = i * (2 * (GU + DN)) + B_LOOP
                u0 = i * (2 * (KP + KT // 2)) + U_LOOP
                gate_up(b0, 1, u0, i * 8 + 4)
                downs(b0 + GU)
                gate_up(b0 + GU + DN, 0, u0 + KP + 8, i * 8 + 8)
                downs(b0 + 2 * GU + DN)

            def out_stats(rb_, tts=range(len(TT))):
                for tt in tts:
                    n = TT[tt][1]
                    dve.wait_ge(s_ote, rb_ * 5 + tt + 1)
                    ins = dve.bn_stats(ostats[0:n, tt, 6 * rb_:6 * rb_ + 6], yo[0:n, tt, rb_ * 512:(rb_ + 1) * 512])
                return ins

            for rb_ in range(DN):
                for q, tts in enumerate(((), (0,), (1, 2), (3, 4))):
                    add(B_LAST + rb_, q, slice(rb_ * 4 + q, rb_ * 4 + q + 1)).then_inc(g_free[q % 2], 1)
                    if rb_ < DN - 1:
                        lo(B_LAST + rb_ + 1, q)
                    if rb_ and tts:
                        out_stats(rb_ - 1, tts)
            c.link(out_stats(DN - 1))
            for tt, (t0, n) in enumerate(TT):
                c.link(dve.bn_aggr(small[0:n, 100 + 2 * tt:102 + 2 * tt], ostats[0:n, tt, :]))
                dve.tensor_scalar(small[0:n, 90 + tt:91 + tt], small[0:n, 101 + 2 * tt:102 + 2 * tt], LN_EPS, None,
                                  ALU.add).then_inc(s_vo, 1)
            dve.wait_ge(s_gb, 32)
            for tt, (t0, n) in enumerate(TT):
                dve.wait_ge(s_so, tt + 1)
                c.link(dve.reciprocal(small[0:n, 80 + tt:81 + tt], small[0:n, 80 + tt:81 + tt]))
                c.link(dve.scalar_tensor_tensor(out=yo[0:n, tt, :], in0=yo[0:n, tt, :], scalar=small[0:n, 100 + 2 * tt:101 + 2 * tt],
                                                in1=g_row[0:n, :], op0=ALU.subtract, op1=ALU.mult))
                dve.scalar_tensor_tensor(out=yo[0:n, tt, :], in0=yo[0:n, tt, :], scalar=small[0:n, 80 + tt:81 + tt],
                                         in1=b_row[0:n, :], op0=ALU.mult, op1=ALU.add).then_inc(s_no, 1)

        @block.gpsimd
        def _(pool):
            c = Count(pool, pool_c)
            pool.dma_start(ident[:, :], I["c_ident"]).then_inc(s_const, 16)
            for n, name in enumerate(("ln_emb_g", "ln_emb_b", "ln_mix_g", "ln_mix_b")):
                src = I[name] if n < 2 else I[name][0]
                pool.dma_start(vec_rows[n * KT:(n + 1) * KT, :], src.rearrange("(k p) -> k p", p=P)).then_inc(s_const, 16)
            for k in range(KT):
                pool.wait_ge(s_xh, k + 1)
                pool.tensor_tensor(xl[:, k, :], xf[:, k % XF_SLOTS, :], f32(xh[:, k, :]), ALU.subtract).then_inc(s_xl, 1)
            pool.wait_ge(s_xl, KT)
            pool.dma_start(ret_rot[:, :, :], I["c_ret_rot"]).then_inc(s_rot_in, 16)

            def rope(x, out, count):
                for par in range(2):
                    pool.wait_ge(g_free[par], count)
                pool.tensor_tensor(rope_p[:, 0, :], x[:, 1, :], ret_rot[:, 0, :], ALU.mult)
                c.link(pool.tensor_tensor(rope_p[:, 1, :], x[:, 0, :], ret_rot[:, 1, :], ALU.mult))
                pool.tensor_tensor(out[:, 1, :], rope_p[:, 0, :], rope_p[:, 1, :], ALU.add).then_inc(s_ropep, 1)

            pool.wait_ge(s_rot_in, 16)
            pool.wait_ge(s_xtr, KT)
            def head_constants(h):
                pool.dma_start(hc[:, :], I["c_head"][bass.ds(h, 1), :, 0:HC_W].rearrange("o p n -> p (o n)")).then_inc(s_hc, 16)

            def sample_inputs(h):
                pool.dma_start(hcs[:, :], I["c_head"][bass.ds(h, 1), :, HC_W:HC_W + HS_W].rearrange(
                    "o p n -> p (o n)")).then_inc(s_hcs, 16)
                for b in range(DEC_B):
                    pool.dma_start(states[:, b], I["state_ret"][0, b, bass.ds(h, 1), :, :].rearrange(
                        "o (k p) e -> p (o k) e", p=P)).then_inc(s_st_in, 16)

            def prompt_state(h):
                wait_apart(pool, s_state, h * 5 + 5)
                pool.dma_start(O["ret_p"][0, 0, bass.ds(h, 1), :, :].rearrange("o (k p) e -> p (o k) e", p=P),
                               state[:, :, :]).then_inc(s_ps_out, 16)
                wait_apart(pool, s_ps_out, h * 16 + 16)

            def sample_states(h):
                for b in range(DEC_B):
                    wait_apart(pool, s_ss, h * DEC_B + (b + 1))
                    pool.dma_start(O["ret_s"][0, b, bass.ds(h, 1), :, :].rearrange("o (k p) e -> p (o k) e", p=P),
                                   states[:, b]).then_inc(s_st_out, 16)

            def ropes(h):
                rope(kq_raw, k_rot, h * 4 + (U_IN + 2))
                rope(kq_raw, q_rot, h * 4 + (U_IN + 3))

            head_constants(0)
            sample_inputs(0)
            ropes(0)
            with pool.Fori(0, HEADS - 1) as i, c.loop(i, HEADS - 1, 2):
                prompt_state(i)
                head_constants(i + 1)
                sample_states(i)
                wait_apart(pool, s_st_out, i * (16 * DEC_B) + 16 * DEC_B)
                sample_inputs(i + 1)
                ropes(i + 1)
            prompt_state(HEADS - 1)

            pool.dma_start(swa_rot[:, :, :], I["c_swa_rot"]).then_inc(s_swc, 16)
            pool.dma_start(perm[:, :, :], I["c_perm"]).then_inc(s_swc, 16)
            pool.dma_start(mask_p[:, :], I["c_mask_p"]).then_inc(s_swc, 16)
            pool.dma_start(sinks[:, :], I["swa_sinks"].to_broadcast([P, 16])).then_inc(s_swc, 16)
            sample_states(HEADS - 1)

            def cosines(count):
                pool.tensor_tensor(z_rot[:, :], z_raw[:, :], swa_rot[:, 0, :], ALU.mult).then_inc(s_zc, 1)

            pool.wait_ge(s_swc, 16 * 4)
            pool.wait_ge(s_ret, HEADS)
            pool.wait_ge(g_free[0], U_IN + B_SWA // 2 + 1)
            cosines(1)

            def kv_outputs(j):
                r = slice(j * DEC_T, (j + 1) * DEC_T)
                for o, new in ((O["k_s"], k_tok[r, 1, :]), (O["v_s"], v_tok[r, 5, :])):
                    pool.dma_start(o[0, j, WINDOW - DEC_T:, :, :].rearrange("t k d -> t (k d)"), new).then_inc(s_kv_out, 16)
                if j == 1:
                    kp = O["k_p"][0, 0].rearrange("t k d -> t (k d)")
                    pool.dma_start(kp, k_tok[:, 0, :]).then_inc(s_kv_out, 16)
                if j == 2:
                    vp = O["v_p"][0, 0].rearrange("t k d -> t (k d)")
                    pool.dma_start(vp[0:112, :], v_tok[16:128, 3, :]).then_inc(s_kv_out, 16)
                    pool.dma_start(vp[112:128, :], v_tok[0:16, 4, :]).then_inc(s_kv_out, 16)
                if j in (3, 4):
                    o, old = (O["k_s"], I["cache_swa_k"]) if j == 3 else (O["v_s"], I["cache_swa_v"])
                    pool.dma_start(o[0, :, 0:WINDOW - DEC_T].rearrange("b t k d -> b (t k d)"),
                                   old[0, :, DEC_T:].rearrange("b t k d -> b (t k d)")).then_inc(s_kv_out, 16)

            def lo(b, q):
                pool.wait_ge(s_hi, b * 4 + (q + 1))
                pool.tensor_tensor(wl[:, q], raw[:, q], f32(wh[:, q]), ALU.subtract).then_inc(s_lo, 1)

            pool.wait_ge(s_lo, (B_SWA + 5) * 4 + 4)
            for j in range(8):
                kv = j // 4
                pool.wait_ge(g_free[j % 2], U_IN + (B_SWA + 2 + j) // 2 + 1)
                if j:
                    pool.wait_ge(s_l, j * 5)
                    pool.wait_ge(s_qs, 32 * j)
                else:
                    pool.wait_ge(s_ev, 5)
                cosines(2 + j)
                lo(B_SWA + 5 + j, 0)
                pool.wait_ge(s_rot, 2 + j)
                for i in range(2):
                    pool.dma_start(qs[kv * HD:(kv + 1) * HD, :, 2 * (j % 4) + i, :],
                                   z_rot[i * HD:(i + 1) * HD, TP:T].rearrange("p (b t) -> p b t", b=DEC_B))\
                        .then_inc(s_qs, 16)
                for q in range(1, SLOTS):
                    lo(B_SWA + 5 + j, q)
                    if q == 1:
                        pool.wait_ge(s_evd, 3)
                        kv_outputs(j)
            def cached(b):
                if b >= CACHE_SLOTS:
                    pool.wait_ge(s_cpv, b - CACHE_SLOTS + 1)
                s = b % CACHE_SLOTS
                pool.dma_start(kc[:, s, :], I["cache_swa_k"][0, b].rearrange("t k d -> t (k d)")).then_inc(c_k[s], 16)
                pool.dma_start(vc[:, s, :], I["cache_swa_v"][0, b].rearrange("t k d -> t (k d)")).then_inc(c_k[s], 16)

            pool.dma_start(mask_c[:, :], I["c_mask_c"]).then_inc(s_cm, 16)
            pool.dma_start(sink_s[:, :], I["swa_sinks"].rearrange("o (h u) -> (o h) u", u=1)[:, None, :].to_broadcast([16, 8, 1]))\
                .then_inc(s_cm, 16)
            for b in range(CACHE_SLOTS):
                cached(b)
            pool.wait_ge(s_sml, 40)
            pool.wait_ge(s_qs, 16 * 16)
            pool.dma_start(mask_n[:, :, :], I["c_mask_n"]).then_inc(s_cm, 16)
            for b in range(CACHE_SLOTS, DEC_B):
                cached(b)
            pool.wait_ge(s_os, 1)
            for kv in range(2):
                for i in range(2):
                    pool.dma_start(osm[i * HD:(i + 1) * HD, kv * 4:kv * 4 + 4, :], os_[kv * HD:(kv + 1) * HD, i:8:2, :])\
                        .then_inc(s_osm, 16)

            pool.wait_ge(s_ones, 3)
            pool.memset(small[:, 158:159], 0.0).then_inc(s_acc, 1)
            acc_o = acc_s[:, :].rearrange("p (o t) -> p o t", o=1)

            def less_shift(r):
                pool.tensor_tensor(yb[:, bass.ds(r, 1), :], yb[:, bass.ds(r, 1), :],
                                   shift[:, :].rearrange("p (o t) -> p o t", o=1), ALU.subtract).then_inc(s_sub, 1)

            def sums(i, par, r, ahead):
                pool.wait_ge(g_free[par], i + (U_OUT2 + 1))
                pool.wait_ge(s_acc, r + 1)
                pool.tensor_tensor(acc_o, acc_o, yb[:, bass.ds(r, 1), :], ALU.add).then_inc(s_acc, 1)
                if ahead:
                    less_shift(r + 2)
                pool.wait_ge(s_sq, r + 1)
                pool.wait_ge(s_acc, r + 2)
                pool.tensor_tensor(acc_q[:, :], acc_q[:, :], ln_t[:, par, :], ALU.add).then_inc(s_accq, 1)

            pool.wait_ge(s_shift, 1)
            less_shift(0)
            less_shift(1)
            with pool.Fori(0, KT // 2 - 1) as i:
                for par in range(2):
                    if par:
                        wait_apart(pool, s_accq, i * 2 + 1)
                    sums(i, par, i * 2 + par, True)
            for par in range(2):
                sums(KT // 2 - 1, par, KT - 2 + par, False)
            pool.wait_ge(s_accq, KT)
            pool.wait_ge(s_mean, 1)
            for r in range(KT):
                pool.tensor_tensor(yb[:, r, :], yb[:, r, :], mean[:, :], ALU.subtract).then_inc(s_cen, 1)
            for r in range(KT):
                pool.wait_ge(s_hl, r + 1)
                pool.tensor_scalar(yb[:, r, :], yb[:, r, :], ALPHA, None, ALU.mult).then_inc(s_yba, 1)

            pool.wait_ge(s_pe, 4 * B_LAST)
            for row, name in ((g_row, "ln_ffn_g"), (b_row, "ln_ffn_b")):
                pool.dma_start(row[:, :], I[name].to_broadcast([P, D])).then_inc(s_gb, 16)
            for tt, (t0, n) in enumerate(TT):
                pool.wait_ge(s_no, tt + 1)
                dst = O["y_s"].rearrange("b t d -> (b t) d") if tt == 4 else O["y_p"][0, t0 - N_META:t0 - N_META + n, :]
                pool.dma_start(dst, yo[0:n, tt, :]).then_inc(s_dout, 16)
            pool.wait_ge(s_dout, 16 * 5)
            pool.wait_ge(s_kv_out, 16 * (3 + 2 * DEC_B + 2))
            pool.wait_ge(s_ps_out, 16 * HEADS)
            pool.wait_ge(s_st_out, 16 * DEC_B * HEADS)


_INS = ["x_prompt", "x_sample", "state_ret", "cache_swa_k", "cache_swa_v", "meta_tokens", "ln_emb_g", "ln_emb_b",
        "w_in", "w_out", "swa_sinks", "ln_mix_g", "ln_mix_b", "w_ffn_gate", "w_ffn_up", "w_ffn_down", "ln_ffn_g", "ln_ffn_b"]
_OUTS = [("y_p", (1, SEQ, D)), ("y_s", (DEC_B, DEC_T, D)), ("ret_p", (1, 1, HEADS, DK, DK)), ("k_p", (1, 1, WINDOW, 2, HD)),
         ("v_p", (1, 1, WINDOW, 2, HD)), ("ret_s", (1, DEC_B, HEADS, DK, DK)), ("k_s", (1, DEC_B, WINDOW, 2, HD)),
         ("v_s", (1, DEC_B, WINDOW, 2, HD))]


def kernel(**inputs):
    import concourse.bacc as bacc
    from concourse.bass_utils import run_bass_kernel_spmd

    nc = bacc.Bacc("TRN2", target_bir_lowering=False, num_devices=1)
    arrays = {n: np.ascontiguousarray(inputs[n]) for n in _INS}
    arrays.update(shape_constants())
    ins = {n: nc.dram_tensor(f"in_{n}", a.shape, F32, kind="ExternalInput").ap() for n, a in arrays.items()}
    outs = {n: nc.dram_tensor(f"out_{n}", s, F32, kind="ExternalOutput").ap() for n, s in _OUTS}
    hymba_step_kernel(nc, ins, outs)
    r = run_bass_kernel_spmd(nc, [{f"in_{n}": a for n, a in arrays.items()}], core_ids=[0])
    return tuple(r.results[0][f"out_{n}"] for n, _ in _OUTS)
```

```python
from contextlib import ExitStack, contextmanager

import numpy as np

import concourse.bass as bass
from concourse import mybir

F32 = mybir.dt.float32
F32R = mybir.dt.float32r
ALU = mybir.AluOpType
ACT = mybir.ActivationFunctionType
AX_X = mybir.AxisListType.X

P = 128
D = 2048
SEQ, N_META = 512, 16
DEC_B, DEC_T = 8, 8
PAST = 4096
HEADS, DK = 4, 256
HD, WINDOW, ROT = 64, 128, 16
FFN = 5632
LN_EPS = 1e-5
ALPHA = 2.0 ** 0.25

TP = N_META + SEQ
TS = DEC_B * DEC_T
T = TP + TS
NT = T // 2
M0 = N_META
TL = T - M0
NL = TL // 2
KT = D // P
KP = 4
SLOTS = 4
HT = FFN // P
GROUPS = HT // KP
Q_COL, K_COL, V_COL, G_COL = 0, 1024, 2048, 3072
SQ_COL, SK_COL, SV_COL = 4096, 5120, 5248
RET_BLOCKS = 8
CHUNKS = [(0, N_META)] + [(N_META + 128 * c, 128) for c in range(4)] + [(TP, TS)]
NCH = len(CHUNKS)
IN_TILES = [128, 128, 128, 128, TS + N_META]
XF_SLOTS = 4
SMP = NCH - 1
NO = NCH - 1
HC_KD, HC_KD0, HC_EPS, HC_G, HC_W = 128, 129, 130, 131, 132
HS_EPS, HS_G, HS_KB = TS, TS + 1, TS + 2
HS_W = HS_KB + DEC_B

PER_HEAD = 2 + 3 * NO
SAMPLE_STEPS = 12
IN_PIECES = (10, 14)
LN_PIECES = (8, 10, 12, 14)
POOL_COLS = 1344
CACHE_SLOTS = 3


def shape_constants():
    f = np.float32
    pos = np.concatenate([np.arange(TP), np.tile(PAST + np.arange(DEC_T), DEC_B)]).astype(f)
    rf = np.power(f(10000.0), -np.linspace(0.0, 1.0, DK // 2, dtype=f)).astype(f)
    ang = (pos[None, :] * rf[:, None]).astype(f).astype(np.float64)
    ret_rot = np.stack([np.cos(ang), np.sin(ang)], 1).astype(f)
    half = ROT // 2
    sf = np.power(f(500000.0), -np.arange(0, ROT, 2, dtype=f) / f(ROT)).astype(f)
    sang = (pos[None, :] * sf[:, None]).astype(f).astype(np.float64)
    swa_rot = np.zeros((P, 2, T), f)
    swa_rot[:, 0] = 1.0
    swap = np.zeros((P, P), f)
    for b in (0, HD):
        for i in range(half):
            swa_rot[b + i, 0] = swa_rot[b + half + i, 0] = np.cos(sang[i])
            swa_rot[b + i, 1] = -np.sin(sang[i])
            swa_rot[b + half + i, 1] = np.sin(sang[i])
            swap[b + half + i, b + i] = swap[b + i, b + half + i] = 1.0
    perm = np.zeros((P, 3, P), f)
    perm[:, 0] = swap
    for kv in range(2):
        for i in range(HD):
            perm[kv * HD + i, 1 + kv, i] = perm[kv * HD + i, 1 + kv, HD + i] = 1.0
    gam = 1.0 - 2.0 ** (-5.0 - np.arange(HEADS, dtype=np.float64))
    hc = np.zeros((HEADS, P, HC_W + HS_W), np.float64)
    j = np.arange(P)[:, None]
    i = np.arange(P)[None, :]
    t = np.arange(P) % DEC_T
    bb = np.arange(P) // DEC_T
    for h in range(HEADS):
        g = gam[h]
        hc[h, :, 0:128] = (i >= j) * g ** -(j + 1.0) / 16.0
        ok = (bb[:, None] == bb[None, :64]) & (t[None, :64] >= t[:, None]) & (np.arange(P)[:, None] < TS)
        hc[h, :, HC_W:HC_W + TS] = ok * (g ** -(t + 1.0))[:, None] / 16.0
        hc[h, :, HC_KD] = g ** (127.0 - np.arange(P)) / 16.0
        hc[h, :N_META, HC_KD0] = g ** (N_META - 1.0 - np.arange(N_META)) / 16.0
        hc[h, :, HC_EPS] = LN_EPS * g ** (-2.0 * (np.arange(P) + 1.0))
        hc[h, :, HC_W + HS_EPS] = LN_EPS * g ** (-2.0 * (t + 1.0))
        hc[h, :, HC_G] = g ** 128
        hc[h, :, HC_W + HS_G] = g ** DEC_T
        for b in range(DEC_B):
            hc[h, :, HC_W + HS_KB + b] = (bb == b) * g ** (DEC_T - 1.0 - t) / 16.0
    neg = f(-1e30)
    q = np.arange(P)[:, None]
    kk = np.arange(2 * P)[None, :]
    diff = q + P - kk
    mask_p = np.where((diff >= 0) & (diff < WINDOW), f(0), neg).astype(f)
    tq = (np.arange(P) % DEC_T)[:, None]
    pc = np.arange(P)[None, :]
    mask_c = np.where(tq + P - pc < WINDOW, f(0), neg).astype(f)
    mask_n = np.full((P, DEC_B, TS), neg, f)
    for b in range(DEC_B):
        for u in range(DEC_T):
            mask_n[:, b, b * DEC_T + u] = np.where(tq[:, 0] >= u, f(0), neg)
    return {
        "c_ret_rot": ret_rot, "c_swa_rot": swa_rot, "c_perm": perm, "c_head": hc.astype(f),
        "c_mask_p": mask_p, "c_mask_c": mask_c, "c_mask_n": mask_n, "c_ident": np.eye(P, dtype=f),
    }


class Count:

    def __init__(self, eng, sem):
        self.eng, self.sem, self.base, self.n = eng, sem, 0, 0

    def link(self, ins, met=None):
        self.n += 1
        ins.then_inc(self.sem, 1)
        value = self.base + self.n
        if met is not None and not isinstance(value, int):
            value = self.eng.to_reg(value)
            self.eng.wait_ge(met, 1)
        self.eng.wait_ge(self.sem, value)

    @contextmanager
    def loop(self, i, times, per):
        base, n = self.base, self.n
        self.base, self.n = i * per + (base + n), 0
        yield
        assert self.n == per, f"{self.n} links in a loop of {per}"
        self.base, self.n = base, n + times * per


def hymba_step_kernel(nc, I, O):
    with ExitStack() as ctx:
        RB = KT * T * 4
        R0, R1, R2, R3, R4 = (n * RB for n in range(5))
        END = 212800
        base = -(-nc.sbuf_base // 32) * 32
        slab = ctx.enter_context(nc.sbuf_tensor("slab", [P, END // 4], F32))

        def at(name, shape, off, dt=F32):
            return nc.alloc_sbuf_tensor_at(name, shape, dt, offset=base + off)

        class Area:

            def __init__(self, off, end):
                self.off, self.end = off, end

            def __call__(self, name, shape, dt=F32):
                a = at(name, shape, self.off, dt)
                self.off += (4 * int(np.prod(shape[1:])) + 31) // 32 * 32
                assert self.off <= self.end, (name, self.off, self.end)
                return a

        xh, xl = at("xh", [P, KT, T], R0, F32R), at("xl", [P, KT, T], R1, F32R)
        mh, ml = at("mh", [P, KT, T], R2, F32R), at("ml", [P, KT, T], R3, F32R)
        yb = at("yb", [P, KT, T], R1)[:, :, M0:T]
        hh, hl = at("hh", [P, KT, TL], R2, F32R), at("hl", [P, KT, TL], R3, F32R)
        fh, fl = at("fh", [P, 2, KP, TL], R0, F32R), at("fl", [P, 2, KP, TL], R0 + RB // 2, F32R)
        g_row, b_row = at("g_row", [P, D], R0 + RB // 4), at("b_row", [P, D], R0 + 3 * RB // 4)
        xin = at("xin", [P, len(IN_TILES), D], R2)
        yo = at("yo", [P, 5, D], R2)

        PIECE = KP * P * 4
        raw = at("raw", [P, SLOTS, KP, P], R4)
        wh = at("wh", [P, SLOTS, KP, P], R4 + SLOTS * PIECE, F32R)
        wl = at("wl", [P, SLOTS, KP, P], R4 + 2 * SLOTS * PIECE, F32R)

        keep = Area(R4 + 3 * SLOTS * PIECE, END)
        ident = keep("ident", [P, P])
        vec = keep("vec", [P, 4, KT])
        small = keep("small", [P, 160])
        R5 = keep.off
        ia = Area(R5, END)
        xf = ia("xf", [P, XF_SLOTS, T])
        vec_rows = ia("vec_rows", [4 * KT, P])
        ra = Area(R5, END)
        ret_rot = ra("ret_rot", [P, 2, T])
        v_raw = ra("v_raw", [P, 2, T])
        kq_raw = ra("kq_raw", [P, 2, T])
        k_rot = ra("k_rot", [P, 2, T])
        q_rot = ra("q_rot", [P, 2, T])
        rope_v = ra("rope_v", [P, 2, T])
        hc = ra("hc", [P, HC_W])
        state = ra("state", [P, 2, DK])
        rb = Area(R2 + RB // 2, R3)
        gate = rb("gate", [P, 2, T])
        ret_out = rb("ret_out", [P, 2, T])
        rope_p = rb("rope_p", [P, 2, T])
        kd = rb("kd", [P, 2, DK])
        vt = rb("vt", [P, 2, DK])
        hcs = rb("hcs", [P, HS_W])
        st_s = rb("st_s", [TS, TS])
        rd = Area(R2 + 6 * T * 4, R2 + RB // 2)
        kb = rd("kb", [P, 2, DK])
        kd_s = rd("kd_s", [P, DK])
        vt_s = rd("vt_s", [P, DK])
        rc = Area(R3 + RB // 2, R4)
        states = rc("states", [P, DEC_B, 2, DK])
        st = rc("st", [P, 2, P])
        yn = rc("yn", [P, DK])
        xs = rc("xs", [P, 2, TS])
        sa = Area(R5, END)
        swa_rot = sa("swa_rot", [P, 2, T])
        perm = sa("perm", [P, 3, P])
        mask_p = sa("mask_p", [P, 2 * P])
        k2 = sa("k2", [P, 2, T])
        v_tok = sa("v_tok", [P, 6, P])
        k_tok = sa("k_tok", [P, 2, P])
        sinks = sa("sinks", [P, 16])
        sink_s = sa("sink_s", [P, 1])
        qs = sa("qs", [P, DEC_B, 8, DEC_T])
        SX = sa.off
        z_raw = sa("z_raw", [P, T])
        z_tmp = sa("z_tmp", [P, T])
        z_rot = sa("z_rot", [P, T])
        sv_raw = at("sv_raw", [P, T], sa.off)
        lg = sa("lg", [P, 2, 2, 2 * P])
        pt = sa("pt", [P, 2, 2, P])
        mask_c = sa("mask_c", [P, P])
        kc = sa("kc", [P, CACHE_SLOTS, P])
        vc = sa("vc", [P, CACHE_SLOTS, P])
        sp = Area(SX, END)
        mask_n = sp("mask_n", [P, DEC_B, TS])
        kct = sp("kct", [P, 2, P])
        ls = sp("ls", [P, 2, 3 * HD])
        ptc = sp("ptc", [P, 2, P])
        ptn = sp("ptn", [TS, 2, P])
        os_ = sp("os_", [P, 8, TS])
        osm = sp("osm", [P, 8, TS])
        ta = Area(R5, END)
        ln_t = ta("ln_t", [P, 2, TL])
        ones = ta("ones", [P, P])
        shift = ta("shift", [P, TL])
        msq = ta("msq", [P, TL])
        acc_s = ta("acc_s", [P, TL])
        acc_q = ta("acc_q", [P, TL])
        mean = ta("mean", [P, TL])
        rstd = ta("rstd", [P, TL])
        ostats = ta("ostats", [P, 5, 24])
        sg = ta("sg", [P, TL])
        fu = ta("fu", [P, TL])

        G = ctx.enter_context(nc.psum_tensor("G", [P, 2, 2, 512], F32))
        A = ctx.enter_context(nc.psum_tensor("A", [P, 4, 512], F32))

        def gt(par):
            return G[:, par, :, 0:NT]

        def gl(par):
            return G[:, par, :, 0:NL]

        def halves(ap):
            return ap.rearrange("p (h t) -> p h t", h=2)

        def f32(ap):
            return ap.bitcast(F32)

        def sem(name):
            return ctx.enter_context(nc.semaphore(name))

        def in_col(what, i, n=1):
            return slice(100 + 5 * i + what, 100 + 5 * i + what + n)

        ST6, MV, VE, SD, RS = slice(0, 24), slice(24, 26), slice(26, 27), slice(27, 28), slice(28, 29)

        raw_in = [sem(f"raw_in{i}") for i in range(SLOTS)]
        g_free = [sem(f"g_free{i}") for i in range(2)]
        x_in = [sem(f"x_in{i}") for i in range(len(IN_TILES))]
        c_k = [sem(f"c_k{i}") for i in range(CACHE_SLOTS)]
        piece_hi = sem("piece_hi")
        piece_lo = sem("piece_lo")
        piece_used = sem("piece_used")
        dve_chain = sem("dve_chain")                    
        act_chain = sem("act_chain")                    
        pool_chain = sem("pool_chain")                  
        const_in = sem("const_in")
        vec_turned = sem("vec_turned")
        vec_ready = sem("vec_ready")
        in_var = sem("in_var")
        in_dev = sem("in_dev")
        in_scale_ready = sem("in_scale_ready")
        in_normed = sem("in_normed")
        in_turned = sem("in_turned")
        x_hi = sem("x_hi")
        x_lo = sem("x_lo")
        rot_in = sem("rot_in")
        head_in = sem("head_in")
        head_s_in = sem("head_s_in")
        states_in = sem("states_in")
        states_out = sem("states_out")
        state_out = sem("state_out")
        rope_a = sem("rope_a")
        rope_b = sem("rope_b")
        kv_turned = sem("kv_turned")
        kv_ready = sem("kv_ready")
        scores = sem("scores")
        scores_decayed = sem("scores_decayed")
        out_ready = sem("out_ready")
        out_var = sem("out_var")
        out_dev = sem("out_dev")
        out_normed = sem("out_normed")
        state_part = sem("state_part")
        state_new = sem("state_new")
        out_turned = sem("out_turned")
        out_kept = sem("out_kept")
        sample_out_ready = sem("sample_out_ready")
        sample_out_kept = sem("sample_out_kept")
        own_keys_ready = sem("own_keys_ready")
        sample_state_part = sem("sample_state_part")
        sample_state_new = sem("sample_state_new")
        gated = sem("gated")
        gated_hi = sem("gated_hi")
        gated_lo = sem("gated_lo")
        swa_in = sem("swa_in")
        q_swapped = sem("q_swapped")
        cos_part = sem("cos_part")
        rotated = sem("rotated")
        kv_step = sem("kv_step")
        kv_step_kept = sem("kv_step_kept")
        logits_ready = sem("logits_ready")
        logits_masked = sem("logits_masked")
        neg_max = sem("neg_max")
        exp_ready = sem("exp_ready")
        probs = sem("probs")
        probs_turned = sem("probs_turned")
        probs_kept = sem("probs_kept")
        mix_ready = sem("mix_ready")
        mix_hi_done = sem("mix_hi_done")
        mix_lo_done = sem("mix_lo_done")
        sample_q = sem("sample_q")
        cache_consts = sem("cache_consts")
        ck_turned = sem("ck_turned")
        ck_kept = sem("ck_kept")
        c_logits = sem("c_logits")
        c_masked = sem("c_masked")
        c_neg_max = sem("c_neg_max")
        c_exp = sem("c_exp")
        c_probs = sem("c_probs")
        c_turned = sem("c_turned")
        c_kept = sem("c_kept")
        c_mixed = sem("c_mixed")
        os_ready = sem("os_ready")
        osm_ready = sem("osm_ready")
        osm_hi = sem("osm_hi")
        osm_lo = sem("osm_lo")
        kv_out = sem("kv_out")
        ones_ready = sem("ones_ready")
        shift_part = sem("shift_part")
        shift_ready = sem("shift_ready")
        shifted = sem("shifted")
        sum_done = sem("sum_done")
        mean_part = sem("mean_part")
        mean_ready = sem("mean_ready")
        mean_squared = sem("mean_squared")
        squared = sem("squared")
        squares_done = sem("squares_done")
        var_part = sem("var_part")
        var_ready = sem("var_ready")
        dev_ready = sem("dev_ready")
        centred = sem("centred")
        normed = sem("normed")
        h_hi = sem("h_hi")
        h_lo = sem("h_lo")
        alpha_h = sem("alpha_h")
        f_hi = sem("f_hi")
        f_lo = sem("f_lo")
        y_turned = sem("y_turned")
        y_kept = sem("y_kept")
        gain_in = sem("gain_in")
        y_var = sem("y_var")
        y_dev = sem("y_dev")
        y_scale = sem("y_scale")
        y_normed = sem("y_normed")
        y_gained = sem("y_gained")
        y_biased_a = sem("y_biased_a")
        y_biased_b = sem("y_biased_b")
        y_out = sem("y_out")

        B_SWA = RET_BLOCKS * HEADS
        B_OUT = B_SWA + 10
        B_FFN = B_OUT + KT
        GU, DN = 2 * KP, KT // KP
        B_LOOP = B_FFN + GU
        LOOPS = (GROUPS - 1) // 2
        B_LAST = B_LOOP + LOOPS * 2 * (GU + DN)
        U_IN = KT // 2
        U_OUT = U_IN + B_OUT // 2
        U_OUT2 = U_OUT + KT // 2
        U_FFN = U_OUT2 + KT // 2
        U_LOOP = U_FFN + KP
        U_LAST = U_LOOP + LOOPS * 2 * (KP + KT // 2)
        w_in, w_out = I["w_in"][0], I["w_out"][0]
        w_gate, w_up, w_down = I["w_ffn_gate"][0], I["w_ffn_up"][0], I["w_ffn_down"][0]
        TT = [(128 * i, 128) for i in range(4)] + [(SEQ, TS)]

        def ret_cols(h):
            return [V_COL + h * DK, V_COL + 128 + h * DK, K_COL + h * DK, K_COL + 128 + h * DK,
                    Q_COL + h * DK, Q_COL + 128 + h * DK, G_COL + h * DK, G_COL + 128 + h * DK]

        def key_col(n):
            return P - CHUNKS[n][1]

        def third_piece(b):
            return b % 2 == 0 and b < DEC_B

        def wait_apart(eng, s, count, met=vec_ready, n=1):
            if isinstance(count, int):
                eng.wait_ge(s, count)
                return
            count = eng.to_reg(count)
            eng.wait_ge(met, n)
            eng.wait_ge(s, count)

        block = ctx.enter_context(nc.Block())

        @block.sync
        def _(sp_):
            def pieces(b, src, col):
                for q in range(SLOTS):
                    wait_apart(sp_, piece_lo, b * 4 + (q + 1), piece_lo, 4)
                    sp_.dma_start(raw[:, q], src[q * 512:(q + 1) * 512, bass.ds(col, P)].rearrange(
                        "(k p) n -> p k n", p=P)).then_inc(raw_in[q], 16)

            def down(b, g, rb):
                for q in range(SLOTS):
                    sp_.wait_ge(piece_lo, b * 4 + (q + 1))
                    sp_.dma_start(raw[:, q], w_down[bass.ds(g * 512, 512), bass.ds(rb * 512 + q * P, P)].rearrange(
                        "(k p) n -> p k n", p=P)).then_inc(raw_in[q], 16)

            def out_pieces(b, i, half):
                for q in range(SLOTS):
                    wait_apart(sp_, piece_lo, b * 4 + (q + 1), piece_lo, 4)
                    r0 = half * (D // 2) + q % 2 * 512
                    sp_.dma_start(raw[:, q], w_out[r0:r0 + 512, bass.ds(i * 256 + q // 2 * P, P)].rearrange(
                        "(k p) n -> p k n", p=P)).then_inc(raw_in[q], 16)

            def gate_up(b0, g, m0=0):
                with sp_.Fori(m0, KP) as m:
                    pieces(m * 2 + b0, w_gate, g * 512 + m * P)
                    pieces(m * 2 + (b0 + 1), w_up, g * 512 + m * P)

            def downs(b0, g):
                with sp_.Fori(0, DN) as rb_:
                    down(rb_ + b0, g, rb_)

            sp_.wait_ge(x_in[1], 16)
            with sp_.Fori(0, HEADS) as h:
                for z, col in enumerate(ret_cols(h)):
                    pieces(h * RET_BLOCKS + z, w_in, col)
            pieces(B_SWA, w_in, SK_COL)
            pieces(B_SWA + 1, w_in, SV_COL)
            with sp_.Fori(0, 8) as j:
                pieces(j + (B_SWA + 2), w_in, j * P + SQ_COL)
            for half in range(2):
                with sp_.Fori(0, KT // 2) as i:
                    out_pieces(i + (B_OUT + half * (KT // 2)), i, half)
            for p in range(2 * SLOTS):
                sp_.wait_ge(piece_lo, B_FFN * 4 + (p + 1))
                sp_.dma_start(raw[:, p % SLOTS], (w_gate, w_up)[p % 2][p // 2 * 512:(p // 2 + 1) * 512, 0:P].rearrange(
                    "(k p) n -> p k n", p=P)).then_inc(raw_in[p % SLOTS], 16)
            gate_up(B_FFN, 0, 1)
            with sp_.Fori(0, LOOPS) as i:
                b0 = i * (2 * (GU + DN)) + B_LOOP
                gate_up(b0, i * 2 + 1)
                downs(b0 + GU, i * 2)
                gate_up(b0 + GU + DN, i * 2 + 2)
                downs(b0 + 2 * GU + DN, i * 2 + 1)
            downs(B_LAST, GROUPS - 1)

            for tt, (t0, n) in enumerate(TT):
                sp_.wait_ge(y_biased_a, tt + 1)
                sp_.wait_ge(y_biased_b, tt + 1)
                dst = O["y_s"].rearrange("b t d -> (b t) d") if tt == 4 else O["y_p"][0, t0:t0 + n, :]
                sp_.dma_start(dst, yo[0:n, tt, :]).then_inc(y_out, 16)
            sp_.wait_ge(y_out, 16 * len(TT))

        @block.tensor
        def _(pe):
            def piece(b, q, par, use, hi, lo, first=False, ks=(0, KP), t0=0):
                nt = NT if t0 == 0 else NL
                if ks[0] == 0:
                    pe.wait_ge(piece_lo, b * 4 + (q + 5))
                    if q == 0 and not first:
                        pe.wait_ge(g_free[par], use)
                if first:
                    pe.wait_ge(x_lo, KP * q + ks[1])
                for k in range(*ks):
                    kk = KP * q + k
                    for w, x, one in ((wh, hi, kk == 0), (wh, lo, False), (wl, hi, False)):
                        for n in range(2):
                            mm = pe.matmul(G[:, par, n, 0:nt], w[:, q, k, :], x[:, kk, t0 + n * nt:t0 + (n + 1) * nt],
                                           start=one, stop=(kk == KT - 1 and w is wl))
                if ks[1] == KP:
                    mm.then_inc(piece_used, 1)

            def ffn_tile(b, par, use):
                for q in range(SLOTS):
                    pe.wait_ge(piece_lo, b * 4 + (q + 5))
                    if q == 0:
                        pe.wait_ge(g_free[par], use)
                    for k in range(KP):
                        kk = KP * q + k
                        for w, x, one in ((wh, hh, kk == 0), (wh, hl, False), (wl, hh, False)):
                            for n in range(2):
                                mm = pe.matmul(G[:, par, n, 0:NL], w[:, q, k, :], x[:, kk, n * NL:(n + 1) * NL],
                                               start=one, stop=(kk == KT - 1 and w is wl))
                    mm.then_inc(piece_used, 1)

            def down(b, gs, use, qs_=range(SLOTS)):
                for q in qs_:
                    pe.wait_ge(piece_lo, b * 4 + (q + 5))
                    pe.wait_ge(g_free[q % 2], use + q // 2)
                    for k in range(KP):
                        for w, x, one in ((wh, fh, k == 0), (wh, fl, False), (wl, fh, False)):
                            for n in range(2):
                                mm = pe.matmul(G[:, q % 2, n, 0:NL], w[:, q, k, :], x[:, gs, k, n * NL:(n + 1) * NL],
                                               start=one, stop=(k == KP - 1 and w is wl))
                    mm.then_inc(piece_used, 1)

            def out_piece(b, q, use, half, ks=(0, KP)):
                if ks[0] == 0:
                    pe.wait_ge(piece_lo, b * 4 + (q + 5))
                    if q % 2 == 0:
                        pe.wait_ge(g_free[q // 2], use)
                for k in range(*ks):
                    kk = half * (KT // 2) + q % 2 * KP + k
                    for w, x, one in ((wh, mh, q % 2 == 0 and k == 0), (wh, ml, False), (wl, mh, False)):
                        for n in range(2):
                            mm = pe.matmul(G[:, q // 2, n, 0:NL], w[:, q, k, :], x[:, kk, M0 + n * NL:M0 + (n + 1) * NL],
                                           start=one, stop=(q % 2 == 1 and k == KP - 1 and w is wl))
                if ks[1] == KP:
                    mm.then_inc(piece_used, 1)

            pe.wait_ge(const_in, 16 * 5)
            pe.transpose(G[:, 0, 0, 0:4 * KT], vec_rows[:, :], ident[0:4 * KT, 0:4 * KT]).then_inc(vec_turned, 1)

            def first_block(i):
                piece(0, i // 2, 0, 0, xh, xl, first=True, ks=(0, KP // 2) if i % 2 == 0 else (KP // 2, KP))

            for k in range(KT):
                if k >= 2:
                    pe.wait_ge(g_free[k % 2], k // 2)
                for c, n in enumerate(IN_TILES):
                    if k == 0:
                        pe.wait_ge(in_normed, c + 1)
                    bank, col = (k % 2 * 2 + c // 3, c % 3 * 128)
                    tr = pe.transpose(A[:, bank, col:col + n], xin[0:n, c, k * P:(k + 1) * P], ident[0:n, 0:n])
                tr.then_inc(in_turned, 1)
                if k >= 5 and k % 2:
                    first_block((k - 5) // 2)
            first_block(6)
            first_block(7)

            def part_a(h, c):
                t0, n = CHUNKS[c]
                if c == 0:
                    wait_apart(pe, rope_a, h * 2 + 2)
                    wait_apart(pe, rope_b, h * 2 + 2)
                else:
                    wait_apart(pe, kv_ready, h * NCH + c)
                for i, x in enumerate((k_rot, k_rot, v_raw, v_raw)):
                    tr = pe.transpose(A[0:n, 0, i * P:(i + 1) * P], x[:, i % 2, t0:t0 + n], ident[:, :])
                tr.then_inc(kv_turned, 1)
                if c == 0:
                    return
                if c >= 4:
                    wait_apart(pe, out_kept, h * NO + (c - 3))
                if c > 1:
                    wait_apart(pe, scores_decayed, h * NO + (c - 1))
                for k in range(2):
                    mm = pe.matmul(A[0:n, 1, 0:n], k_rot[:, k, t0:t0 + n], q_rot[:, k, t0:t0 + n],
                                   start=(k == 0), stop=(k == 1))
                mm.then_inc(scores, 1)

            def part_b(h, c):
                t0, n = CHUNKS[c]
                wait_apart(pe, kv_ready, h * NCH + (c + 1))
                if c > 0:
                    wait_apart(pe, scores_decayed, h * NO + c)
                    if c > 1:
                        wait_apart(pe, out_normed, h * NO + (c - 1))
                    wait_apart(pe, state_new, h * 5 + c)
                    for k in range(2):
                        pe.matmul(A[0:n, 2, 0:DK], q_rot[:, k, t0:t0 + n], state[:, k, :], start=(k == 0), stop=False)
                    pe.matmul(A[0:n, 2, 0:DK], st[0:n, c % 2, 0:n], vt[0:n, c % 2, :],
                              start=False, stop=True).then_inc(out_ready, 1)
                for k in range(2):
                    mm = pe.matmul(A[:, 3, k * DK:(k + 1) * DK], kd[0:n, c % 2, k * P:(k + 1) * P], vt[0:n, c % 2, :],
                                   start=True, stop=True)
                mm.then_inc(state_part, 1)

            def part_c(h, c, bank=1):
                t0, n = CHUNKS[c]
                wait_apart(pe, out_normed, h * NO + c)
                if bank == 1:
                    wait_apart(pe, scores_decayed, h * NO + min(c + 2, NO))
                if c > 1:
                    wait_apart(pe, out_kept, h * NO + (c - 1))
                for e in range(2):
                    tr = pe.transpose(A[:, bank, e * P:e * P + n], yn[0:n, e * P:(e + 1) * P], ident[0:n, 0:n])
                tr.then_inc(out_turned, 1)

            def sample_out(h):
                wait_apart(pe, scores_decayed, h * NO + NO)
                wait_apart(pe, kv_ready, h * NCH + NCH)
                wait_apart(pe, out_normed, h * NO + (NO - 1))
                wait_apart(pe, states_in, h * (16 * DEC_B) + 16 * DEC_B)
                for e in range(2):
                    pe.matmul(A[:, 2, e * TS:(e + 1) * TS], vt_s[0:TS, e * P:(e + 1) * P], st_s[:, :],
                              start=(e == 0), stop=False, skip_group_check=True)
                for b in range(DEC_B):
                    for e in range(2):
                        for k in range(2):
                            c0 = e * TS + b * DEC_T
                            mm = pe.matmul(A[:, 2, c0:c0 + DEC_T], states[:, b, k, e * P:(e + 1) * P],
                                           q_rot[:, k, TP + b * DEC_T:TP + (b + 1) * DEC_T],
                                           start=False, stop=(b == DEC_B - 1 and e == 1 and k == 1), skip_group_check=True)
                mm.then_inc(sample_out_ready, 1)

            def sample_turn(h):
                wait_apart(pe, sample_out_kept, h + 1)
                wait_apart(pe, out_kept, h * NO + (NO - 1))
                for e in range(2):
                    tr = pe.transpose(A[0:TS, 1, e * P:(e + 1) * P], xs[:, e, :], ident[:, :])
                tr.then_inc(out_ready, 1)

            def sample_state(h, b):
                bank = (3, 0)[b % 2]
                wait_apart(pe, own_keys_ready, h * DEC_B + (b + 1))
                if b >= 2:
                    wait_apart(pe, sample_state_new, h * DEC_B + (b - 1))
                if b == 0:
                    wait_apart(pe, state_new, h * 5 + 5)
                for k in range(2):
                    mm = pe.matmul(A[:, bank, k * DK:(k + 1) * DK], kb[0:TS, b % 2, k * P:(k + 1) * P], vt_s[0:TS, :],
                                   start=True, stop=True)
                mm.then_inc(sample_state_part, 1)

            def sample_step(h, i):
                if i == 0:
                    part_c(h, 4)
                elif i == 1:
                    sample_out(h)
                elif i == 2:
                    sample_turn(h)
                elif i < 3 + DEC_B:
                    sample_state(h, i - 3)
                elif i == 3 + DEC_B:
                    part_c(h, SMP, bank=2)

            def values_keys_queries(h, last=None):
                for z in range(1 if last is None else 0, 6):
                    for q in range(SLOTS):
                        piece(h * RET_BLOCKS + z, q, z % 2, h * 4 + (U_IN + z // 2), xh, xl, t0=M0 if z >= 4 else 0)
                        if last is not None:
                            sample_step(last, 4 * z + q)

            def prompt(h):
                for t in range(8):
                    z = 6 + t // 4
                    piece(h * RET_BLOCKS + z, t % 4, z % 2, h * 4 + (U_IN + 3), xh, xl, t0=M0)
                    if 2 <= t:
                        part_a(h, t - 2)
                    if 3 <= t:
                        part_b(h, t - 3)
                    if 5 <= t:
                        part_c(h, t - 4)

            values_keys_queries(0)
            prompt(0)
            with pe.Fori(0, HEADS - 1) as i:
                values_keys_queries(i + 1, i)
                prompt(i + 1)

            for i in range(SAMPLE_STEPS):
                b = B_SWA + i // 4
                piece(b, i % 4, b % 2, U_IN + b // 2, xh, xl, t0=0 if i < 8 else M0)
                sample_step(HEADS - 1, i)

            def swap(src, bank, t0=0):
                nt = NT if t0 == 0 else NL
                for n in range(2):
                    mm = pe.matmul(A[:, bank + n, 0:nt], perm[:, src, :],
                                   (z_raw if src == 0 else z_rot)[:, t0 + n * nt:t0 + (n + 1) * nt],
                                   start=True, stop=True)
                return mm

            piece(B_SWA + 3, 0, 1, U_IN + B_SWA // 2 + 1, xh, xl, t0=M0)
            pe.wait_ge(swa_in, 16 * 4)
            pe.wait_ge(g_free[0], U_IN + B_SWA // 2 + 1)
            pe.wait_ge(gated_lo, HEADS)
            swap(0, 0).then_inc(kv_step, 1)
            piece(B_SWA + 3, 1, 1, 0, xh, xl, t0=M0)
            pe.wait_ge(g_free[1], U_IN + B_SWA // 2 + 1)
            for n, (t0, w) in enumerate(CHUNKS):
                tr = pe.transpose(A[0:w, 2 + n // 4, (n % 4) * P:(n % 4 + 1) * P], sv_raw[:, t0:t0 + w], ident[:, :])
            tr.then_inc(kv_step, 1)
            piece(B_SWA + 3, 2, 1, 0, xh, xl, t0=M0)
            pe.wait_ge(rotated, 1)
            swap(1, 0).then_inc(kv_step, 1)
            pe.wait_ge(kv_step_kept, 1)
            pe.transpose(A[:, 2, 0:P], z_rot[:, TP - P:TP], ident[:, :])
            pe.transpose(A[0:TS, 2, P:2 * P], z_rot[:, TP:T], ident[:, :]).then_inc(kv_step, 1)
            piece(B_SWA + 3, 3, 1, 0, xh, xl, t0=M0)
            pe.wait_ge(kv_step_kept, 2)
            swap(2, 0).then_inc(kv_step, 1)

            def logits(j, n):
                kv = j // 4
                t0 = CHUNKS[n + 1][0]
                k0, k1 = CHUNKS[n][0], t0 + P
                if j * 4 + n:
                    pe.wait_ge(logits_masked, j * 4 + n)
                for i in range(2):
                    mm = pe.matmul(A[:, 2 + i, key_col(n):2 * P],
                                   z_rot[i * HD:(i + 1) * HD, t0:t0 + P], k2[i * HD:(i + 1) * HD, kv, k0:k1],
                                   start=True, stop=True)
                mm.then_inc(logits_ready, 1)

            def turn_probs(j, n):
                pe.wait_ge(probs, j * 4 + n + 1)
                if j * 4 + n:
                    pe.wait_ge(probs_kept, j * 4 + n)
                for kt in range(2):
                    kw = CHUNKS[n + kt][1]
                    for i in range(2):
                        c = (kt * 2 + i) * P
                        tr = pe.transpose(A[0:kw, 0, c:c + P], lg[:, n % 2, i, (kt + 1) * P - kw:(kt + 1) * P], ident[:, :])
                tr.then_inc(probs_turned, 1)

            def weigh(j, n):
                kv = j // 4
                pe.wait_ge(probs_kept, j * 4 + n + 1)
                if j * 4 + n:
                    pe.wait_ge(mix_lo_done, j * 4 + n)
                for i in range(2):
                    for kt in range(2):
                        kw = CHUNKS[n + kt][1]
                        mm = pe.matmul(A[i * HD:(i + 1) * HD, 1, 0:P], v_tok[0:kw, n + kt, kv * HD:(kv + 1) * HD],
                                       pt[0:kw, kt, i, :], start=(kt == 0), stop=(kt == 1))
                mm.then_inc(mix_ready, 1)

            def ret_out_piece(p, ks=(0, KP)):
                out_piece(B_OUT + p // 4, p % 4, U_OUT + p // 4, 0, ks)

            for j in range(8):
                def half_piece(i):
                    ks = (0, KP // 2) if i % 2 == 0 else (KP // 2, KP)
                    if j < 6:
                        piece(B_SWA + 4 + j, i // 2, j % 2, U_IN + (B_SWA + 4 + j) // 2, xh, xl, ks=ks, t0=M0)
                    else:
                        ret_out_piece(4 * (j - 6) + i // 2, ks)

                half_piece(0)
                if j:
                    weigh(j - 1, 2)
                half_piece(1)
                pe.wait_ge(g_free[j % 2], U_IN + (B_SWA + 2 + j) // 2 + 1)
                if j:
                    pe.wait_ge(probs_kept, j * 4 - 1)
                    pe.wait_ge(mix_lo_done, j * 4 - 1)
                else:
                    pe.wait_ge(kv_step_kept, 4)
                swap(0, 0, M0).then_inc(q_swapped, 1)
                half_piece(2)
                pe.wait_ge(rotated, 2 + j)
                if j:
                    turn_probs(j - 1, 3)
                logits(j, 0)
                if j:
                    weigh(j - 1, 3)
                half_piece(3)
                logits(j, 1)
                half_piece(4)
                turn_probs(j, 0)
                logits(j, 2)
                half_piece(5)
                weigh(j, 0)
                turn_probs(j, 1)
                logits(j, 3)
                half_piece(6)
                weigh(j, 1)
                half_piece(7)
                turn_probs(j, 2)
            ret_pieces = iter(range(8, 4 * (KT // 2)))
            ret_out_piece(next(ret_pieces))
            weigh(7, 2)
            turn_probs(7, 3)
            ret_out_piece(next(ret_pieces))
            weigh(7, 3)

            def cache_turn(b):
                pe.wait_ge(c_k[b % CACHE_SLOTS], 32 * (b // CACHE_SLOTS + 1))
                if b:
                    pe.wait_ge(ck_kept, b)
                else:
                    pe.wait_ge(mix_lo_done, 32)
                pe.transpose(A[:, 0, 0:P], kc[:, b % CACHE_SLOTS, :], ident[:, :]).then_inc(ck_turned, 1)

            def cache_logits(b):
                pe.wait_ge(ck_kept, b + 1)
                if b == 0:
                    pe.wait_ge(sample_q, 16 * 16)
                else:
                    pe.wait_ge(c_masked, b)
                for kv in range(2):
                    r = slice(kv * HD, (kv + 1) * HD)
                    q_b = qs[r, b, :, :].rearrange("p r t -> p (r t)")
                    pe.matmul(A[r, 1, 0:P], q_b, kct[r, b % 2, :], start=True, stop=True)
                    mm = pe.matmul(A[r, 1, P:P + TS], q_b, k2[r, kv, TP:T], start=True, stop=True)
                mm.then_inc(c_logits, 1)

            def cache_probs(b):
                pe.wait_ge(c_probs, b + 1)
                if b:
                    pe.wait_ge(c_kept, b)
                pe.transpose(A[:, 2, 0:P], ls[:, b % 2, 0:P], ident[:, :])
                pe.transpose(A[0:TS, 2, P:2 * P], ls[:, b % 2, P:P + TS], ident[:, :]).then_inc(c_turned, 1)

            def cache_weigh(b):
                pe.wait_ge(c_kept, b + 1)
                for kv in range(2):
                    r = slice(kv * HD, (kv + 1) * HD)
                    o = A[r, 3, b * TS:(b + 1) * TS]
                    pe.matmul(o, vc[:, b % CACHE_SLOTS, r], ptc[:, b % 2, r], start=(b == 0), stop=False,
                              skip_group_check=True)
                    mm = pe.matmul(o, v_tok[0:TS, 5, r], ptn[:, b % 2, r], start=False, stop=(b == DEC_B - 1),
                                   skip_group_check=True)
                mm.then_inc(c_mixed, 1)

            for b in range(DEC_B + 1):
                if b:
                    ret_out_piece(next(ret_pieces))
                if b < DEC_B:
                    cache_turn(b)
                    ret_out_piece(next(ret_pieces))
                    cache_logits(b)
                if b:
                    cache_probs(b - 1)
                if third_piece(b):
                    ret_out_piece(next(ret_pieces))
                if b:
                    cache_weigh(b - 1)
            for p in ret_pieces:
                ret_out_piece(p)

            def column_sums(x, bank=0):
                for n in range(2):
                    mm = pe.matmul(A[:, bank + n, 0:NL], ones[:, :], x[:, n * NL:(n + 1) * NL], start=True, stop=True)
                return mm

            pe.wait_ge(osm_lo, 1)
            for q in range(SLOTS):
                out_piece(B_OUT + KT // 2, q, U_OUT2, 1)
                if q == 0:
                    pe.wait_ge(ones_ready, 3)
                    column_sums(yb[:, 0, :]).then_inc(shift_part, 1)
            with pe.Fori(1, KT // 2) as i:
                for q in range(SLOTS):
                    out_piece(i + (B_OUT + KT // 2), q, i + U_OUT2, 1)

            pe.wait_ge(shift_ready, 1)
            pe.wait_ge(sum_done, KT + 1)
            column_sums(acc_s).then_inc(mean_part, 1)
            pe.wait_ge(squares_done, KT)
            column_sums(acc_q, 2).then_inc(var_part, 1)

            def gate_up(b0, u0, m0=0):
                with pe.Fori(m0, KP) as m:
                    ffn_tile(m * 2 + b0, 0, m + u0)
                    ffn_tile(m * 2 + (b0 + 1), 1, m + u0)

            def downs(b0, u0, gs, fl_count):
                wait_apart(pe, f_lo, fl_count)
                with pe.Fori(0, DN) as r:
                    down(r + b0, gs, r * 2 + u0)

            for p in range(2 * SLOTS):
                pe.wait_ge(piece_lo, B_FFN * 4 + (p + 5))
                if p < 2:
                    pe.wait_ge(g_free[p], U_FFN)
                if p:
                    pe.wait_ge(h_lo, KP * (p // 2) + KP)
                for k in range(KP):
                    kk = KP * (p // 2) + k
                    if p == 0:
                        pe.wait_ge(h_lo, k + 1)
                    for w, x, one in ((wh, hh, kk == 0), (wh, hl, False), (wl, hh, False)):
                        for n in range(2):
                            mm = pe.matmul(G[:, p % 2, n, 0:NL], w[:, p % SLOTS, k, :], x[:, kk, n * NL:(n + 1) * NL],
                                           start=one, stop=(kk == KT - 1 and w is wl))
                mm.then_inc(piece_used, 1)
            gate_up(B_FFN, U_FFN, 1)
            with pe.Fori(0, LOOPS) as i:
                b0 = i * (2 * (GU + DN)) + B_LOOP
                u0 = i * (2 * (KP + KT // 2)) + U_LOOP
                gate_up(b0, u0)
                downs(b0 + GU, u0 + KP, 0, i * 8 + 4)
                gate_up(b0 + GU + DN, u0 + KP + 8)
                downs(b0 + 2 * GU + DN, u0 + 2 * KP + 8, 1, i * 8 + 8)
            pe.wait_ge(f_lo, KP * GROUPS)

            def turn_out(rb_, tts=range(len(TT))):
                for par in range(2):
                    pe.wait_ge(g_free[par], U_LAST + 2 * rb_ + 2)
                for tt in tts:
                    t0, n = TT[tt]
                    e = rb_ * 5 + tt
                    if e >= 4:
                        pe.wait_ge(y_kept, e - 3)
                    for q in range(4):
                        tr = pe.transpose(A[0:n, e % 4, q * P:(q + 1) * P], yb[:, rb_ * 4 + q, t0:t0 + n], ident[:, :])
                    tr.then_inc(y_turned, 1)

            for rb_ in range(DN):
                for q, tts in enumerate(((), (0, 1), (2, 3), (4,))):
                    down(B_LAST + rb_, 0, U_LAST + 2 * rb_, (q,))
                    if rb_ and tts:
                        turn_out(rb_ - 1, tts)
            turn_out(DN - 1)

        @block.scalar
        def _(act):
            c = Count(act, act_chain)

            def hi(b, q, free=True):
                act.wait_ge(raw_in[q], b * 16 + 16)
                if free:
                    act.wait_ge(piece_used, b * 4 + (q - 3))
                act.copy(wh[:, q], raw[:, q]).then_inc(piece_hi, 1)

            def his(b, qs_):
                for q in qs_:
                    hi(b, q)

            for i in range(4):
                act.dma_start(xin[:, i, :], I["x_prompt"][0, i * P:(i + 1) * P, :]).then_inc(x_in[i], 16)
            act.dma_start(xin[0:TS, 4, :], I["x_sample"].rearrange("b t d -> (b t) d")).then_inc(x_in[4], 16)
            act.dma_start(xin[TS:TS + N_META, 4, :], I["meta_tokens"]).then_inc(x_in[4], 16)
            for i, n in enumerate(IN_TILES):
                act.wait_ge(in_var, i + 1)
                act.activation(small[0:n, in_col(3, i)], small[0:n, in_col(2, i)], ACT.Sqrt).then_inc(in_dev, 1)
                act.wait_ge(in_scale_ready, i + 1)
                act.activation(xin[0:n, i, :], xin[0:n, i, :], ACT.Identity, bias=small[0:n, in_col(4, i)],
                               scale=small[0:n, in_col(3, i)]).then_inc(in_normed, 1)
            act.wait_ge(vec_turned, 1)
            act.copy(vec[:, :, :], G[:, 0, 0, 0:4 * KT].rearrange("p (n k) -> p n k", n=4)).then_inc(vec_ready, 1)
            for k in range(KT):
                act.wait_ge(g_free[k % 2], k // 2 + 1)
                act.copy(xh[:, k, :], xf[:, k % XF_SLOTS, :]).then_inc(x_hi, 1)
                if k < SLOTS:
                    hi(0, k, free=False)
                if k in IN_PIECES:
                    hi(1, IN_PIECES.index(k))

            def copy_tile(b, par, dst, t0=0):
                act.wait_ge(piece_used, b * 4 + 4)
                return act.copy(halves(dst[:, t0:T]), gt(par) if t0 == 0 else gl(par))

            def tokens_first(h, i):
                t0, n = CHUNKS[i]
                act.wait_ge(kv_turned, h * NCH + (i + 1))
                if i == SMP:
                    act.wait_ge(sample_state_new, h * DEC_B)
                    act.copy(kd_s[0:n, :], A[0:n, 0, 0:DK])
                    act.copy(vt_s[0:n, :], A[0:n, 0, DK:2 * DK]).then_inc(kv_ready, 1)
                    return
                if i >= 2:
                    act.wait_ge(state_part, h * 5 + (i - 1))
                act.mul(kd[0:n, i % 2, :], A[0:n, 0, 0:DK], hc[0:n, (HC_KD0 if i == 0 else HC_KD):][:, 0:1])
                act.copy(vt[0:n, i % 2, :], A[0:n, 0, DK:2 * DK]).then_inc(kv_ready, 1)

            def root(h, i):
                n = CHUNKS[i][1]
                act.wait_ge(out_var, h * NO + i)
                act.activation(small[0:n, SD], small[0:n, VE], ACT.Sqrt).then_inc(out_dev, 1)

            def sample_step(h, i):
                if i == 1:
                    act.wait_ge(sample_out_ready, h + 1)
                    act.copy(xs[:, :, :], A[:, 2, 0:2 * TS].rearrange("p (e t) -> p e t", e=2)).then_inc(sample_out_kept, 1)
                elif i == 2:
                    root(h, SMP)
                elif i == SAMPLE_STEPS:
                    act.wait_ge(gated, h + 1)
                    act.copy(mh[:, bass.ds(h * 2, 2), M0:T], ret_out[:, :, M0:T]).then_inc(gated_hi, 1)

            def values_keys_queries(h, last=None):
                for z in range(6):
                    b = h * RET_BLOCKS + z
                    for q in range(SLOTS):
                        if q == 3:
                            if z == 4:
                                act.wait_ge(rope_a, h * 2 + 1)
                                act.wait_ge(rope_b, h * 2 + 1)
                            dst = (v_raw, kq_raw, kq_raw)[z // 2][:, z % 2, :]
                            copy_tile(b, z % 2, dst, M0 if z >= 4 else 0).then_inc(g_free[z % 2], 1)
                        if last is not None or z or q >= len(IN_PIECES):
                            hi(b + 1, q)
                        if last is not None:
                            sample_step(last, 4 * z + q)

            def prompt(h):
                act.wait_ge(head_in, h * 16 + 16)
                for t in range(8):
                    b = h * RET_BLOCKS + 6 + t // 4
                    hi(b + 1, t % 4)
                    if t % 4 == 3:
                        act.wait_ge(piece_used, b * 4 + 4)
                        act.activation(halves(gate[:, t // 4, M0:T]), gl(t // 4), ACT.Silu).then_inc(g_free[t // 4], 1)
                    if 2 <= t:
                        tokens_first(h, t - 2)
                    if 4 <= t:
                        root(h, t - 3)

            values_keys_queries(0)
            prompt(0)
            with act.Fori(0, HEADS - 1) as i:
                values_keys_queries(i + 1, i)
                prompt(i + 1)

            for i in range(SAMPLE_STEPS):
                b = B_SWA + i // 4
                if i in (3, 7):
                    copy_tile(b, b % 2, (z_raw if i == 3 else sv_raw)[:, :]).then_inc(g_free[b % 2], 1)
                hi(b + 1, i % 4)
                sample_step(HEADS - 1, i)
            sample_step(HEADS - 1, SAMPLE_STEPS)
            b = B_SWA + 3
            hi(b + 1, 0)
            hi(b + 1, 1)
            act.wait_ge(kv_step, 2)
            act.copy(v_tok[0:M0, 0, :], A[0:M0, 2, 0:P])
            act.copy(v_tok[:, 1:4, :], A[:, 2, P:].rearrange("p (n d) -> p n d", n=3))
            act.copy(v_tok[:, 4, :], A[:, 3, 0:P])
            act.copy(v_tok[0:TS, 5, :], A[0:TS, 3, P:2 * P]).then_inc(kv_step_kept, 1)
            act.wait_ge(rotated, 1)
            copy_tile(b - 1, 0, z_raw[:, :], M0).then_inc(g_free[0], 1)
            hi(b + 1, 2)
            act.wait_ge(kv_step, 3)
            act.copy(halves(k2[:, 0, :]), A[:, 0:2, 0:NT]).then_inc(kv_step_kept, 1)
            act.wait_ge(kv_step, 4)
            act.copy(k_tok[:, 0, :], A[:, 2, 0:P])
            act.copy(k_tok[0:TS, 1, :], A[0:TS, 2, P:2 * P]).then_inc(kv_step_kept, 1)
            hi(b + 1, 3)
            act.wait_ge(kv_step, 5)
            act.copy(halves(k2[:, 1, :]), A[:, 0:2, 0:NT]).then_inc(kv_step_kept, 1)

            def exps(j, n):
                c0 = key_col(n)
                s0 = 40 + 8 * (n % 2)
                act.wait_ge(neg_max, j * 4 + n + 1)
                for i in range(2):
                    act.activation(lg[:, n % 2, i, c0:], lg[:, n % 2, i, c0:], ACT.Exp,
                                   bias=small[:, s0 + i:s0 + i + 1], accum_out=small[:, s0 + 4 + i:s0 + 5 + i])
                act.activation(small[:, s0 + 6:s0 + 8], small[:, s0 + 2:s0 + 4], ACT.Exp).then_inc(exp_ready, 1)

            def keep_probs(j, n):
                act.wait_ge(probs_turned, j * 4 + n + 1)
                src = A[:, 0, :].rearrange("p (k i q) -> p k i q", k=2, i=2)
                if n == 0:
                    act.copy(pt[0:M0, 0, :, :], src[0:M0, 0, :, :])
                    ins = act.copy(pt[:, 1, :, :], src[:, 1, :, :])
                else:
                    ins = act.copy(pt[:, :, :, :], src)
                ins.then_inc(probs_kept, 1)

            def mix_hi(j, n):
                t0 = CHUNKS[n + 1][0]
                act.wait_ge(mix_ready, j * 4 + n + 1)
                act.copy(mh[:, 8 + j, t0:t0 + P], A[:, 1, 0:P]).then_inc(mix_hi_done, 1)

            act.wait_ge(states_out, 16 * DEC_B * HEADS)
            for j in range(8):
                b = B_SWA + 3 + j

                def h_(q):
                    hi(b + 2, q)
                if j:
                    mix_hi(j - 1, 2)
                h_(0)
                if j:
                    keep_probs(j - 1, 3)
                    mix_hi(j - 1, 3)
                exps(j, 0)
                if j < 7:
                    copy_tile(b, (j + 1) % 2, z_raw[:, :], M0).then_inc(g_free[(j + 1) % 2], 1)
                h_(1)
                keep_probs(j, 0)
                exps(j, 1)
                h_(2)
                mix_hi(j, 0)
                exps(j, 2)
                keep_probs(j, 1)
                mix_hi(j, 1)
                exps(j, 3)
                h_(3)
                keep_probs(j, 2)

            def cache_exp(b):
                s0 = 60 + 8 * (b % 2)
                act.wait_ge(c_neg_max, b + 1)
                act.activation(ls[:, b % 2, :], ls[:, b % 2, :], ACT.Exp, bias=small[:, s0:s0 + 1],
                               accum_out=small[:, s0 + 2:s0 + 3])
                act.activation(small[:, s0 + 3:s0 + 4], small[:, s0 + 1:s0 + 2], ACT.Exp).then_inc(c_exp, 1)

            ret_pieces = iter(range(8, 4 * (KT // 2)))

            def ret_hi(p):
                hi(B_OUT + 1 + p // 4, p % 4)

            ret_hi(next(ret_pieces))
            mix_hi(7, 2)
            keep_probs(7, 3)
            ret_hi(next(ret_pieces))
            mix_hi(7, 3)
            for b in range(DEC_B + 1):
                if b:
                    ret_hi(next(ret_pieces))
                if b < DEC_B:
                    act.wait_ge(ck_turned, b + 1)
                    if b == 0:
                        act.wait_ge(mix_lo_done, 32)
                    act.copy(kct[:, b % 2, :], A[:, 0, 0:P]).then_inc(ck_kept, 1)
                    ret_hi(next(ret_pieces))
                if b:
                    act.wait_ge(c_turned, b)
                    act.copy(ptc[:, (b - 1) % 2, :], A[:, 2, 0:P])
                    act.copy(ptn[:, (b - 1) % 2, :], A[0:TS, 2, P:2 * P]).then_inc(c_kept, 1)
                if b < DEC_B:
                    cache_exp(b)
                if third_piece(b):
                    ret_hi(next(ret_pieces))
            act.wait_ge(c_mixed, DEC_B)
            act.copy(os_[:, :, :].rearrange("p r (b t) -> p b r t", b=DEC_B),
                     A[:, 3, :].rearrange("p (b r t) -> p b r t", b=DEC_B, r=8)).then_inc(os_ready, 1)
            for p in ret_pieces:
                ret_hi(p)
            act.wait_ge(osm_ready, 64)
            act.copy(mh[:, 8:16, TP:T], osm[:, :, :]).then_inc(osm_hi, 1)

            def square(r, par, done):
                act.wait_ge(g_free[par], done)
                if not isinstance(r, int) or r >= 2:
                    act.wait_ge(squares_done, r - 1)
                act.activation(ln_t[:, par, :], yb[:, r, :] if isinstance(r, int) else
                               yb[:, bass.ds(r, 1), :].rearrange("p o t -> p (o t)"), ACT.Square).then_inc(squared, 1)

            b = B_OUT + KT // 2
            his(b + 1, range(3))
            square(0, 0, U_OUT2 + 1)
            hi(b + 1, 3)
            with act.Fori(1, KT // 2) as i:
                hi(i + (b + 1), 0)
                square(i * 2 - 1, 1, i + U_OUT2)
                hi(i + (b + 1), 1)
                hi(i + (b + 1), 2)
                square(i * 2, 0, i + (U_OUT2 + 1))
                hi(i + (b + 1), 3)
            square(KT - 1, 1, U_FFN)

            def first_hi(p):
                hi(B_FFN + 1 + p // 4, p % 4)

            act.wait_ge(mean_ready, 1)
            act.activation(msq[:, :], mean[:, :], ACT.Square).then_inc(mean_squared, 1)
            act.wait_ge(var_ready, 1)
            act.activation(rstd[:, :], rstd[:, :], ACT.Sqrt).then_inc(dev_ready, 1)
            for r in range(KT):
                act.wait_ge(normed, r + 1)
                c.link(act.activation(yb[:, r, :], ln_t[:, r % 2, :], ACT.Identity,
                                      bias=vec[:, 3, r:r + 1], scale=vec[:, 2, r:r + 1]))
                act.copy(hh[:, r, :], yb[:, r, :]).then_inc(h_hi, 1)
                if r in LN_PIECES:
                    first_hi(LN_PIECES.index(r))
            for p in range(len(LN_PIECES), 7):
                first_hi(p)

            def gate_up(b0, gs, u0, m0=0):
                with act.Fori(m0, KP) as m:
                    b = m * 2 + b0
                    his(b + 1, range(3))
                    act.wait_ge(piece_used, b * 4 + 4)
                    act.activation(halves(sg[:, :]), gl(0), ACT.Silu).then_inc(g_free[0], 1)
                    hi(b + 1, 3)
                    his(b + 2, range(3))
                    act.wait_ge(g_free[1], m + (u0 + 1))
                    act.copy(fh[:, gs, bass.ds(m, 1), :], fu[:, :].rearrange("p (o t) -> p o t", o=1)).then_inc(f_hi, 1)
                    hi(b + 2, 3)

            def downs(b0):
                with act.Fori(0, DN) as r:
                    his(r + (b0 + 1), range(4))

            act.wait_ge(piece_used, B_FFN * 4 + 7)
            act.activation(halves(sg[:, :]), gl(0), ACT.Silu).then_inc(g_free[0], 1)
            act.wait_ge(g_free[1], U_FFN + 1)
            act.copy(fh[:, 0, 0, :], fu[:, :]).then_inc(f_hi, 1)
            hi(B_FFN + 2, 3)
            gate_up(B_FFN, 0, U_FFN, 1)
            with act.Fori(0, LOOPS) as i:
                b0 = i * (2 * (GU + DN)) + B_LOOP
                u0 = i * (2 * (KP + KT // 2)) + U_LOOP
                gate_up(b0, 1, u0)
                downs(b0 + GU)
                gate_up(b0 + GU + DN, 0, u0 + KP + 8)
                downs(b0 + 2 * GU + DN)

            def out_copy(rb_, tts=range(len(TT))):
                for tt in tts:
                    n = TT[tt][1]
                    e = rb_ * 5 + tt
                    act.wait_ge(y_turned, e + 1)
                    act.copy(yo[0:n, tt, rb_ * 512:(rb_ + 1) * 512], A[0:n, e % 4, :]).then_inc(y_kept, 1)

            for rb_ in range(DN):
                for q, tts in enumerate(((), (0, 1), (2, 3), (4,))):
                    if rb_ < DN - 1:
                        hi(B_LAST + rb_ + 1, q)
                    if rb_:
                        out_copy(rb_ - 1, tts)
            out_copy(DN - 1)
            for tt, (t0, n) in enumerate(TT):
                act.wait_ge(y_var, tt + 1)
                act.activation(small[0:n, 80 + tt:81 + tt], small[0:n, 90 + tt:91 + tt], ACT.Sqrt).then_inc(y_dev, 1)
            for tt, (t0, n) in enumerate(TT):
                act.wait_ge(y_scale, tt + 1)
                act.activation(yo[0:n, tt, :], yo[0:n, tt, :], ACT.Identity, bias=small[0:n, 110 + tt:111 + tt],
                               scale=small[0:n, 80 + tt:81 + tt]).then_inc(y_normed, 1)

        @block.vector
        def _(dve):
            c = Count(dve, dve_chain)

            def lo(b, q):
                dve.wait_ge(piece_hi, b * 4 + (q + 1))
                dve.tensor_tensor(wl[:, q], raw[:, q], f32(wh[:, q]), ALU.subtract).then_inc(piece_lo, 1)

            def los(b, qs_):
                for q in qs_:
                    lo(b, q)

            dve.memset(small[:, 159:160], 0.0).then_inc(piece_lo, 4)

            def in_scale(i):
                n = IN_TILES[i]
                dve.wait_ge(in_dev, i + 1)
                c.link(dve.reciprocal(small[0:n, in_col(3, i)], small[0:n, in_col(3, i)]))
                dve.scalar_tensor_tensor(out=small[0:n, in_col(4, i)], in0=small[0:n, in_col(0, i)], scalar=-1.0,
                                         in1=small[0:n, in_col(3, i)], op0=ALU.mult, op1=ALU.mult).then_inc(in_scale_ready, 1)

            for i, n in enumerate(IN_TILES):
                dve.wait_ge(x_in[i], 32 if i == 4 else 16)
                for k in range(4):
                    ins = dve.bn_stats(small[0:n, 6 * k:6 * k + 6], xin[0:n, i, 512 * k:512 * (k + 1)])
                    if k == 0 and i:
                        in_scale(i - 1)
                c.link(ins)
                c.link(dve.bn_aggr(small[0:n, in_col(0, i, 2)], small[0:n, ST6]))
                dve.tensor_scalar(small[0:n, in_col(2, i)], small[0:n, in_col(1, i)], LN_EPS, None, ALU.add).then_inc(in_var, 1)
            in_scale(4)
            dve.wait_ge(vec_ready, 1)
            for k in range(KT):
                dve.wait_ge(in_turned, k + 1)
                if k >= XF_SLOTS:
                    dve.wait_ge(x_lo, k - XF_SLOTS + 1)
                x = xf[:, k % XF_SLOTS, :]
                b0 = k % 2 * 2
                for dst, src in ((x[:, 16:400], A[:, b0, 0:384]), (x[:, 400:T], A[:, b0 + 1, 0:192]),
                                 (x[:, 0:16], A[:, b0 + 1, 192:208])):
                    ins = dve.tensor_scalar(dst, src, vec[:, 0, k:k + 1], vec[:, 1, k:k + 1], ALU.mult, ALU.add)
                ins.then_inc(g_free[k % 2], 1)
                if 1 <= k <= SLOTS:
                    lo(0, k - 1)
                if k - 1 in IN_PIECES:
                    lo(1, IN_PIECES.index(k - 1))

            def rope(x, out, count, t0):
                for par in range(2):
                    dve.wait_ge(g_free[par], count)
                dve.wait_ge(rot_in, 16)
                dve.tensor_tensor(rope_v[:, 0, t0:], x[:, 0, t0:], ret_rot[:, 0, t0:], ALU.mult)
                c.link(dve.tensor_tensor(rope_v[:, 1, t0:], x[:, 1, t0:], ret_rot[:, 1, t0:], ALU.mult))
                dve.tensor_tensor(out[:, 0, t0:], rope_v[:, 0, t0:], rope_v[:, 1, t0:], ALU.subtract).then_inc(rope_a, 1)

            def masked(h, i):
                n = CHUNKS[i][1]
                dve.wait_ge(scores, h * NO + i)
                if i == SMP:
                    dve.wait_ge(head_s_in, h * 16 + 16)
                    dve.tensor_tensor(st_s[:, :], A[0:n, 1, 0:n], hcs[0:n, 0:n], ALU.mult).then_inc(scores_decayed, 1)
                    return
                if i >= 3:
                    dve.wait_ge(out_ready, h * NO + (i - 2))
                dve.tensor_tensor(st[0:n, i % 2, 0:n], A[0:n, 1, 0:n], hc[0:n, 0:n], ALU.mult).then_inc(scores_decayed, 1)

            def norm(h, i):
                n = CHUNKS[i][1]
                src = A[0:n, 1 if i == SMP else 2, 0:DK]
                dve.wait_ge(out_ready, h * NO + i)
                c.link(dve.bn_stats(small[0:n, 0:6], src), met=vec_ready)
                c.link(dve.bn_aggr(small[0:n, MV], small[0:n, 0:6]))
                eps = hcs[0:n, HS_EPS:HS_EPS + 1] if i == SMP else hc[0:n, HC_EPS:HC_EPS + 1]
                dve.tensor_tensor(small[0:n, VE], small[0:n, 25:26], eps, ALU.add).then_inc(out_var, 1)
                dve.wait_ge(out_dev, h * NO + i)
                c.link(dve.reciprocal(small[0:n, RS], small[0:n, SD]))
                if i > 1:
                    dve.wait_ge(out_turned, h * NO + (i - 1))
                dve.tensor_scalar(yn[0:n, :], src, small[0:n, 24:25], small[0:n, RS],
                                  ALU.subtract, ALU.mult).then_inc(out_normed, 1)

            def new_state(h, i):
                dve.wait_ge(state_part, h * 5 + (i + 1))
                sv = A[:, 3, :].rearrange("p (k e) -> p k e", k=2)
                if i == 0:
                    dve.tensor_copy(state[:, :, :], sv).then_inc(state_new, 1)
                else:
                    dve.scalar_tensor_tensor(out=state[:, :, :], in0=state[:, :, :], scalar=hc[:, HC_G:HC_G + 1],
                                             in1=sv, op0=ALU.mult, op1=ALU.add).then_inc(state_new, 1)

            def turned(h, i, bank=1):
                t0, n = CHUNKS[i]
                dve.wait_ge(out_turned, h * NO + i)
                dve.tensor_copy(ret_out[:, :, t0:t0 + n],
                                A[:, bank, 0:DK].rearrange("p (e t) -> p e t", e=2)[:, :, 0:n]).then_inc(out_kept, 1)

            def own_keys(h, b):
                if b == 0:
                    dve.wait_ge(kv_ready, h * NCH + NCH)
                dve.tensor_scalar(kb[0:TS, b % 2, :], kd_s[0:TS, :], hcs[0:TS, HS_KB + b:HS_KB + b + 1], None,
                                  ALU.mult).then_inc(own_keys_ready, 1)

            def sample_state(h, b):
                bank = (3, 0)[b % 2]
                dve.wait_ge(sample_state_part, h * DEC_B + (b + 1))
                dve.scalar_tensor_tensor(out=states[:, b], in0=states[:, b], scalar=hcs[:, HS_G:HS_G + 1],
                                         in1=A[:, bank, :].rearrange("p (k e) -> p k e", k=2),
                                         op0=ALU.mult, op1=ALU.add).then_inc(sample_state_new, 1)

            def sample_step(h, i):
                if i == 0:
                    turned(h, 4)
                    own_keys(h, 0)
                    own_keys(h, 1)
                elif i == 2:
                    norm(h, SMP)
                elif 3 <= i < 3 + DEC_B:
                    sample_state(h, i - 3)
                    if i - 1 < DEC_B:
                        own_keys(h, i - 1)
                elif i == 3 + DEC_B:
                    turned(h, SMP, bank=2)
                    dve.wait_ge(out_kept, h * NO + NO)
                    for par in range(2):
                        dve.wait_ge(g_free[par], h * 4 + (U_IN + 4))
                    dve.tensor_tensor(ret_out[:, :, M0:], ret_out[:, :, M0:], gate[:, :, M0:], ALU.mult).then_inc(gated, 1)
                elif i == SAMPLE_STEPS:
                    dve.wait_ge(gated_hi, h + 1)
                    dve.tensor_tensor(ml[:, bass.ds(h * 2, 2), M0:T], ret_out[:, :, M0:], f32(mh[:, bass.ds(h * 2, 2), M0:T]),
                                      ALU.subtract).then_inc(gated_lo, 1)

            def values_keys_queries(h, last=None):
                for z in range(6):
                    b = h * RET_BLOCKS + z
                    for q in range(SLOTS):
                        if last is not None or z or q >= len(IN_PIECES):
                            lo(b + 1, q)
                        if last is not None:
                            sample_step(last, 4 * z + q)
                    if z in (3, 5):
                        rope(kq_raw, k_rot if z == 3 else q_rot, h * 4 + (U_IN + (2 if z == 3 else 3)), 0 if z == 3 else M0)

            def prompt(h):
                dve.wait_ge(head_in, h * 16 + 16)
                for t in range(8):
                    lo(h * RET_BLOCKS + (7 + t // 4), t % 4)
                    if 3 <= t:
                        masked(h, t - 2)
                    if 4 <= t:
                        norm(h, t - 3)
                    if 3 <= t:
                        new_state(h, t - 3)
                    if 5 <= t:
                        turned(h, t - 4)

            values_keys_queries(0)
            prompt(0)
            with dve.Fori(0, HEADS - 1) as i, c.loop(i, HEADS - 1, PER_HEAD):
                values_keys_queries(i + 1, i)
                prompt(i + 1)
            for i in range(SAMPLE_STEPS):
                lo(B_SWA + i // 4 + 1, i % 4)
                sample_step(HEADS - 1, i)
            sample_step(HEADS - 1, SAMPLE_STEPS)

            def rotate(count, sem_, val, t0=0):
                dve.wait_ge(sem_, val)
                c.link(dve.tensor_tensor(halves(z_tmp[:, t0:]), A[:, 0:2, 0:(T - t0) // 2], halves(swa_rot[:, 1, t0:]), ALU.mult))
                dve.wait_ge(cos_part, count)
                dve.tensor_tensor(z_rot[:, t0:], z_rot[:, t0:], z_tmp[:, t0:], ALU.add).then_inc(rotated, 1)

            dve.wait_ge(swa_in, 16 * 4)
            lo(B_SWA + 4, 0)
            rotate(1, kv_step, 1)
            los(B_SWA + 4, range(1, 4))

            def soft_a(j, n):
                c0 = key_col(n)
                s0 = 40 + 8 * (n % 2)
                l = lg[:, n % 2, :, c0:]
                dve.wait_ge(logits_ready, j * 4 + n + 1)
                dve.scalar_tensor_tensor(out=l, in0=A[:, 2:4, c0:2 * P],
                                         scalar=HD ** -0.5, in1=mask_p[:, None, c0:].to_broadcast([P, 2, 2 * P - c0]),
                                         op0=ALU.mult, op1=ALU.add).then_inc(logits_masked, 1)
                dve.wait_ge(logits_masked, j * 4 + n + 1)
                c.link(dve.tensor_reduce(small[:, s0:s0 + 2], l, AX_X, ALU.max))
                c.link(dve.tensor_tensor(small[:, s0:s0 + 2], small[:, s0:s0 + 2], sinks[:, 2 * j:2 * j + 2], ALU.max))
                c.link(dve.tensor_tensor(small[:, s0 + 2:s0 + 4], sinks[:, 2 * j:2 * j + 2], small[:, s0:s0 + 2],
                                         ALU.subtract))
                dve.tensor_scalar(small[:, s0:s0 + 2], small[:, s0:s0 + 2], -1.0, None, ALU.mult).then_inc(neg_max, 1)

            def soft_b(j, n):
                c0 = key_col(n)
                s0 = 40 + 8 * (n % 2)
                dve.wait_ge(exp_ready, j * 4 + n + 1)
                c.link(dve.tensor_tensor(small[:, s0 + 4:s0 + 6], small[:, s0 + 4:s0 + 6], small[:, s0 + 6:s0 + 8], ALU.add))
                c.link(dve.reciprocal(small[:, s0 + 4:s0 + 6], small[:, s0 + 4:s0 + 6]))
                for i in range(2):
                    ins = dve.tensor_scalar(lg[:, n % 2, i, c0:], lg[:, n % 2, i, c0:],
                                            small[:, s0 + 4 + i:s0 + 5 + i], None, ALU.mult)
                ins.then_inc(probs, 1)

            def mix_lo(j, n):
                t0 = CHUNKS[n + 1][0]
                dve.wait_ge(mix_hi_done, j * 4 + n + 1)
                dve.tensor_tensor(ml[:, 8 + j, t0:t0 + P], A[:, 1, 0:P], f32(mh[:, 8 + j, t0:t0 + P]),
                                  ALU.subtract).then_inc(mix_lo_done, 1)

            def residual(p):
                if p % 2:
                    r = p // 2
                    dve.wait_ge(piece_used, B_OUT * 4 + (p + 1))
                    c.link(dve.tensor_tensor(yb[:, r, :], f32(xh[:, r, M0:T]), f32(xl[:, r, M0:T]), ALU.add))
                    dve.scalar_tensor_tensor(out=halves(yb[:, r, :]), in0=halves(yb[:, r, :]), scalar=ALPHA, in1=gl(r % 2),
                                             op0=ALU.mult, op1=ALU.add).then_inc(g_free[r % 2], 1)

            def ret_lo(p):
                lo(B_OUT + 1 + p // 4, p % 4)
                residual(p)

            dve.wait_ge(states_out, 16 * DEC_B * HEADS)
            for j in range(8):
                def l_(q):
                    if j >= 6:
                        residual(4 * (j - 6) + q)
                if j:
                    dve.wait_ge(sample_q, 32 * j)
                if j:
                    mix_lo(j - 1, 2)
                l_(0)
                rotate(2 + j, q_swapped, 1 + j, M0)
                soft_a(j, 0)
                if j:
                    mix_lo(j - 1, 3)
                soft_b(j, 0)
                soft_a(j, 1)
                l_(1)
                soft_b(j, 1)
                soft_a(j, 2)
                l_(2)
                mix_lo(j, 0)
                soft_b(j, 2)
                soft_a(j, 3)
                mix_lo(j, 1)
                l_(3)
                soft_b(j, 3)

            def cache_soft_a(b):
                s0 = 60 + 8 * (b % 2)
                dve.wait_ge(c_logits, b + 1)
                dve.scalar_tensor_tensor(out=ls[:, b % 2, 0:P], in0=A[:, 1, 0:P], scalar=HD ** -0.5, in1=mask_c[:, :],
                                         op0=ALU.mult, op1=ALU.add)
                dve.scalar_tensor_tensor(out=ls[:, b % 2, P:P + TS], in0=A[:, 1, P:P + TS], scalar=HD ** -0.5,
                                         in1=mask_n[:, b, :], op0=ALU.mult, op1=ALU.add).then_inc(c_masked, 1)
                dve.wait_ge(c_masked, b + 1)
                c.link(dve.tensor_reduce(small[:, s0:s0 + 1], ls[:, b % 2, :], AX_X, ALU.max))
                c.link(dve.tensor_tensor(small[:, s0:s0 + 1], small[:, s0:s0 + 1], sink_s[:, :], ALU.max))
                c.link(dve.tensor_tensor(small[:, s0 + 1:s0 + 2], sink_s[:, :], small[:, s0:s0 + 1], ALU.subtract))
                dve.tensor_scalar(small[:, s0:s0 + 1], small[:, s0:s0 + 1], -1.0, None, ALU.mult).then_inc(c_neg_max, 1)

            def cache_soft_b(b):
                s0 = 60 + 8 * (b % 2)
                dve.wait_ge(c_exp, b + 1)
                c.link(dve.tensor_tensor(small[:, s0 + 2:s0 + 3], small[:, s0 + 2:s0 + 3], small[:, s0 + 3:s0 + 4], ALU.add))
                c.link(dve.reciprocal(small[:, s0 + 2:s0 + 3], small[:, s0 + 2:s0 + 3]))
                dve.tensor_scalar(ls[:, b % 2, :], ls[:, b % 2, :], small[:, s0 + 2:s0 + 3], None, ALU.mult).then_inc(c_probs, 1)

            ret_pieces = iter(range(8, 4 * (KT // 2)))
            dve.wait_ge(piece_lo, (B_OUT + 3) * 4 + 4)
            ret_lo(next(ret_pieces))
            mix_lo(7, 2)
            ret_lo(next(ret_pieces))
            mix_lo(7, 3)
            dve.wait_ge(cache_consts, 16 * 3)
            for b in range(DEC_B + 1):
                if b:
                    ret_lo(next(ret_pieces))
                if b < DEC_B:
                    ret_lo(next(ret_pieces))
                    cache_soft_a(b)
                    cache_soft_b(b)
                if third_piece(b):
                    ret_lo(next(ret_pieces))
            for p in ret_pieces:
                ret_lo(p)
            dve.wait_ge(osm_hi, 1)
            dve.tensor_tensor(ml[:, 8:16, TP:T], osm[:, :, :], f32(mh[:, 8:16, TP:T]), ALU.subtract).then_inc(osm_lo, 1)

            dve.wait_ge(osm_lo, 1)
            dve.memset(ones[:, :], 1.0 / D).then_inc(ones_ready, 1)
            dve.memset(acc_s[:, :], 0.0).then_inc(ones_ready, 1)
            dve.memset(acc_q[:, :], 0.0).then_inc(ones_ready, 1)

            def complete(b, q, r):
                dve.wait_ge(shifted, r + 1)
                dve.wait_ge(piece_used, b * 4 + (q + 1))
                y = yb[:, bass.ds(r, 1), :].rearrange("p o (h t) -> p (o h) t", h=2)
                dve.tensor_tensor(y, y, gl(q // 2), ALU.add).then_inc(g_free[q // 2], 1)

            b = B_OUT + KT // 2
            lo(b + 1, 0)
            dve.wait_ge(shift_part, 1)
            dve.tensor_scalar(halves(shift[:, :]), A[:, 0:2, 0:NL], float(KT), None, ALU.mult).then_inc(shift_ready, 1)
            lo(b + 1, 1)
            complete(b, 1, 0)
            lo(b + 1, 2)
            lo(b + 1, 3)
            complete(b, 3, 1)
            with dve.Fori(1, KT // 2) as i:
                for q in range(SLOTS):
                    lo(i + (b + 1), q)
                    if q % 2:
                        complete(i + b, q, i * 2 + q // 2)

            dve.wait_ge(mean_part, 1)
            dve.tensor_copy(halves(mean[:, :]), A[:, 0:2, 0:NL]).then_inc(mean_ready, 1)
            dve.wait_ge(mean_squared, 1)
            dve.wait_ge(var_part, 1)
            dve.scalar_tensor_tensor(out=halves(rstd[:, :]), in0=A[:, 2:4, 0:NL], scalar=LN_EPS, in1=halves(msq[:, :]),
                                     op0=ALU.add, op1=ALU.subtract).then_inc(var_ready, 1)
            dve.wait_ge(dev_ready, 1)
            c.link(dve.reciprocal(rstd[:, :], rstd[:, :]))

            def first_lo(p):
                lo(B_FFN + 1 + p // 4, p % 4)

            def split_h(r):
                dve.wait_ge(h_hi, r + 1)
                dve.tensor_tensor(hl[:, r, :], yb[:, r, :], f32(hh[:, r, :]), ALU.subtract).then_inc(h_lo, 1)

            for r in range(KT):
                dve.wait_ge(centred, r + 1)
                dve.tensor_tensor(ln_t[:, r % 2, :], yb[:, r, :], rstd[:, :], ALU.mult).then_inc(normed, 1)
                if r:
                    split_h(r - 1)
                    if r - 1 in LN_PIECES:
                        first_lo(LN_PIECES.index(r - 1))
            split_h(KT - 1)
            if KT - 1 in LN_PIECES:
                first_lo(LN_PIECES.index(KT - 1))
            for p in range(len(LN_PIECES), 7):
                first_lo(p)

            def gate_up(b0, gs, u0, m0, first=0):
                with dve.Fori(first, KP) as m:
                    b = m * 2 + b0
                    los(b + 1, range(4))
                    los(b + 2, range(3))
                    dve.wait_ge(g_free[0], m + (u0 + 1))
                    dve.wait_ge(piece_used, b * 4 + 8)
                    dve.tensor_tensor(halves(fu[:, :]), gl(1), halves(sg[:, :]), ALU.mult).then_inc(g_free[1], 1)
                    lo(b + 2, 3)
                    dve.wait_ge(f_hi, m + m0 + 1)
                    dve.tensor_tensor(fl[:, gs, bass.ds(m, 1), :], fu[:, :].rearrange("p (o t) -> p o t", o=1),
                                      f32(fh[:, gs, bass.ds(m, 1), :]), ALU.subtract).then_inc(f_lo, 1)

            def add(b, q, r):
                dve.wait_ge(piece_used, b * 4 + (q + 1))
                y = yb[:, r, :].rearrange("p o (h t) -> p (o h) t", h=2)
                return dve.tensor_tensor(y, y, gl(q % 2), ALU.add)

            def downs(b0):
                with dve.Fori(0, DN) as rb_:
                    b = rb_ + b0
                    for q in range(SLOTS):
                        add(b, q, bass.ds(rb_ * 4 + q, 1)).then_inc(g_free[q % 2], 1)
                        lo(b + 1, q)

            dve.wait_ge(g_free[0], U_FFN + 1)
            dve.wait_ge(piece_used, B_FFN * 4 + 8)
            dve.tensor_tensor(halves(fu[:, :]), gl(1), halves(sg[:, :]), ALU.mult).then_inc(g_free[1], 1)
            lo(B_FFN + 2, 3)
            dve.wait_ge(f_hi, 1)
            dve.tensor_tensor(fl[:, 0, 0, :], fu[:, :], f32(fh[:, 0, 0, :]), ALU.subtract).then_inc(f_lo, 1)
            gate_up(B_FFN, 0, U_FFN, 0, 1)
            dve.wait_ge(alpha_h, KT)
            with dve.Fori(0, LOOPS) as i:
                b0 = i * (2 * (GU + DN)) + B_LOOP
                u0 = i * (2 * (KP + KT // 2)) + U_LOOP
                gate_up(b0, 1, u0, i * 8 + 4)
                downs(b0 + GU)
                gate_up(b0 + GU + DN, 0, u0 + KP + 8, i * 8 + 8)
                downs(b0 + 2 * GU + DN)

            def out_stats(rb_, tts=range(len(TT))):
                for tt in tts:
                    n = TT[tt][1]
                    dve.wait_ge(y_kept, rb_ * 5 + tt + 1)
                    ins = dve.bn_stats(ostats[0:n, tt, 6 * rb_:6 * rb_ + 6], yo[0:n, tt, rb_ * 512:(rb_ + 1) * 512])
                return ins

            for rb_ in range(DN):
                for q, tts in enumerate(((), (0,), (1, 2), (3, 4))):
                    add(B_LAST + rb_, q, slice(rb_ * 4 + q, rb_ * 4 + q + 1)).then_inc(g_free[q % 2], 1)
                    if rb_ < DN - 1:
                        lo(B_LAST + rb_ + 1, q)
                    if rb_ and tts:
                        out_stats(rb_ - 1, tts)
            c.link(out_stats(DN - 1))
            for tt, (t0, n) in enumerate(TT):
                c.link(dve.bn_aggr(small[0:n, 100 + 2 * tt:102 + 2 * tt], ostats[0:n, tt, :]))
                dve.tensor_scalar(small[0:n, 90 + tt:91 + tt], small[0:n, 101 + 2 * tt:102 + 2 * tt], LN_EPS, None,
                                  ALU.add).then_inc(y_var, 1)
            for tt, (t0, n) in enumerate(TT):
                dve.wait_ge(y_dev, tt + 1)
                c.link(dve.reciprocal(small[0:n, 80 + tt:81 + tt], small[0:n, 80 + tt:81 + tt]))
                dve.scalar_tensor_tensor(out=small[0:n, 110 + tt:111 + tt], in0=small[0:n, 100 + 2 * tt:101 + 2 * tt], scalar=-1.0,
                                         in1=small[0:n, 80 + tt:81 + tt], op0=ALU.mult, op1=ALU.mult).then_inc(y_scale, 1)
            dve.wait_ge(gain_in, 32)
            for tt, (t0, n) in enumerate(TT):
                dve.wait_ge(y_normed, tt + 1)
                dve.tensor_tensor(yo[0:n, tt, :], yo[0:n, tt, :], g_row[0:n, :], ALU.mult).then_inc(y_gained, 1)
                dve.wait_ge(y_gained, tt + 1)
                dve.tensor_tensor(yo[0:n, tt, POOL_COLS:], yo[0:n, tt, POOL_COLS:], b_row[0:n, POOL_COLS:], ALU.add)\
                    .then_inc(y_biased_a, 1)

        @block.gpsimd
        def _(pool):
            c = Count(pool, pool_chain)
            pool.dma_start(ident[:, :], I["c_ident"]).then_inc(const_in, 16)
            for n, name in enumerate(("ln_emb_g", "ln_emb_b", "ln_mix_g", "ln_mix_b")):
                src = I[name] if n < 2 else I[name][0]
                pool.dma_start(vec_rows[n * KT:(n + 1) * KT, :], src.rearrange("(k p) -> k p", p=P)).then_inc(const_in, 16)
            for k in range(KT):
                pool.wait_ge(x_hi, k + 1)
                pool.tensor_tensor(xl[:, k, :], xf[:, k % XF_SLOTS, :], f32(xh[:, k, :]), ALU.subtract).then_inc(x_lo, 1)
            pool.wait_ge(x_lo, KT)
            pool.dma_start(ret_rot[:, :, :], I["c_ret_rot"]).then_inc(rot_in, 16)

            def rope(x, out, count, t0):
                for par in range(2):
                    pool.wait_ge(g_free[par], count)
                pool.tensor_tensor(rope_p[:, 0, t0:], x[:, 1, t0:], ret_rot[:, 0, t0:], ALU.mult)
                c.link(pool.tensor_tensor(rope_p[:, 1, t0:], x[:, 0, t0:], ret_rot[:, 1, t0:], ALU.mult))
                pool.tensor_tensor(out[:, 1, t0:], rope_p[:, 0, t0:], rope_p[:, 1, t0:], ALU.add).then_inc(rope_b, 1)

            pool.wait_ge(rot_in, 16)
            pool.wait_ge(in_turned, KT)
            def head_constants(h):
                pool.dma_start(hc[:, :], I["c_head"][bass.ds(h, 1), :, 0:HC_W].rearrange("o p n -> p (o n)")).then_inc(head_in, 16)

            def sample_inputs(h):
                pool.dma_start(hcs[:, :], I["c_head"][bass.ds(h, 1), :, HC_W:HC_W + HS_W].rearrange(
                    "o p n -> p (o n)")).then_inc(head_s_in, 16)
                for b in range(DEC_B):
                    pool.dma_start(states[:, b], I["state_ret"][0, b, bass.ds(h, 1), :, :].rearrange(
                        "o (k p) e -> p (o k) e", p=P)).then_inc(states_in, 16)

            def prompt_state(h):
                wait_apart(pool, state_new, h * 5 + 5)
                pool.dma_start(O["ret_p"][0, 0, bass.ds(h, 1), :, :].rearrange("o (k p) e -> p (o k) e", p=P),
                               state[:, :, :]).then_inc(state_out, 16)
                wait_apart(pool, state_out, h * 16 + 16)

            def sample_states(h):
                for b in range(DEC_B):
                    wait_apart(pool, sample_state_new, h * DEC_B + (b + 1))
                    pool.dma_start(O["ret_s"][0, b, bass.ds(h, 1), :, :].rearrange("o (k p) e -> p (o k) e", p=P),
                                   states[:, b]).then_inc(states_out, 16)

            def ropes(h):
                rope(kq_raw, k_rot, h * 4 + (U_IN + 2), 0)
                rope(kq_raw, q_rot, h * 4 + (U_IN + 3), M0)

            head_constants(0)
            sample_inputs(0)
            ropes(0)
            with pool.Fori(0, HEADS - 1) as i, c.loop(i, HEADS - 1, 2):
                prompt_state(i)
                head_constants(i + 1)
                sample_states(i)
                wait_apart(pool, states_out, i * (16 * DEC_B) + 16 * DEC_B)
                sample_inputs(i + 1)
                ropes(i + 1)
            prompt_state(HEADS - 1)

            pool.dma_start(swa_rot[:, :, :], I["c_swa_rot"]).then_inc(swa_in, 16)
            pool.dma_start(perm[:, :, :], I["c_perm"]).then_inc(swa_in, 16)
            pool.dma_start(mask_p[:, :], I["c_mask_p"]).then_inc(swa_in, 16)
            pool.dma_start(sinks[:, :], I["swa_sinks"].to_broadcast([P, 16])).then_inc(swa_in, 16)
            sample_states(HEADS - 1)

            def cosines(t0):
                pool.tensor_tensor(z_rot[:, t0:], z_raw[:, t0:], swa_rot[:, 0, t0:], ALU.mult).then_inc(cos_part, 1)

            pool.wait_ge(swa_in, 16 * 4)
            pool.wait_ge(gated_lo, HEADS)
            pool.wait_ge(g_free[0], U_IN + B_SWA // 2 + 1)
            cosines(0)

            def kv_outputs(j):
                r = slice(j * DEC_T, (j + 1) * DEC_T)
                for o, new in ((O["k_s"], k_tok[r, 1, :]), (O["v_s"], v_tok[r, 5, :])):
                    pool.dma_start(o[0, j, WINDOW - DEC_T:, :, :].rearrange("t k d -> t (k d)"), new).then_inc(kv_out, 16)
                if j == 1:
                    kp = O["k_p"][0, 0].rearrange("t k d -> t (k d)")
                    pool.dma_start(kp, k_tok[:, 0, :]).then_inc(kv_out, 16)
                if j == 2:
                    vp = O["v_p"][0, 0].rearrange("t k d -> t (k d)")
                    pool.dma_start(vp, v_tok[:, 4, :]).then_inc(kv_out, 16)
                if j in (3, 4):
                    o, old = (O["k_s"], I["cache_swa_k"]) if j == 3 else (O["v_s"], I["cache_swa_v"])
                    pool.dma_start(o[0, :, 0:WINDOW - DEC_T].rearrange("b t k d -> b (t k d)"),
                                   old[0, :, DEC_T:].rearrange("b t k d -> b (t k d)")).then_inc(kv_out, 16)

            def lo(b, q):
                pool.wait_ge(piece_hi, b * 4 + (q + 1))
                pool.tensor_tensor(wl[:, q], raw[:, q], f32(wh[:, q]), ALU.subtract).then_inc(piece_lo, 1)

            pool.wait_ge(piece_lo, (B_SWA + 5) * 4 + 4)
            for j in range(8):
                kv = j // 4
                pool.wait_ge(g_free[j % 2], U_IN + (B_SWA + 2 + j) // 2 + 1)
                if j:
                    pool.wait_ge(logits_ready, j * 4)
                    pool.wait_ge(sample_q, 32 * j)
                else:
                    pool.wait_ge(kv_step, 5)
                cosines(M0)
                lo(B_SWA + 5 + j, 0)
                pool.wait_ge(rotated, 2 + j)
                for i in range(2):
                    pool.dma_start(qs[kv * HD:(kv + 1) * HD, :, 2 * (j % 4) + i, :],
                                   z_rot[i * HD:(i + 1) * HD, TP:T].rearrange("p (b t) -> p b t", b=DEC_B))\
                        .then_inc(sample_q, 16)
                for q in range(1, SLOTS):
                    lo(B_SWA + 5 + j, q)
                    if q == 1:
                        pool.wait_ge(kv_step_kept, 3)
                        kv_outputs(j)
            def cached(b):
                if b >= CACHE_SLOTS:
                    pool.wait_ge(c_mixed, b - CACHE_SLOTS + 1)
                s = b % CACHE_SLOTS
                pool.dma_start(kc[:, s, :], I["cache_swa_k"][0, b].rearrange("t k d -> t (k d)")).then_inc(c_k[s], 16)
                pool.dma_start(vc[:, s, :], I["cache_swa_v"][0, b].rearrange("t k d -> t (k d)")).then_inc(c_k[s], 16)

            pool.dma_start(mask_c[:, :], I["c_mask_c"]).then_inc(cache_consts, 16)
            pool.dma_start(sink_s[:, :], I["swa_sinks"].rearrange("o (h u) -> (o h) u", u=1)[:, None, :].to_broadcast([16, 8, 1]))\
                .then_inc(cache_consts, 16)
            for b in range(CACHE_SLOTS):
                cached(b)
            pool.wait_ge(mix_lo_done, 32)
            pool.wait_ge(sample_q, 16 * 16)
            pool.dma_start(mask_n[:, :, :], I["c_mask_n"]).then_inc(cache_consts, 16)
            for b in range(CACHE_SLOTS, DEC_B):
                cached(b)
            pool.wait_ge(os_ready, 1)
            for kv in range(2):
                for i in range(2):
                    pool.dma_start(osm[i * HD:(i + 1) * HD, kv * 4:kv * 4 + 4, :], os_[kv * HD:(kv + 1) * HD, i:8:2, :])\
                        .then_inc(osm_ready, 16)

            pool.wait_ge(ones_ready, 3)
            pool.memset(small[:, 158:159], 0.0).then_inc(sum_done, 1)
            acc_o = acc_s[:, :].rearrange("p (o t) -> p o t", o=1)

            def less_shift(r):
                pool.tensor_tensor(yb[:, bass.ds(r, 1), :], yb[:, bass.ds(r, 1), :],
                                   shift[:, :].rearrange("p (o t) -> p o t", o=1), ALU.subtract).then_inc(shifted, 1)

            def sums(i, par, r, ahead):
                pool.wait_ge(g_free[par], i + (U_OUT2 + 1))
                pool.wait_ge(sum_done, r + 1)
                pool.tensor_tensor(acc_o, acc_o, yb[:, bass.ds(r, 1), :], ALU.add).then_inc(sum_done, 1)
                if ahead:
                    less_shift(r + 2)
                pool.wait_ge(squared, r + 1)
                pool.wait_ge(sum_done, r + 2)
                pool.tensor_tensor(acc_q[:, :], acc_q[:, :], ln_t[:, par, :], ALU.add).then_inc(squares_done, 1)

            pool.wait_ge(shift_ready, 1)
            less_shift(0)
            less_shift(1)
            with pool.Fori(0, KT // 2 - 1) as i:
                for par in range(2):
                    if par:
                        wait_apart(pool, squares_done, i * 2 + 1)
                    sums(i, par, i * 2 + par, True)
            for par in range(2):
                sums(KT // 2 - 1, par, KT - 2 + par, False)
            pool.wait_ge(squares_done, KT)
            pool.wait_ge(mean_ready, 1)
            for r in range(KT):
                pool.tensor_tensor(yb[:, r, :], yb[:, r, :], mean[:, :], ALU.subtract).then_inc(centred, 1)
            for r in range(KT):
                pool.wait_ge(h_lo, r + 1)
                pool.tensor_scalar(yb[:, r, :], yb[:, r, :], ALPHA, None, ALU.mult).then_inc(alpha_h, 1)

            pool.wait_ge(piece_used, 4 * B_LAST)
            for row, name in ((g_row, "ln_ffn_g"), (b_row, "ln_ffn_b")):
                pool.dma_start(row[:, :], I[name].to_broadcast([P, D])).then_inc(gain_in, 16)
            for tt, (t0, n) in enumerate(TT):
                pool.wait_ge(y_gained, tt + 1)
                pool.tensor_tensor(yo[0:n, tt, 0:POOL_COLS], yo[0:n, tt, 0:POOL_COLS], b_row[0:n, 0:POOL_COLS], ALU.add)\
                    .then_inc(y_biased_b, 1)
            pool.wait_ge(kv_out, 16 * (2 + 2 * DEC_B + 2))
            pool.wait_ge(state_out, 16 * HEADS)
            pool.wait_ge(states_out, 16 * DEC_B * HEADS)


_INS = ["x_prompt", "x_sample", "state_ret", "cache_swa_k", "cache_swa_v", "meta_tokens", "ln_emb_g", "ln_emb_b",
        "w_in", "w_out", "swa_sinks", "ln_mix_g", "ln_mix_b", "w_ffn_gate", "w_ffn_up", "w_ffn_down", "ln_ffn_g", "ln_ffn_b"]
_OUTS = [("y_p", (1, SEQ, D)), ("y_s", (DEC_B, DEC_T, D)), ("ret_p", (1, 1, HEADS, DK, DK)), ("k_p", (1, 1, WINDOW, 2, HD)),
         ("v_p", (1, 1, WINDOW, 2, HD)), ("ret_s", (1, DEC_B, HEADS, DK, DK)), ("k_s", (1, DEC_B, WINDOW, 2, HD)),
         ("v_s", (1, DEC_B, WINDOW, 2, HD))]


def kernel(**inputs):
    import concourse.bacc as bacc
    from concourse.bass_utils import run_bass_kernel_spmd

    nc = bacc.Bacc("TRN2", target_bir_lowering=False, num_devices=1)
    arrays = {n: np.ascontiguousarray(inputs[n]) for n in _INS}
    arrays.update(shape_constants())
    ins = {n: nc.dram_tensor(f"in_{n}", a.shape, F32, kind="ExternalInput").ap() for n, a in arrays.items()}
    outs = {n: nc.dram_tensor(f"out_{n}", s, F32, kind="ExternalOutput").ap() for n, s in _OUTS}
    hymba_step_kernel(nc, ins, outs)
    r = run_bass_kernel_spmd(nc, [{f"in_{n}": a for n, a in arrays.items()}], core_ids=[0])
    return tuple(r.results[0][f"out_{n}"] for n, _ in _OUTS)
```
